# Optimizing a Trainium2 kernel written in Bass

```python
import math
import jax
import jax.numpy as jnp
from jax import lax
import numpy as np

D_MODEL = 1024
BATCH = 1
SEQ = 512
DEPTH = 2
DEC_BATCH = 1
DEC_SEQ = 32
PAST_LEN = 256

CHUNK = 64
NORM_EPS = 1e-6

A_HEADS = 4
A_DK = 128
A_DV = 128
A_W = A_HEADS * A_DV
A_COLS = 4 * A_W + 2 * A_HEADS
FORGET_BIAS_LO = 3.0
FORGET_BIAS_HI = 6.0

B_HEADS = 8
B_KV = 2
B_GROUP = B_HEADS // B_KV
B_HD = 64
B_W = B_HEADS * B_HD
B_COLS = B_W + 2 * B_KV * B_HD
WINDOW = 128
WIN_CHUNKS = WINDOW // CHUNK
NUM_BUCKETS = 32
REL_MAX_DIST = 256

C_HEADS = 8
C_HD = 64
C_W = C_HEADS * C_HD
C_DECAY_LORA = 64
C_AAA_LORA = 64
C_GATE_LORA = 128
C_COLS = 3 * C_W + C_DECAY_LORA + C_AAA_LORA + C_GATE_LORA
GN_EPS = 64e-5

N_BRANCH = 3
IN_COLS = A_COLS + B_COLS + C_COLS + N_BRANCH * D_MODEL
D_FF = -(-8 * D_MODEL // (3 * 256)) * 256

kernel_name = 'hybrid_streaming_encoder_step'

def _split(x, sizes):
    out, start = [], 0
    for s in sizes:
        out.append(x[..., start:start + s])
        start += s
    return out

def _rms_norm(x, g):
    xf = x.astype(jnp.float32)
    y = xf * lax.rsqrt(jnp.mean(xf * xf, axis=-1, keepdims=True) + NORM_EPS)
    return (y * g.astype(jnp.float32)).astype(x.dtype)

def _mlstm_chunk(carry, blk):
    c_mat, n_vec, m_prev = carry
    q, k, v, lf, li = blk
    L = q.shape[2]
    F = jnp.cumsum(lf, axis=-1)
    causal = jnp.tril(jnp.ones((L, L), dtype=bool))
    dlog = jnp.where(causal, F[..., :, None] - F[..., None, :] + li[..., None, :], -jnp.inf)
    m_inter = F + m_prev[..., None]
    m_t = jnp.maximum(m_inter, jnp.max(dlog, axis=-1))
    w = jnp.exp(dlog - m_t[..., None]) * jnp.einsum('bhtk,bhsk->bhts', q, k)
    inter = jnp.exp(m_inter - m_t)
    num = jnp.einsum('bhts,bhsv->bhtv', w, v) + inter[..., None] * jnp.einsum('bhtk,bhkv->bhtv', q, c_mat)
    den = jnp.sum(w, axis=-1) + inter * jnp.einsum('bhtk,bhk->bht', q, n_vec)
    h = num / jnp.maximum(jnp.abs(den), jnp.exp(-m_t))[..., None]
    m_new = m_t[..., -1]
    wk = jnp.exp(F[..., -1:] - F + li - m_new[..., None])
    decay = jnp.exp(F[..., -1] + m_prev - m_new)
    c_new = decay[..., None, None] * c_mat + jnp.einsum('bhs,bhsk,bhsv->bhkv', wk, k, v)
    n_new = decay[..., None] * n_vec + jnp.einsum('bhs,bhsk->bhk', wk, k)
    return (c_new, n_new, m_new), h

def _mlstm_mixer(cols, state, gate_bias, norm_g):
    Bsz, T, _ = cols.shape
    chunk = min(CHUNK, T)
    nc = T // chunk
    q, k, v, o, ig, fg = _split(cols, [A_W, A_W, A_W, A_W, A_HEADS, A_HEADS])
    gate_bias = gate_bias.astype(jnp.float32)

    def heads(t):
        return t.reshape(Bsz, T, A_HEADS, -1).transpose(0, 2, 1, 3)

    q, k, v = heads(q), heads(k) * (A_DK ** -0.5), heads(v)
    li = (ig + gate_bias[:A_HEADS]).transpose(0, 2, 1)
    lf = jax.nn.log_sigmoid(fg + gate_bias[A_HEADS:]).transpose(0, 2, 1)

    def blocks(t):
        t = t.reshape(t.shape[:2] + (nc, chunk) + t.shape[3:])
        return jnp.moveaxis(t, 2, 0)

    state = tuple(s.astype(jnp.float32) for s in state)
    state, h = lax.scan(_mlstm_chunk, state, (blocks(q), blocks(k), blocks(v), blocks(lf), blocks(li)))
    h = jnp.moveaxis(h, 0, 2).reshape(Bsz, A_HEADS, T, A_DV)
    h = h * lax.rsqrt(jnp.mean(h * h, axis=-1, keepdims=True) + NORM_EPS)
    h = h.transpose(0, 2, 1, 3).reshape(Bsz, T, A_W) * norm_g.astype(jnp.float32)
    return jax.nn.sigmoid(o) * h, state

def _rel_bucket(rel):
    half = NUM_BUCKETS // 2
    exact = half // 2
    n = jnp.abs(rel)
    far = exact + (jnp.log(jnp.maximum(n, 1).astype(jnp.float32) / exact)
                   / math.log(REL_MAX_DIST / exact) * (half - exact)).astype(jnp.int32)
    far = jnp.minimum(far, half - 1)
    return jnp.where(rel > 0, half, 0) + jnp.where(n < exact, n, far)

def _rel_bias(table, n_q, n_before):
    rel = (jnp.arange(n_before + n_q)[None, :] - n_before) - jnp.arange(n_q)[:, None]
    bias = table[_rel_bucket(rel)].astype(jnp.float32)
    return jnp.transpose(bias, (2, 0, 1)).reshape(B_KV, B_GROUP, n_q, n_before + n_q)

def _sink_attention(q, k, v, bias, valid, sinks):
    s = jnp.einsum('...qngd,...knd->...ngqk', q, k) * (B_HD ** -0.5) + bias
    if valid is not None:
        s = jnp.where(valid[..., None, None, None, :], s, -1e30)
    sk = sinks.astype(jnp.float32).reshape(B_KV, B_GROUP, 1, 1)
    mx = jnp.maximum(jnp.max(s, axis=-1, keepdims=True), sk)
    p = jnp.exp(s - mx)
    p = p / (jnp.sum(p, axis=-1, keepdims=True) + jnp.exp(sk - mx))
    return jnp.einsum('...ngqk,...knd->...qngd', p, v)

def _swa_prompt(q, k, v, table, sinks):
    Bsz, T, _ = q.shape
    nc = T // CHUNK
    pad = WIN_CHUNKS * CHUNK
    k4 = k.reshape(Bsz, T, B_KV, B_HD)
    v4 = v.reshape(Bsz, T, B_KV, B_HD)

    def band(t):
        t = jnp.pad(t, ((0, 0), (pad, 0), (0, 0), (0, 0))).reshape(Bsz, nc + WIN_CHUNKS, CHUNK, B_KV, B_HD)
        return jnp.concatenate([t[:, c:c + nc] for c in range(WIN_CHUNKS + 1)], axis=2)

    kpos = jnp.arange(nc)[:, None] * CHUNK - pad + jnp.arange(pad + CHUNK)[None, :]
    out = _sink_attention(q.reshape(Bsz, nc, CHUNK, B_KV, B_GROUP, B_HD), band(k4), band(v4),
                          _rel_bias(table, CHUNK, pad), kpos >= 0, sinks)
    keep = min(WINDOW, T)
    return out.reshape(Bsz, T, B_W), k4[:, T - keep:], v4[:, T - keep:]

def _swa_sample(q, k, v, k_cache, v_cache, table, sinks):
    Bsz, T, _ = q.shape
    n_before = k_cache.shape[1]
    kf = jnp.concatenate([k_cache.astype(jnp.float32), k.reshape(Bsz, T, B_KV, B_HD)], axis=1)
    vf = jnp.concatenate([v_cache.astype(jnp.float32), v.reshape(Bsz, T, B_KV, B_HD)], axis=1)
    out = _sink_attention(q.reshape(Bsz, T, B_KV, B_GROUP, B_HD), kf, vf,
                          _rel_bias(table, T, n_before), None, sinks)
    return out.reshape(Bsz, T, B_W), kf[:, T:], vf[:, T:]

def _rwkv_step(S, inp):
    r, w, k, v, kk, a = inp
    S = (S * w[:, :, None, :]
         + jnp.einsum('bhij,bhj->bhi', S, -kk)[..., None] * (kk * a)[:, :, None, :]
         + v[..., None] * k[:, :, None, :])
    return S, jnp.einsum('bhij,bhj->bhi', S, r)

def _rwkv_mixer(cols, shift_prev, S0, mu, w0, w_w2, a0, w_a2, w_g2, k_k, k_a, r_k, gn_g, gn_b):
    Bsz, T, _ = cols.shape
    f32 = jnp.float32
    prev = jnp.concatenate([shift_prev.astype(f32), cols[:, :-1]], axis=1)
    xm = cols + (prev - cols) * mu.astype(f32)
    r, k, v, wl, al, gl = _split(xm, [C_W, C_W, C_W, C_DECAY_LORA, C_AAA_LORA, C_GATE_LORA])
    w = -jax.nn.softplus(-(w0 + jnp.tanh(wl) @ w_w2)) - 0.5
    decay = jnp.exp(-jnp.exp(w))
    a = jax.nn.sigmoid(a0 + al @ w_a2)
    g = jax.nn.sigmoid(gl) @ w_g2

    def heads(t):
        return t.reshape(Bsz, T, C_HEADS, C_HD)

    kk = heads(k * k_k)
    kk = kk / jnp.maximum(jnp.sqrt(jnp.sum(kk * kk, axis=-1, keepdims=True)), 1e-12)
    k = k * (1.0 + (a - 1.0) * k_a)
    r_h, k_h, v_h = heads(r), heads(k), heads(v)

    def tm(t):
        return jnp.moveaxis(t, 1, 0)

    S, y = lax.scan(_rwkv_step, S0.astype(f32),
                    (tm(r_h), tm(heads(decay)), tm(k_h), tm(v_h), tm(kk), tm(heads(a))))
    y = jnp.moveaxis(y, 0, 1)
    mean = jnp.mean(y, axis=-1, keepdims=True)
    var = jnp.mean(jnp.square(y - mean), axis=-1, keepdims=True)
    y = ((y - mean) * lax.rsqrt(var + GN_EPS)).reshape(Bsz, T, C_W) * gn_g + gn_b
    bonus = jnp.sum(r_h * k_h * r_k.reshape(C_HEADS, C_HD), axis=-1, keepdims=True) * v_h
    y = (y + bonus.reshape(Bsz, T, C_W)) * g
    return y, S, cols[:, -1:]

def _layer(x, st, P, l):
    Bsz, T, _ = x.shape
    swa_k, swa_v, mc, mn, mm, rs, rshift = st
    xn = _rms_norm(x, P['norm_mix_pre'][l])
    cols = jnp.einsum('btd,dc->btc', xn, P['w_in'][l]).astype(jnp.float32)
    ca, cb, cc, cg = _split(cols, [A_COLS, B_COLS, C_COLS, N_BRANCH * D_MODEL])

    h_a, (mc, mn, mm) = _mlstm_mixer(ca, (mc, mn, mm), P['a_gate_bias'][l], P['a_norm'][l])

    qb, kb, vb = _split(cb, [B_W, B_KV * B_HD, B_KV * B_HD])
    if swa_k is None:
        h_b, swa_k, swa_v = _swa_prompt(qb, kb, vb, P['rel_bias'], P['b_sinks'][l])
    else:
        h_b, swa_k, swa_v = _swa_sample(qb, kb, vb, swa_k, swa_v, P['rel_bias'], P['b_sinks'][l])

    h_c, rs, rshift = _rwkv_mixer(cc, rshift, rs, P['c_mu'][l], P['c_w0'][l], P['c_w_w2'][l],
                                  P['c_a0'][l], P['c_w_a2'][l], P['c_w_g2'][l], P['c_k_k'][l],
                                  P['c_k_a'][l], P['c_r_k'][l], P['c_gn_g'][l], P['c_gn_b'][l])

    gates = jax.nn.sigmoid(cg).reshape(Bsz, T, N_BRANCH, D_MODEL)
    merged = (gates[:, :, 0] * (h_a @ P['w_branch_a'][l])
              + gates[:, :, 1] * (h_b @ P['w_branch_b'][l])
              + gates[:, :, 2] * (h_c @ P['w_branch_c'][l]))
    mix = (merged @ P['w_out'][l]).astype(x.dtype)
    x = x + _rms_norm(mix, P['norm_mix_post'][l])

    xn = _rms_norm(x, P['norm_ffn_pre'][l])
    gate, up = _split(jnp.einsum('btd,df->btf', xn, P['w_ffn_in'][l]), [D_FF, D_FF])
    f = jnp.einsum('btf,fd->btd', jax.nn.silu(gate) * up, P['w_ffn_out'][l]).astype(x.dtype)
    x = x + _rms_norm(f, P['norm_ffn_post'][l])
    return x, (swa_k, swa_v, mc, mn, mm, rs, rshift)

def _trunk(x, layer_states, P):
    new = []
    for l in range(DEPTH):
        x, st = _layer(x, layer_states[l], P, l)
        new.append(st)
    return x, [jnp.stack([s[i] for s in new]) for i in range(7)]

def setup_inputs(seed: int = 0) -> dict:
    key = jax.random.key(seed)
    keys = iter(jax.random.split(key, 48))

    def nrm(shape, scale=1.0):
        return jax.random.normal(next(keys), shape, jnp.float32) * scale

    def gain(shape):
        return 1.0 + nrm(shape, 0.05)

    swa_len = min(WINDOW, PAST_LEN)
    forget_bias = jnp.linspace(FORGET_BIAS_LO, FORGET_BIAS_HI, A_HEADS, dtype=jnp.float32)
    return {
        'x_prompt': nrm((BATCH, SEQ, D_MODEL)),
        'x_sample': nrm((DEC_BATCH, DEC_SEQ, D_MODEL)),
        'cache_swa_k': nrm((DEPTH, DEC_BATCH, swa_len, B_KV, B_HD)),
        'cache_swa_v': nrm((DEPTH, DEC_BATCH, swa_len, B_KV, B_HD)),
        'state_mlstm_c': nrm((DEPTH, DEC_BATCH, A_HEADS, A_DK, A_DV), 0.5),
        'state_mlstm_n': nrm((DEPTH, DEC_BATCH, A_HEADS, A_DK), 0.5),
        'state_mlstm_m': nrm((DEPTH, DEC_BATCH, A_HEADS), 0.5),
        'state_rwkv_s': nrm((DEPTH, DEC_BATCH, C_HEADS, C_HD, C_HD), 0.5),
        'state_rwkv_shift': nrm((DEPTH, DEC_BATCH, 1, C_COLS)),
        'w_in': nrm((DEPTH, D_MODEL, IN_COLS), D_MODEL ** -0.5),
        'norm_mix_pre': gain((DEPTH, D_MODEL)),
        'norm_mix_post': gain((DEPTH, D_MODEL)),
        'norm_ffn_pre': gain((DEPTH, D_MODEL)),
        'norm_ffn_post': gain((DEPTH, D_MODEL)),
        'a_gate_bias': jnp.concatenate([nrm((DEPTH, A_HEADS), 0.1),
                                        forget_bias + nrm((DEPTH, A_HEADS), 0.1)], axis=-1),
        'a_norm': gain((DEPTH, A_W)),
        'rel_bias': nrm((NUM_BUCKETS, B_HEADS), 0.5),
        'b_sinks': nrm((DEPTH, B_HEADS), 0.5),
        'c_mu': jax.random.uniform(next(keys), (DEPTH, C_COLS), jnp.float32),
        'c_w0': nrm((DEPTH, C_W), 0.5) - 1.0,
        'c_w_w2': nrm((DEPTH, C_DECAY_LORA, C_W), 0.1),
        'c_a0': nrm((DEPTH, C_W), 0.1),
        'c_w_a2': nrm((DEPTH, C_AAA_LORA, C_W), 0.5 * C_AAA_LORA ** -0.5),
        'c_w_g2': nrm((DEPTH, C_GATE_LORA, C_W), C_GATE_LORA ** -0.5),
        'c_k_k': 0.85 + nrm((DEPTH, C_W), 0.05),
        'c_k_a': 1.0 + nrm((DEPTH, C_W), 0.05),
        'c_r_k': nrm((DEPTH, C_W), 0.1),
        'c_gn_g': gain((DEPTH, C_W)),
        'c_gn_b': nrm((DEPTH, C_W), 0.01),
        'w_branch_a': nrm((DEPTH, A_W, D_MODEL), A_W ** -0.5),
        'w_branch_b': nrm((DEPTH, B_W, D_MODEL), B_W ** -0.5),
        'w_branch_c': nrm((DEPTH, C_W, D_MODEL), C_W ** -0.5),
        'w_out': nrm((DEPTH, D_MODEL, D_MODEL), D_MODEL ** -0.5),
        'w_ffn_in': nrm((DEPTH, D_MODEL, 2 * D_FF), D_MODEL ** -0.5),
        'w_ffn_out': nrm((DEPTH, D_FF, D_MODEL), D_FF ** -0.5),
    }

def reference(x_prompt, x_sample, cache_swa_k, cache_swa_v, state_mlstm_c, state_mlstm_n, state_mlstm_m,
              state_rwkv_s, state_rwkv_shift, w_in, norm_mix_pre, norm_mix_post, norm_ffn_pre, norm_ffn_post,
              a_gate_bias, a_norm, rel_bias, b_sinks, c_mu, c_w0, c_w_w2, c_a0, c_w_a2, c_w_g2, c_k_k, c_k_a,
              c_r_k, c_gn_g, c_gn_b, w_branch_a, w_branch_b, w_branch_c, w_out, w_ffn_in, w_ffn_out):
    P = {
        'w_in': w_in, 'norm_mix_pre': norm_mix_pre, 'norm_mix_post': norm_mix_post,
        'norm_ffn_pre': norm_ffn_pre, 'norm_ffn_post': norm_ffn_post,
        'a_gate_bias': a_gate_bias, 'a_norm': a_norm, 'rel_bias': rel_bias, 'b_sinks': b_sinks,
        'c_mu': c_mu, 'c_w0': c_w0, 'c_w_w2': c_w_w2, 'c_a0': c_a0, 'c_w_a2': c_w_a2, 'c_w_g2': c_w_g2,
        'c_k_k': c_k_k, 'c_k_a': c_k_a, 'c_r_k': c_r_k, 'c_gn_g': c_gn_g, 'c_gn_b': c_gn_b,
        'w_branch_a': w_branch_a, 'w_branch_b': w_branch_b, 'w_branch_c': w_branch_c, 'w_out': w_out,
        'w_ffn_in': w_ffn_in, 'w_ffn_out': w_ffn_out,
    }
    f32 = jnp.float32
    bp = x_prompt.shape[0]
    fresh = (None, None,
             jnp.zeros((bp, A_HEADS, A_DK, A_DV), f32), jnp.zeros((bp, A_HEADS, A_DK), f32),
             jnp.zeros((bp, A_HEADS), f32), jnp.zeros((bp, C_HEADS, C_HD, C_HD), f32),
             jnp.zeros((bp, 1, C_COLS), f32))
    y_prompt, p_states = _trunk(x_prompt, [fresh] * DEPTH, P)
    carried = [(cache_swa_k[l], cache_swa_v[l], state_mlstm_c[l], state_mlstm_n[l], state_mlstm_m[l],
                state_rwkv_s[l], state_rwkv_shift[l]) for l in range(DEPTH)]
    y_sample, s_states = _trunk(x_sample, carried, P)
    p_swa_k, p_swa_v, p_mlstm_c, p_mlstm_n, p_mlstm_m, p_rwkv_s, p_rwkv_shift = p_states
    s_swa_k, s_swa_v, s_mlstm_c, s_mlstm_n, s_mlstm_m, s_rwkv_s, s_rwkv_shift = s_states
    return (y_prompt, y_sample,
            p_swa_k, p_swa_v, p_mlstm_c, p_mlstm_n, p_mlstm_m, p_rwkv_s, p_rwkv_shift,
            s_swa_k, s_swa_v, s_mlstm_c, s_mlstm_n, s_mlstm_m, s_rwkv_s, s_rwkv_shift)


_drawn_inputs = setup_inputs


def setup_inputs(seed=0):
    import zlib

    import numpy as np

    out = dict(_drawn_inputs(seed))
    spreads = {}
    factors = {'b_sinks': 8.0, 'c_k_k': 3.246, 'c_gn_b': 2.861}
    for name, (base, spread) in spreads.items():
        noise = np.random.default_rng([zlib.crc32(name.encode()), seed]).standard_normal(out[name].shape)
        drawn = base * np.exp(spread * noise) if base else spread * noise
        out[name] = jnp.asarray(drawn.astype(out[name].dtype))
    for name, factor in factors.items():
        out[name] = (out[name] * factor).astype(out[name].dtype)
    return out
```

```python
import math
from contextlib import ExitStack

import numpy as np

import concourse.bass as bass
from concourse import mybir

P = 128
D = 1024
TP, TS = 512, 32
T = TP + TS
DEPTH = 2
KD = D // P
A_H, A_W = 4, 512
A_COLS = 4 * A_W + 2 * A_H
B_W, B_HD = 512, 64
B_COLS = 768
C_W, C_H = 512, 8
C_COLS = 1792
CT = C_COLS // P
OFF_B = A_COLS
OFF_C = A_COLS + B_COLS
OFF_G = OFF_C + C_COLS
D_FF = 2816
KF = D_FF // P
WINDOW = 128
CHUNK = 64
NORM_EPS, GN_EPS = 1e-6, 64e-5
HALF = T // 2
SPLIT_C = 256
CW = TP + 1 + TS
KEYS = WINDOW + CHUNK
KEYS_S = WINDOW + TS
NRAW, NSPLIT = 3, 2
GROUPS = 5
PARAM_ROWS = [("norm_mix_pre", KD), ("norm_mix_post", KD), ("norm_ffn_pre", KD), ("norm_ffn_post", KD),
              ("c_mu", CT), ("state_rwkv_shift", CT), ("a_norm", 4), ("c_w0", 4), ("c_a0", 4), ("c_k_k", 4),
              ("c_k_a", 4), ("c_r_k", 4), ("c_gn_g", 4), ("c_gn_b", 4)]
PARAM_AT, _n = {}, 0
for _name, _rows in PARAM_ROWS:
    PARAM_AT[_name] = _n
    _n += _rows
NPARAM = _n


def group(g):
    return (P, P * g) if g < 4 else (TS, TP)


def shape_constants():
    c = {}
    c["ident"] = np.eye(P)
    c["ones"] = np.ones((P, P))
    c["headones"] = np.kron(np.eye(2), np.ones((64, 64)))
    s = np.arange(64)[:, None]
    t = np.arange(64)[None, :]
    both = lambda m: np.tile(m.astype(np.float64), (2, 1))
    c["lt_le"] = np.concatenate([both(s < t), both(s <= t)], axis=1)
    level = []
    for b in (1, 2, 4, 8, 16, 32):
        same = (s // (2 * b)) == (t // (2 * b))
        level.append(both(same & (s % (2 * b) < b) & (t % (2 * b) >= b)))
    c["levels"] = np.concatenate(level, axis=1)
    c["level0_neg"] = -both((s // 2 == t // 2) & (s % 2 == 1) & (t % 2 == 0))
    c["eye64"] = both(s == t)
    a = np.arange(P)
    c["future_neg"] = np.where(a[:, None] > a[None, :], -1e30, 0.0)
    m = np.ones((P, 512))
    m[:, ::64] = 0
    c["scan64"] = m
    m = np.ones((P, 128))
    m[:, ::32] = 0
    c["scan32"] = m
    sel = np.zeros((P, 4 * P))
    for h in range(4):
        sel[h, h * P:(h + 1) * P] = 1
    c["sel"] = sel
    m = np.ones((P, T))
    m[:, 0:TP:P] = 0
    m[:, TP] = 0
    c["scan_rows"] = m
    rel = np.arange(256) - 63 - WINDOW
    half, exact = 16, 8
    n = np.abs(rel)
    far = exact + (np.log(np.maximum(n, 1).astype(np.float32) / np.float32(exact)) / math.log(256 / exact)
                   * (half - exact)).astype(np.int32)
    bucket = np.where(rel > 0, half, 0) + np.where(n < exact, n, np.minimum(far, half - 1))
    hot = np.zeros((P, 256))
    hot[np.clip(bucket, 0, 31), np.arange(256)] = 1
    c["bucket_hot"] = hot
    v = np.zeros((P, 8))
    v[:, 0] = NORM_EPS
    v[:, 1] = GN_EPS
    v[:, 2] = 10 * math.log(2)
    v[:, 3] = 1.0
    c["scalars"] = v
    at, cols, parts = {}, 0, []
    for k, x in c.items():
        at[k] = (cols, x.shape[1])
        cols += x.shape[1]
        parts.append(x)
    return at, np.concatenate(parts, axis=1).astype(np.float32)


class Count:

    def __init__(self, sem):
        self.sem, self.value, self.seen = sem, 0, {}

    def inc(self, ins, n=1):
        ins.then_inc(self.sem, n)
        self.value += n

    def wait_next(self, eng, who, n=1):
        self.seen[who] = self.seen.get(who, 0) + n
        eng.wait_ge(self.sem, self.seen[who])


class Lane:

    def __init__(self, eng, chain):
        self.eng, self.chain = eng, chain

    def __call__(self, ins, count=None):
        c = count or self.chain
        c.inc(ins)
        self.eng.wait_ge(c.sem, c.value)


class Bank:

    def __init__(self, name, tensor, sem):
        self.t = tensor
        self.full = {r: Count(sem(f"{name}_full_for_{r}")) for r in ("act", "dve")}
        self.empty = {r: Count(sem(f"{name}_emptied_by_{r}")) for r in ("act", "dve")}
        self.last = None
        self.marks = {}

    def claim(self, pe):
        if self.last:
            pe.wait_ge(self.empty[self.last].sem, self.full[self.last].value)

    def filled(self, ins, reader, mark=None):
        self.full[reader].inc(ins)
        self.last = reader
        self.marks[mark] = (self.empty[reader].sem, self.full[reader].value)

    def read(self, eng, reader):
        self.full[reader].wait_next(eng, reader)

    def wait_emptied(self, eng, mark):
        eng.wait_ge(*self.marks[mark])


def make_plan():
    plan = [("load_x",)]
    for l in range(DEPTH):
        plan += [("norm_pre", l, 0)]
        plan += [("cols_c", l, j) for j in range(CT)]
        plan += [("c_shift_out", l)]
        for g in range(GROUPS):
            plan += [("c_prep", l, g), ("c_gram", l, g), ("c_invert", l, g), ("c_chain", l, g), ("c_finish", l, g)]
        plan += [("cols_a", l, j) for j in range(17)]
        plan += [("cols_b", l, j) for j in range(6)]
        plan += [("a_rows", l)]
        plan += [("a_chunk", l, g) for g in range(GROUPS)]
        plan += [("a_finish", l)]
        plan += [("b_values", l)]
        plan += [("b_chunk", l, c) for c in range(9)]
        for m in range(KD):
            for b in range(3):
                plan += [("gate", l, b, m), ("branch", l, b, m)]
        plan += [("merge_split", l)]
        plan += [("mix", l, m) for m in range(KD)]
        plan += [("norm_post", l, 1)]
        plan += [("norm_pre", l, 2)]
        for j in range(KF):
            plan += [("ffn_gate", l, j), ("ffn_up", l, j)]
        plan += [("ffn_out", l, m, q) for m in range(KD) for q in range(3)]
        plan += [("norm_post", l, 3)]
    plan += [("store_y",)]
    return plan


GEMMS = {"cols_c": "act", "cols_a": "act", "cols_b": "act", "gate": "act", "branch": "dve", "mix": "act",
         "ffn_gate": "dve", "ffn_up": "dve", "ffn_out": "act"}
UNSPLIT = {"branch"}


def view(ap, free, start=0):
    return bass.AP(tensor=ap.tensor, offset=ap.offset + start, ap=[list(ap.ap[0])] + [list(x) for x in free])


def build(nc, a, o):
    F32, F32R = mybir.dt.float32, mybir.dt.float32r
    ALU, ACT, AX = mybir.AluOpType, mybir.ActivationFunctionType, mybir.AxisListType
    plan = make_plan()
    const_at, const_np = shape_constants()
    NCONST = const_np.shape[1]
    consts_dram = nc.inline_tensor(const_np, name="shape_constants").ap()
    bias_dram = nc.dram_tensor("bias_skewed", (8, 64 * 256), F32, kind="Internal").ap()

    base = [(nc.sbuf_base + 63) // 64 * 64]
    limit = nc.sbuf_usable_end

    def region(nbytes):
        at = base[0]
        base[0] += (nbytes + 63) // 64 * 64
        assert base[0] <= limit, (base[0], limit)
        return at

    def place(name, shape, at, dt=F32):
        n = 4 * int(np.prod(shape[1:]))
        assert at + n <= limit, (name, at + n, limit)
        return nc.alloc_sbuf_tensor_at(name, shape, dt, offset=at)

    def fixed(name, shape, dt=F32):
        return place(name, shape, region(4 * int(np.prod(shape[1:]))), dt)

    cst = fixed("consts", [P, NCONST])
    prm = fixed("params", [P, DEPTH, NPARAM])
    half_w0a0 = fixed("half_w0a0", [P, DEPTH, 8])
    bias_p = fixed("bias_prompt", [P, 4, KEYS])
    bias_s = fixed("bias_sample", [P, 2, KEYS_S])
    lora = fixed("lora", [P, 1024])
    sinks = fixed("sinks", [P, 8])
    gate_bias = fixed("gate_bias", [P, 1])
    m_init = fixed("m_init", [P, 1])
    shift_out = fixed("shift_out", [P, 2 * CT])
    stats = fixed("stats", [P, 64])
    s_nat = fixed("c_state_natural", [P, 4, 64])
    s_out = fixed("c_state_out", [P, 4, 64])
    shift_rows = fixed("shift_rows", [2 * CT, P])
    x = fixed("x", [P, KD, T])
    xnh_at = region(2 * 4 * KD * T)
    xh = place("xn_high", [P, KD, T], xnh_at, F32R)
    xl = place("xn_low", [P, KD, T], xnh_at + 4 * KD * T, F32R)
    wraw = fixed("w_raw", [P, NRAW, 8, P])
    wh = fixed("w_high", [P, NSPLIT, 8, P], F32R)
    wl = fixed("w_low", [P, NSPLIT, 8, P], F32R)
    arena = base[0]
    cc_at = arena
    craw_at = (cc_at + 4 * CT * CW + 63) // 64 * 64
    acols_at = (craw_at + 4 * 2 * (CW + 1) + 63) // 64 * 64
    work = (acols_at + 4 * 16 * T + 63) // 64 * 64
    cc = place("c_cols", [P, CT, CW], cc_at)
    craw = place("c_raw", [P, 2, CW + 1], craw_at)
    acols = place("a_cols", [P, 16, T], acols_at)
    bq = place("b_queries", [P, 4 * T], (cc_at + 4 * 4 * CW + 63) // 64 * 64)
    bkv = place("b_keys_values", [P, 2, T], (cc_at + 4 * 4 * CW + 63) // 64 * 64 + 4 * 4 * T)
    bh = place("b_heads", [P, 4, T], work)
    merged = place("merged", [P, KD, T], acols_at + 4 * 4 * T)

    def worker(start):
        at = [start]

        def w(name, shape, dt=F32):
            t = place(name, shape, at[0], dt)
            at[0] += (4 * int(np.prod(shape[1:])) + 31) // 32 * 32
            return t
        return w

    w = worker(work)
    decay_log, in_rate, kk, scratch, kprime, cum = (w(n, [P, 512]) for n in (
        "c_decay_log", "c_in_rate", "c_kk", "c_scratch", "c_kprime", "c_cum"))
    kap_r = w("c_kappa_r", [P, 4, 2, P])
    tanh_w = w("c_tanh_w", [64, P])
    sig_g = w("c_sig_g", [P, P])
    vt, kt, bt = (w(n, [P, 512]) for n in ("c_v_tokens", "c_k_tokens", "c_b_tokens"))
    a_rb = w("c_a_rb", [P, 8, 2, 64])
    b_rk = w("c_b_rk", [P, 8, 2, 64])
    inv, invT, a_lev, w_lev, neg_z = (t[:].rearrange("p (h t) -> p h t", t=64) for t in (scratch, kk, decay_log, in_rate, kprime))
    rhs_z = w("c_rhs_z", [P, 8, 64])
    state = w("c_state", [P, 2, 4, 64])
    w = worker(work)
    r_li, r_lf, r_f, r_m, r_g, r_in, r_nm, r_wk = (w(n, [P, T]) for n in (
        "a_li", "a_lf", "a_f", "a_m", "a_g", "a_inter", "a_negm", "a_wk"))
    a_den = w("a_den", [P, 4, T])
    dexp, wts, qt, kw = (w(n, [P, 512]) for n in ("a_dexp", "a_weights", "a_q_inter", "a_k_weighted"))
    bcols_end = (cc_at + 4 * 4 * CW + 63) // 64 * 64 + 4 * 6 * T
    vo = place("a_values_ones", [P, 4, 256], (bcols_end + 31) // 32 * 32)
    cn = place("a_state", [P, 4, 256], (bcols_end + 31) // 32 * 32 + 4096)
    assert (bcols_end + 31) // 32 * 32 + 8192 <= cc_at + 4 * CT * CW
    a_cols_t = w("a_cols_tokens", [P, 8])
    a_dec = w("a_decay", [P, 4])
    m_prev = w("a_m_prev", [P, 8])
    g_last = w("a_g_last", [P, 8])
    ncol = w("a_n_col", [P, 4])
    c_diff = place("c_diff", [P, 2, CW], work)
    w = worker(work + 4 * 4096)
    sc = w("b_scores", [P, 4, KEYS])
    pt0 = w("b_probsT_first", [P, 512])
    pt1 = w("b_probsT_second", [P, 512])
    va = w("b_values_even", [P, 5, P])
    vb = w("b_values_odd", [P, 4, P])
    ks = w("b_keys_sample", [P, KEYS_S])
    kcache = w("b_k_cache", [P, P])
    vcache = w("b_v_cache", [P, P])
    kout = w("b_k_out", [P, 2, P])
    w = worker(work)
    squares = w("squares", [P, KD, T])
    mixed = w("mixed", [P, KD, T])
    rstd = w("rstd", [P, T])
    w = worker(work + 4 * 5120)
    gate_t = w("gate_tanh", [P, 2, T])
    prod = w("gate_product", [P, 2, T])
    w = worker(arena)
    hid_h = w("hidden_high", [P, KF, T], F32R)
    hid_l = w("hidden_low", [P, KF, T], F32R)
    ffn_t = w("ffn_tanh", [P, 2, T])
    ffn_p = w("ffn_product", [P, 2, T])
    assert work + 4 * 2 * KD * T <= limit
    ffn_y = place("ffn_y", [P, KD, T], xnh_at)
    sq2 = place("squares_ffn", [P, KD, T], arena)
    w = worker(arena)
    x_tok = w("x_tokens", [P, 5, D])
    prm_rows = w("param_rows", [P, DEPTH, P])
    bias_line = w("bias_line", [8, 256])
    table = w("bias_table", [32, 8])
    y_tok = place("y_tokens", [P, 5, D], arena)

    ctx = ExitStack()
    with ctx:
        gp = ctx.enter_context(nc.psum_tensor("psum_products", [P, 4, 512], F32))
        mp = [ctx.enter_context(nc.psum_tensor(f"psum_mixer{i}", [P, 512], F32)) for i in range(4)]
        nsem = [0]

        def sem(name):
            nsem[0] += 1
            return ctx.enter_context(nc.semaphore(name))

        def count(name):
            return Count(sem(name))

        def C(name, lo=0, n=None):
            at, width = const_at[name]
            return cst[:, at + lo:at + (width if n is None else lo + n)]

        bank = [Bank(f"bank{i}", mp[i], sem) for i in range(4)]
        landed = [count(f"weights_landed{i}") for i in range(NRAW)]
        high_ready, low_ready = count("w_high_ready"), count("w_low_ready")
        products = count("products_done")
        emptied = {r: count(f"products_emptied_by_{r}") for r in ("act", "dve")}
        xn_part, xh_ready, xl_ready = count("xn_ready"), count("xn_high_ready"), count("xn_low_ready")
        sq_ready = count("squares_ready")
        chains = {e: count(f"{e}_steps") for e in ("act", "dve", "pe", "pool")}
        ld_const, ld_x, ld_prm, ld_layer = (count(n) for n in ("consts_in", "x_in", "params_in", "layer_in"))
        bias_out, bias_in = count("bias_written"), count("bias_read")
        stored = count("outputs_stored")
        flows = {}

        def flow(name):
            if name not in flows:
                flows[name] = count(name)
            return flows[name]

        units = [s for s in plan if s[0] in GEMMS]
        unit_no = {s: i for i, s in enumerate(units)}
        split_no, unsplit_no, n_split, n_unsplit = {}, {}, 0, 0
        for s in units:
            if s[0] in UNSPLIT:
                unsplit_no[s] = n_unsplit
                n_unsplit += 1
            else:
                split_no[s] = n_split
                n_split += 1
        tiles, reads = {}, {"act": 0, "dve": 0}
        order = []
        for s in units:
            key = s[:3] if s[0] == "ffn_out" else s
            if key not in tiles:
                r = GEMMS[s[0]]
                reads[r] += 1
                tiles[key] = (len(order) % 2, r, reads[r])
                order.append(key)
        tile_no = {k: i for i, k in enumerate(order)}

        def unit_parts(s):
            kind, l = s[0], s[1]

            def cols(src, c0, n=P, m0=0, rows=None):
                v = src[l] if rows is None else src[l, rows[0]:rows[1]]
                nk = v.shape[0] // P
                return ((slice(0, P), slice(0, nk), slice(m0, m0 + n)),
                        v[:, c0:c0 + n].rearrange("(k p) m -> p k m", p=P))

            if kind == "cols_c":
                return [cols(a["w_in"], OFF_C + s[2] * P)]
            if kind == "cols_a":
                if s[2] < 16:
                    return [cols(a["w_in"], s[2] * P)]
                return [cols(a["w_in"], 4 * A_W, A_H, 0), cols(a["w_in"], 4 * A_W + A_H, A_H, 32)]
            if kind == "cols_b":
                if s[2] < 4:
                    return [cols(a["w_in"], OFF_B + s[2] * 64, 64, 0), cols(a["w_in"], OFF_B + 256 + s[2] * 64, 64, 64)]
                return [cols(a["w_in"], OFF_B + s[2] * P)]
            if kind == "gate":
                return [cols(a["w_in"], OFF_G + s[2] * D + s[3] * P)]
            if kind == "branch":
                c0 = s[3] * P
                if s[2] == 1:
                    v = a["w_branch_b"][l].rearrange("(v m d) n -> v d m n", v=2, d=64)
                    return [((slice(64 * i, 64 * i + 64), slice(0, 4), slice(0, P)), v[i, :, :, c0:c0 + P])
                            for i in range(2)]
                return [cols(a["w_branch_a" if s[2] == 0 else "w_branch_c"], c0)]
            if kind == "mix":
                return [cols(a["w_out"], s[2] * P)]
            if kind == "ffn_gate":
                return [cols(a["w_ffn_in"], s[2] * P)]
            if kind == "ffn_up":
                return [cols(a["w_ffn_in"], D_FF + s[2] * P)]
            k0 = 8 * s[3]
            return [cols(a["w_ffn_out"], s[2] * P, rows=(k0 * P, min(k0 + 8, KF) * P))]

        landed_at = {}
        tot = [0] * NRAW
        for i, s in enumerate(units):
            tot[i % NRAW] += 16 * len(unit_parts(s))
            landed_at[s] = (i % NRAW, tot[i % NRAW])

        def nk_of(s):
            return 4 if s[0] == "branch" else (min(8, KF - 8 * s[3]) if s[0] == "ffn_out" else 8)

        def pair_view(pair, lo=0, hi=P):
            return gp[lo:hi, 2 * pair:2 * pair + 2, 0:HALF]

        def halves(ap):
            return ap.rearrange("p (b n) -> p b n", b=2)

        def c_group(g):
            return (P, P * g, 2, 64) if g < 4 else (TS, TP + 1, 1, TS)

        def gv(t, n):
            return t[:, 0:4 * n].rearrange("p (f n) -> p f n", n=n)

        def pb(l, name, n, width):
            at = PARAM_AT[name]
            return view(prm[:, l, at:at + n], [[1, n], [0, width]])

        block = ctx.enter_context(nc.Block())

        @block.tensor
        def _(pe):
            def mm(out, lhsT, rhs, start=True, stop=True):
                return pe.matmul(out, lhsT, rhs, start=start, stop=stop, skip_group_check=True)

            def order_after(ins):
                chains["pe"].inc(ins)
                pe.wait_ge(chains["pe"].sem, chains["pe"].value)

            def gemm(s, rh=None, rl=None, rhs=None, first=True, last=True, cut=HALF, wait_k=False, k0=0, nk=8, spare=False):
                key = s[:3] if s[0] == "ffn_out" else s
                pair, reader, turn = tiles[key]
                if s in split_no:
                    n = split_no[s]
                    pe.wait_ge(low_ready.sem, n + 1)
                    slot = n % NSPLIT
                else:
                    at, value = landed_at[s]
                    pe.wait_ge(landed[at].sem, value)
                    slot = unit_no[s] % NRAW
                if first and tile_no[key] >= 2:
                    _, r, t = tiles[order[tile_no[key] - 2]]
                    pe.wait_ge(emptied[r].sem, t)
                for k in range(nk):
                    if wait_k:
                        xl_ready.wait_next(pe, "pe")
                    if rhs is None:
                        passes = [(wh[:, slot, k], rh[:, k0 + k]), (wh[:, slot, k], rl[:, k0 + k]),
                                  (wl[:, slot, k], rh[:, k0 + k])]
                    else:
                        passes = [(wraw[:, slot, k], rhs[k])]
                    for i, (wt, act_) in enumerate(passes):
                        pieces = [(0, 0, 0, cut), (1, 0, cut, T - cut)]
                        if spare:
                            pieces = [(0, 0, 0, cut), (1, 0, cut, TP - cut), (1, TP - cut, TP + 1, TS)]
                        for b, to, at, n in pieces:
                            last_mm = mm(gp[:, 2 * pair + b, to:to + n], wt, act_[:, at:at + n],
                                         start=first and k == 0 and i == 0 and to == 0,
                                         stop=last and k == nk - 1 and i == len(passes) - 1)
                products.inc(last_mm)

            def sum_squares(src):
                bank[0].claim(pe)
                bank[1].claim(pe)
                for k in range(KD):
                    sq_ready.wait_next(pe, "pe")
                    for b in range(2):
                        last = mm(mp[b][:, 0:HALF], C("ones"), src[:, k, b * HALF:(b + 1) * HALF],
                                  start=(k == 0), stop=(k == KD - 1))
                        if k == KD - 1:
                            bank[b].filled(last, "act")

            def load_x():
                pe.wait_ge(ld_const.sem, 32)
                pe.wait_ge(ld_prm.sem, 16 * DEPTH * len(PARAM_ROWS))
                bank[0].claim(pe)
                for l in range(DEPTH):
                    last = pe.transpose(mp[0][:, l * P:l * P + NPARAM], prm_rows[0:NPARAM, l, :], C("ident")[0:NPARAM, 0:NPARAM])
                bank[0].filled(last, "act")
                bank[1].claim(pe)
                bank[1].filled(mm(mp[1][0:8, 0:256], table[:], C("bucket_hot")[0:32]), "dve")
                pe.wait_ge(ld_x.sem, 16 * 5)
                for k in range(KD):
                    b = bank[2 + k % 2]
                    b.claim(pe)
                    for t in range(4):
                        last = pe.transpose(b.t[:, t * P:(t + 1) * P], x_tok[:, t, k * P:(k + 1) * P], C("ident"))
                    b.filled(last, "act" if k % 2 else "dve")
                bank[0].claim(pe)
                for k in range(KD):
                    last = pe.transpose(mp[0][:, k * TS:(k + 1) * TS], x_tok[0:TS, 4, k * P:(k + 1) * P],
                                        C("ident")[0:TS, 0:TS])
                bank[0].filled(last, "act")

            def c_shift_out():
                flow("shift_cols").wait_next(pe, "pe")
                bank[0].claim(pe)
                bank[0].filled(pe.transpose(mp[0][0:2 * CT, 0:P], shift_out[:], C("ident")), "act")

            def c_prep(l, g):
                n, at, nch, L = c_group(g)
                if g == 0:
                    pe.wait_ge(ld_layer.sem, 16 * 12 * (l + 1))
                bank[0].claim(pe)
                flow("c_tanh_w").wait_next(pe, "pe")
                for f in range(4):
                    last = mm(mp[0][:, f * n:(f + 1) * n], lora[0:64, f * P:(f + 1) * P], tanh_w[:, 0:n])
                bank[0].filled(last, "act", ("c_lw", l, g))
                bank[1].claim(pe)
                for f in range(4):
                    last = mm(mp[1][:, f * n:(f + 1) * n], lora[64:128, f * P:(f + 1) * P], cc[64:128, 12, at:at + n])
                bank[1].filled(last, "act", ("c_la", l, g))
                bank[2].claim(pe)
                flow("c_kk_sq").wait_next(pe, "pe")
                bank[2].filled(mm(mp[2][:, 0:4 * n], C("headones"), scratch[:, 0:4 * n]), "dve")
                bank[0].claim(pe)
                for f in range(4):
                    last = pe.transpose(mp[0][0:n, f * P:(f + 1) * P], cc[:, 8 + f, at:at + n], C("ident"))
                bank[0].filled(last, "act")
                bank[3].claim(pe)
                flow("c_rk").wait_next(pe, "pe")
                bank[3].filled(mm(mp[3][:, 0:4 * n], C("headones"), scratch[:, 0:4 * n]), "dve")
                flow("c_scaled").wait_next(pe, "pe")
                for b, src in ((1, kprime), (2, in_rate)):
                    bank[b].claim(pe)
                    for f in range(4):
                        last = pe.transpose(mp[b][0:n, f * P:(f + 1) * P], gv(src, n)[:, f, :], C("ident"))
                    bank[b].filled(last, "act")

            def heads():
                for p in range(4):
                    for q in range(2):
                        yield 2 * p + q, p, q

            def c_gram(l, g):
                n, at, nch, L = c_group(g)

                def grams(banks, src, q):
                    for p in range(4):
                        h = 2 * p + q
                        for c in range(nch):
                            out = mp[banks[h // 4]][64 * c:64 * c + L, (h % 4) * 2 * L:(h % 4 + 1) * 2 * L]
                            last = mm(out.rearrange("p (u t) -> p u t", u=2),
                                      gv(src, n)[64 * q:64 * q + 64, p, c * L:c * L + L],
                                      kap_r[64 * q:64 * q + 64, p, :, c * L:c * L + L])
                        if p % 2 == 1:
                            ends.append((banks[h // 4], last))

                ends = []
                for b in (0, 3, 1):
                    bank[b].claim(pe)
                grams((0, 3), in_rate, 0)
                for q in range(2):
                    for p in range(4):
                        for c in range(nch):
                            last = mm(mp[1][64 * c:64 * c + L, (2 * p + q) * L:(2 * p + q + 1) * L],
                                      kap_r[64 * q:64 * q + 64, p, 0, c * L:c * L + L],
                                      gv(in_rate, n)[64 * q:64 * q + 64, p, c * L:c * L + L])
                    if q == 0:
                        order_after(last)
                        ends = []
                        grams((0, 3), in_rate, 1)
                        for b, ins in ends:
                            bank[b].filled(ins, "dve")
                bank[1].filled(last, "dve")
                bank[2].claim(pe)
                bank[0].claim(pe)
                ends = []
                grams((2, 0), kprime, 1)
                order_after(ends[-1][1])
                ends = []
                grams((2, 0), kprime, 0)
                for b, ins in ends:
                    bank[b].filled(ins, "dve")

            def c_invert(l, g):
                n, at, nch, L = c_group(g)
                levels = 6 if L == 64 else 5

                def product(b, lhsT, rhs, reader):
                    bank[b].claim(pe)
                    for h in range(8):
                        for c in range(nch):
                            r = slice(64 * c, 64 * c + L)
                            last = mm(mp[b][r, h * L:(h + 1) * L], lhsT[r, h, 0:L], rhs[r, h, 0:L])
                    bank[b].filled(last, reader)

                for k in range(1, levels):
                    flow("c_level").wait_next(pe, "pe")
                    product(1, a_lev, inv, "act")
                    bank[1].claim(pe)
                    if k < levels - 1:
                        product(3, invT, w_lev, "dve")
                    product(2, w_lev, invT, "dve")

            def c_chain(l, g):
                n, at, nch, L = c_group(g)
                if g == 4:
                    pe.wait_ge(flow("c_state_in").sem, 16 * (l + 1))
                    bank[0].claim(pe)
                    for h, p, q in heads():
                        last = mm(mp[0][64 * q:64 * q + 64, p * 64:(p + 1) * 64], s_nat[64 * q:64 * q + 64, p, :],
                                  C("ident")[64 * q:64 * q + 64, 64 * q:64 * q + 64])
                    bank[0].filled(last, "dve")
                for c in range(nch):
                    r = slice(64 * c, 64 * c + L)
                    cur = (2 * g + c) % 2
                    bank[0].claim(pe)
                    for h in range(8):
                        last = mm(mp[0][r, h * 64:(h + 1) * 64], b_rk[r, h, 0, 0:L], vt[r, h * 64:(h + 1) * 64],
                                  start=h == 0, stop=False)
                    order_after(last)
                    flow("c_state").wait_next(pe, "pe")
                    for q in (c, 1 - c):
                        for p in range(4):
                            last = mm(mp[0][r, (2 * p + q) * 64:(2 * p + q + 1) * 64],
                                      kap_r[64 * q:64 * q + 64, p, 0, c * L:c * L + L],
                                      state[64 * q:64 * q + 64, cur, p, :], start=False, stop=q != c)
                        if q == c:
                            order_after(last)
                    bank[0].filled(last, "dve")
                    bank[3].claim(pe)
                    for h, p, q in heads():
                        last = mm(mp[3][64 * q:64 * q + 64, p * L:(p + 1) * L], state[64 * q:64 * q + 64, cur, p, :],
                                  kap_r[64 * q:64 * q + 64, p, 1, c * L:c * L + L], start=p == 0, stop=False)
                    order_after(last)
                    bank[1].claim(pe)
                    bank[0].claim(pe)
                    for h in range(8):
                        last = mm(mp[1][r, h * 64:(h + 1) * 64], invT[r, h, 0:L], rhs_z[r, h, :])
                    bank[1].filled(last, "dve")
                    bank[2].claim(pe)
                    bank[1].claim(pe)
                    for h, p, q in heads():
                        out = mp[2][64 * q:64 * q + 64, p * 64:(p + 1) * 64]
                        mm(out, kt[r, h * 64:(h + 1) * 64], vt[r, h * 64:(h + 1) * 64], stop=False)
                        last = mm(out, bt[r, h * 64:(h + 1) * 64], neg_z[r, h, :], start=False)
                    bank[2].filled(last, "dve")
                    for h, p, q in heads():
                        out = mp[3][64 * q:64 * q + 64, p * L:(p + 1) * L]
                        mm(out, vt[r, h * 64:(h + 1) * 64], b_rk[r, h, 1, 0:L], start=False, stop=False)
                        last = mm(out, neg_z[r, h, :], a_rb[r, h, 1, 0:L], start=False)
                    bank[3].filled(last, "act")

            def c_finish(l, g):
                n, at, nch, L = c_group(g)
                y = cc[:, 0:4, at:at + n]
                bank[0].claim(pe)
                bank[3].claim(pe)
                bank[0].filled(mm(mp[0][:, 0:4 * n], C("headones"), y), "dve")
                bank[1].claim(pe)
                flow("c_gate_in").wait_next(pe, "pe")
                for f in range(4):
                    last = mm(mp[1][:, f * n:(f + 1) * n], lora[:, 512 + f * P:512 + (f + 1) * P], sig_g[:, 0:n])
                bank[1].filled(last, "act")
                bank[2].claim(pe)
                flow("c_dev_sq").wait_next(pe, "pe")
                bank[2].filled(mm(mp[2][:, 0:4 * n], C("headones"), scratch[:, 0:4 * n]), "act")
                if g >= 3:
                    flow("c_state").wait_next(pe, "pe")
                    cur = 0 if g == 3 else 1
                    bank[3].claim(pe)
                    for h, p, q in heads():
                        last = mm(mp[3][64 * q:64 * q + 64, p * 64:(p + 1) * 64], state[64 * q:64 * q + 64, cur, p, :],
                                  C("ident")[64 * q:64 * q + 64, 64 * q:64 * q + 64])
                    bank[3].filled(last, "act", ("c_state", l, g))

            def a_chunk(l, g):
                n, at = group(g)
                if g == 0:
                    flow("a_rows").wait_next(pe, "pe")
                sel = lambda h, m: C("sel")[0:4, h * P:h * P + m]
                bank[0].claim(pe)
                for h in range(4):
                    last = mm(mp[0][0:n, h * n:(h + 1) * n], sel(h, n), r_g[0:4, at:at + n])
                bank[0].filled(last, "dve", ("a_g", l, g))
                bank[1].claim(pe)
                for h in range(4):
                    last = mm(mp[1][:, h * n:(h + 1) * n], sel(h, P), r_in[0:4, at:at + n])
                bank[1].filled(last, "dve")
                bank[2].claim(pe)
                mm(mp[2][0:n, 0:4], r_li[0:4, at:at + n], C("ident")[0:4, 0:4])
                bank[2].filled(mm(mp[2][0:n, 4:8], r_wk[0:4, at:at + n], C("ident")[0:4, 0:4]), "act")
                bank[3].claim(pe)
                for h in range(4):
                    last = mm(mp[3][0:n, h * n:(h + 1) * n], acols[:, 4 + h, at:at + n], acols[:, h, at:at + n])
                bank[3].filled(last, "dve")
                for b, c0 in ((0, 4), (1, 8)):
                    bank[b].claim(pe)
                    for h in range(4):
                        last = pe.transpose(mp[b][0:n, h * P:(h + 1) * P], acols[:, c0 + h, at:at + n], C("ident"))
                    bank[b].filled(last, "act")
                bank[0].claim(pe)
                for h in range(4):
                    last = mm(mp[0][:, h * n:(h + 1) * n], sel(h, P), r_nm[0:4, at:at + n])
                bank[0].filled(last, "dve")
                bank[3].claim(pe)
                bank[1].claim(pe)
                if g == 4:
                    flow("a_n_spread").wait_next(pe, "pe")
                for b, c0, mark in ((3, P, ("a_den", l, g)), (2, 0, None)):
                    bank[b].claim(pe)
                    for h in range(4):
                        out = mp[b][:, h * n:(h + 1) * n]
                        mm(out, vo[0:n, h, c0:c0 + P], wts[0:n, h * n:(h + 1) * n], stop=False)
                        last = mm(out, cn[:, h, c0:c0 + P], qt[:, h * n:(h + 1) * n], start=False)
                    bank[b].filled(last, "act", mark)
                for b in range(2):
                    bank[1 + b].claim(pe)
                    for i in range(2):
                        h = 2 * b + i
                        last = mm(mp[1 + b][:, i * 256:(i + 1) * 256], kw[0:n, h * P:(h + 1) * P], vo[0:n, h, :])
                    bank[1 + b].filled(last, "dve", ("a_state", l, g))

            def a_finish(l):
                for h in range(4):
                    flow("a_h_sq").wait_next(pe, "pe")
                    for b in range(2):
                        bk = 2 * (h % 2) + b
                        bank[bk].claim(pe)
                        bank[bk].filled(mm(mp[bk][:, 0:HALF], C("ones"), (r_li, r_wk)[h % 2][:, b * HALF:(b + 1) * HALF]),
                                        "dve", ("a_norm", l, h))

            def b_values(l):
                bank[0].claim(pe)
                for j in range(4):
                    last = pe.transpose(mp[0][:, j * P:(j + 1) * P], bkv[:, 1, j * P:(j + 1) * P], C("ident"))
                bank[0].filled(last, "act")
                bank[1].claim(pe)
                for j in range(4):
                    m = P if j < 3 else 64
                    last = pe.transpose(mp[1][0:m, j * P:(j + 1) * P], bkv[:, 1, 64 + j * P:64 + j * P + m], C("ident"))
                bank[1].filled(last, "dve")
                bank[2].claim(pe)
                pe.transpose(mp[2][:, 0:P], bkv[:, 0, TP - P:TP], C("ident"))
                pe.transpose(mp[2][0:TS, P:2 * P], bkv[:, 0, TP:T], C("ident"))
                bank[2].filled(pe.transpose(mp[2][0:TS, 2 * P:3 * P], bkv[:, 1, TP:T], C("ident")), "act", ("b_values", l))
                bank[3].claim(pe)
                pe.wait_ge(flow("b_cache_in").sem, 32 * (l + 1))
                bank[3].filled(pe.transpose(mp[3][:, 0:P], kcache[:], C("ident")), "dve")

            def b_chunk(l, c):
                sample = c == 8
                if c == 0:
                    flow("b_values").wait_next(pe, "pe")
                if sample:
                    n, nk, nt, at = TS, KEYS_S, 2, TP
                    keys = ks[:, :]
                else:
                    n, nt, at = CHUNK, 4, CHUNK * c
                    nk = CHUNK * min(3, c + 1)
                    keys = bkv[:, 0, at + CHUNK - nk:at + CHUNK]
                per = nt // 2
                hpt = P // n
                first_n, second_n = min(nk, P), max(nk - P, 0)
                for v in range(2):
                    r = slice(64 * v, 64 * v + 64)
                    bank[v].claim(pe)
                    for i in range(per):
                        last = mm(mp[v][:, i * nk:(i + 1) * nk], bq[r, 4 * at + i * P:4 * at + (i + 1) * P], keys[r, :])
                    bank[v].filled(last, "dve")
                flow("b_probs").wait_next(pe, "pe")
                bank[2].claim(pe)
                for t in range(nt):
                    last = pe.transpose(mp[2][0:first_n, t * P:(t + 1) * P], sc[:, t, 0:first_n], C("ident"))
                bank[2].filled(last, "act")
                if second_n:
                    bank[3].claim(pe)
                    for t in range(nt):
                        last = pe.transpose(mp[3][0:second_n, t * P:(t + 1) * P], sc[:, t, P:P + second_n], C("ident"))
                    bank[3].filled(last, "dve")
                    bank[3].claim(pe)
                bank[2].claim(pe)
                bank[0].claim(pe)
                for t in range(nt):
                    v, i = t // per, t % per
                    r = slice(64 * v, 64 * v + 64)
                    if sample:
                        va0, va1 = vcache[:, r], va[0:TS, 4, r]
                    else:
                        start = at + CHUNK - nk
                        src = va if start % P == 0 else vb
                        j = start // P
                        va0, va1 = src[0:first_n, j, r], (src[0:64, j + 1, r] if second_n else None)
                    out = mp[0][r, i * P:(i + 1) * P]
                    last = mm(out, va0, pt0[0:first_n, t * P:(t + 1) * P], stop=not second_n)
                    if second_n:
                        last = mm(out, va1, pt1[0:second_n, t * P:(t + 1) * P], start=False)
                bank[0].filled(last, "act")

            def store_y():
                for t in range(5):
                    n, at = group(t)
                    for b in range(2):
                        bk = 2 * (t % 2) + b
                        bank[bk].claim(pe)
                        for k in range(4):
                            last = pe.transpose(mp[bk][0:n, k * P:(k + 1) * P], x[:, 4 * b + k, at:at + n], C("ident"))
                        bank[bk].filled(last, "act" if b else "dve", ("y", t, b))

            first_user = {}
            for s in plan:
                kind = s[0]
                if kind == "load_x":
                    load_x()
                elif kind == "norm_pre":
                    sum_squares(squares if s[2] == 0 or s[2] == 2 else sq2)
                    first_user["norm"] = True
                elif kind == "norm_post":
                    sum_squares(squares if s[2] == 1 else sq2)
                elif kind in ("cols_c", "cols_a", "cols_b", "gate", "ffn_gate", "ffn_up"):
                    gemm(s, rh=xh, rl=xl, cut=SPLIT_C if kind == "cols_c" or (kind == "cols_b" and s[2] < 4) else HALF, wait_k=first_user.pop("norm", False))
                elif kind == "branch":
                    if s[3] == 0:
                        if s[2] == 0:
                            flow("a_h").wait_next(pe, "pe")
                        elif s[2] == 1:
                            bank[0].claim(pe)
                        else:
                            flow("c_h").wait_next(pe, "pe", GROUPS)
                    gemm(s, rhs=[(acols, bh, cc)[s[2]][:, k, :] for k in range(4)], nk=4, spare=s[2] == 2)
                elif kind == "merge_split":
                    pass
                elif kind == "mix":
                    gemm(s, rh=xh, rl=xl, wait_k=s[2] == 0)
                elif kind == "ffn_out":
                    l, m, q = s[1:]
                    if m == 0 and q == 0:
                        flow("hidden").wait_next(pe, "pe", KF)
                    gemm(s, rh=hid_h, rl=hid_l, k0=8 * q, nk=nk_of(s), first=q == 0, last=q == 2)
                elif kind == "c_shift_out":
                    c_shift_out()
                elif kind == "store_y":
                    pe.wait_ge(flow("x_new").sem, KD * 2 * DEPTH)
                    store_y()
                else:
                    {"c_prep": c_prep, "c_gram": c_gram, "c_invert": c_invert, "c_chain": c_chain, "c_finish": c_finish,
                     "a_rows": lambda l: None, "a_chunk": a_chunk, "a_finish": a_finish, "b_values": b_values,
                     "b_chunk": b_chunk}[kind](*s[1:])

        @block.scalar
        def _(act):
            step = Lane(act, chains["act"])

            def fn(out, in_, f, **kw_):
                return act.activation(out, in_, f, **kw_)

            def split_high(n):
                if n >= n_split:
                    return
                s = split_units[n]
                if n >= NSPLIT:
                    act.wait_ge(products.sem, unit_no[split_units[n - NSPLIT]] + 1)
                at, value = landed_at[s]
                act.wait_ge(landed[at].sem, value)
                nk = nk_of(s)
                high_ready.inc(fn(wh[:, n % NSPLIT, 0:nk], wraw[:, unit_no[s] % NRAW, 0:nk], ACT.Copy))

            def product_done(s):
                act.wait_ge(products.sem, unit_no[s] + 1)
                return tiles[s[:3] if s[0] == "ffn_out" else s][0]

            def load_x():
                act.wait_ge(ld_const.sem, 32)
                bank[0].read(act, "act")
                step(fn(prm[:, :, :], mp[0][:, 0:DEPTH * P].rearrange("p (l n) -> p l n", n=P)[:, :, 0:NPARAM], ACT.Copy),
                     bank[0].empty["act"])
                for k in range(1, KD, 2):
                    bank[3].read(act, "act")
                    step(fn(x[:, k, 0:TP], mp[3][:], ACT.Copy), bank[3].empty["act"])
                bank[0].read(act, "act")
                step(fn(x[:, :, TP:T], mp[0][:, 0:KD * TS].rearrange("p (k n) -> p k n", n=TS), ACT.Copy), bank[0].empty["act"])
                flow("x_even").wait_next(act, "act", 4)

            def norm(src, sq, which):
                for k in range(KD):
                    if which in ("x", "x_new"):
                        if which == "x_new":
                            flow("x_new").wait_next(act, "act")
                    sq_ready.inc(fn(sq[:, k, :], src[:, k, :], ACT.Square))
                for b in range(2):
                    bank[b].read(act, "act")
                    step(fn(rstd[:, b * HALF:(b + 1) * HALF], mp[b][:, 0:HALF], ACT.Ln, scale=1.0 / D,
                            bias=C("scalars", 0, 1)), bank[b].empty["act"])
                step(fn(rstd[:], rstd[:], ACT.Exp, scale=-0.5), flow("rstd"))

            def norm_pre(l, w_):
                norm(x, squares, "x" if l == 0 and w_ == 0 else "x_new")
                for k in range(KD):
                    xn_part.wait_next(act, "act")
                    xh_ready.inc(fn(xh[:, k, :], squares[:, k, :], ACT.Copy))

            def norm_post(l, w_):
                if w_ == 1:
                    norm(mixed, squares, "")
                else:
                    norm(ffn_y, sq2, "")

            def cols_c(s):
                l, j = s[1:]
                i = l * CT + j
                pair = product_done(s)
                if i >= 2:
                    act.wait_ge(flow("c_col").sem, i - 1)
                step(fn(craw[:, j % 2, 1:1 + TP].rearrange("p (b n) -> p b n", b=2),
                        gp[:, 2 * pair:2 * pair + 2, 0:SPLIT_C], ACT.Copy))
                step(fn(craw[:, j % 2, TP + 2:TP + 2 + TS], gp[:, 2 * pair + 1, SPLIT_C:SPLIT_C + TS], ACT.Copy),
                     emptied["act"])
                at = PARAM_AT["state_rwkv_shift"] + j
                step(fn(craw[:, j % 2, TP + 1:TP + 2], prm[:, l, at:at + 1], ACT.Copy), flow("c_raw"))

            def c_shift_out(l):
                bank[0].read(act, "act")
                if l > 0:
                    act.wait_ge(flow("shift_stored").sem, 32 * l)
                step(fn(shift_rows[:], mp[0][0:2 * CT, 0:P], ACT.Copy), bank[0].empty["act"])
                step(fn(stats[0:1, 60:61], stats[0:1, 60:61], ACT.Copy), flow("shift_rows"))

            def c_prep(l, g):
                n, at, nch, L = c_group(g)
                if g == 0:
                    act.wait_ge(flow("c_col").sem, CT * (l + 1))
                step(fn(tanh_w[:, 0:n], cc[0:64, 12, at:at + n], ACT.Tanh), flow("c_tanh_w"))
                step(fn(sig_g[:, 0:n], cc[:, 13, at:at + n], ACT.Tanh, scale=0.5), flow("c_sig_raw"))
                for b, dst, name in ((0, decay_log, "c_lw"), (1, in_rate, "c_la")):
                    bank[b].read(act, "act")
                    for f in range(4):
                        ins = fn(gv(dst, n)[:, f, :], mp[b][:, f * n:(f + 1) * n], ACT.Tanh, scale=0.5,
                                 bias=half_w0a0[:, l, 4 * b + f:4 * b + f + 1])
                        step(ins, bank[b].empty["act"] if f == 3 else None)
                    if b == 0:
                        flow("c_kk_raw").wait_next(act, "act")
                        step(fn(scratch[:, 0:4 * n], kk[:, 0:4 * n], ACT.Square), flow("c_kk_sq"))
                flow("c_ss").wait_next(act, "act")
                step(fn(kprime[:, 0:4 * n], kprime[:, 0:4 * n], ACT.Ln, scale=float(2 ** 20)))
                step(fn(kprime[:, 0:4 * n], kprime[:, 0:4 * n], ACT.Exp, scale=-0.5, bias=C("scalars", 2, 1)), flow("c_rn"))
                bank[0].read(act, "act")
                step(fn(vt[0:n, :], mp[0][0:n, :], ACT.Copy), bank[0].empty["act"])
                flow("c_cum").wait_next(act, "act")
                en = rhs_z[:, :, :].rearrange("p a b -> p (a b)")[:, 0:4 * n]
                step(fn(en, cum[:, 0:4 * n], ACT.Exp, scale=-1.0))
                step(fn(cum[:, 0:4 * n], cum[:, 0:4 * n], ACT.Exp))
                step(fn(decay_log[:, 0:4 * n], decay_log[:, 0:4 * n], ACT.Exp), flow("c_exps"))
                for b, dst in ((1, kt), (2, bt)):
                    bank[b].read(act, "act")
                    step(fn(dst[0:n, :], mp[b][0:n, :], ACT.Copy), bank[b].empty["act"])

            def c_invert(l, g):
                n, at, nch, L = c_group(g)
                for k in range(1, 6 if L == 64 else 5):
                    bank[1].read(act, "act")
                    step(fn(w_lev[0:n, :, 0:L], mp[1][0:n, 0:8 * L].rearrange("p (h t) -> p h t", t=L), ACT.Copy),
                         bank[1].empty["act"])

            def c_chain(l, g):
                n, at, nch, L = c_group(g)
                for c in range(nch):
                    bank[3].read(act, "act")
                    step(fn(cc[:, 0:4, at + c * L:at + c * L + L], mp[3][:, 0:4 * L].rearrange("p (f t) -> p f t", t=L),
                            ACT.Copy), bank[3].empty["act"])

            def c_finish(l, g):
                n, at, nch, L = c_group(g)
                flow("c_dev").wait_next(act, "act")
                step(fn(scratch[:, 0:4 * n], kk[:, 0:4 * n], ACT.Square), flow("c_dev_sq"))
                bank[1].read(act, "act")
                step(fn(cum[:, 0:4 * n], mp[1][:, 0:4 * n], ACT.Copy), bank[1].empty["act"])
                bank[2].read(act, "act")
                step(fn(kprime[:, 0:4 * n], mp[2][:, 0:4 * n], ACT.Ln, scale=1.0 / 64, bias=C("scalars", 1, 1)),
                     bank[2].empty["act"])
                step(fn(kprime[:, 0:4 * n], kprime[:, 0:4 * n], ACT.Exp, scale=-0.5), flow("c_gn_r"))
                if g >= 3:
                    bank[3].read(act, "act")
                    before = 2 * l + g - 3
                    if before:
                        act.wait_ge(flow("c_state_stored").sem, 16 * before)
                    step(fn(s_out[:, :, :], mp[3][:, 0:256].rearrange("p (f t) -> p f t", t=64), ACT.Copy),
                         bank[3].empty["act"])

            def cols_a(s):
                l, j = s[1:]
                pair = product_done(s)
                if j < 16:
                    step(fn(halves(acols[:, j, :]), pair_view(pair), ACT.Copy), emptied["act"])
                    return
                act.wait_ge(flow("c_h").sem, GROUPS * (l + 1))
                step(fn(halves(r_li[0:4, :]), pair_view(pair, 0, 4), ACT.Identity, bias=gate_bias[0:4, :]))
                step(fn(halves(r_nm[32:36, :]), pair_view(pair, 32, 36), ACT.Identity, bias=gate_bias[32:36, :]),
                     emptied["act"])

            def cols_b(s):
                l, j = s[1:]
                pair = product_done(s)
                act.wait_ge(flow("c_h").sem, GROUPS * (l + 1))
                if j < 4:
                    step(fn(view(bq[:], [[4 * SPLIT_C, 2], [SPLIT_C, 4], [1, CHUNK]], CHUNK * j),
                            gp[:, 2 * pair:2 * pair + 2, 0:SPLIT_C].rearrange("p b (c t) -> p b c t", t=CHUNK), ACT.Copy))
                    step(fn(bq[:, 4 * TP + TS * j:4 * TP + TS * (j + 1)], gp[:, 2 * pair + 1, SPLIT_C:SPLIT_C + TS], ACT.Copy),
                         emptied["act"])
                    return
                step(fn(halves(bkv[:, j - 4, :]), pair_view(pair), ACT.Copy), emptied["act"])

            def a_rows(l):
                flow("a_abs").wait_next(act, "act")
                step(fn(r_wk[0:4, :], r_g[0:4, :], ACT.Exp))
                step(fn(r_wk[0:4, :], r_wk[0:4, :], ACT.Ln, bias=C("scalars", 3, 1)[0:4]), flow("a_ln"))
                flow("a_exp_in").wait_next(act, "act")
                step(fn(r_in[0:4, :], r_in[0:4, :], ACT.Exp))
                step(fn(r_wk[0:4, :], r_wk[0:4, :], ACT.Exp))
                step(fn(r_nm[0:4, :], r_m[0:4, :], ACT.Exp, scale=-1.0), flow("a_rows"))

            def a_chunk(l, g):
                n, at = group(g)
                bank[2].read(act, "act")
                step(fn(a_cols_t[0:n, :], mp[2][0:n, 0:8], ACT.Copy), bank[2].empty["act"])
                step(fn(a_cols_t[0:n, 4:8], a_cols_t[0:n, 4:8], ACT.Copy, scale=P ** -0.5), flow("a_cols_t"))
                bank[0].wait_emptied(act, ("a_g", l, g))
                step(fn(dexp[0:n, 0:4 * n], dexp[0:n, 0:4 * n], ACT.Exp), flow("a_dexp"))
                bank[0].read(act, "act")
                for h in range(4):
                    step(fn(kw[0:n, h * P:(h + 1) * P], mp[0][0:n, h * P:(h + 1) * P], ACT.Copy,
                            scale=a_cols_t[0:n, 4 + h:5 + h]), bank[0].empty["act"] if h == 3 else None)
                bank[1].read(act, "act")
                step(fn(vo[0:n, :, 0:P], mp[1][0:n, :].rearrange("p (h v) -> p h v", v=P), ACT.Copy), bank[1].empty["act"])
                bank[3].read(act, "act")
                step(fn(a_den[:, :, at:at + n], gv(mp[3], n), ACT.Abs), bank[3].empty["act"])
                bank[2].read(act, "act")
                step(fn(acols[:, 0:4, at:at + n], mp[2][:, 0:4 * n].rearrange("p (h t) -> p h t", t=n), ACT.Copy),
                     bank[2].empty["act"])

            def a_finish(l):
                step(fn(acols[:, 12:16, :], acols[:, 12:16, :], ACT.Tanh, scale=0.5), flow("a_o_tanh"))
                flow("a_den_ok").wait_next(act, "act")
                step(fn(a_den[:], a_den[:], ACT.Square), flow("a_den_sq"))
                for h in range(4):
                    if h >= 2:
                        bank[2 * (h % 2) + 1].wait_emptied(act, ("a_norm", l, h - 2))
                    step(fn((r_li, r_wk)[h % 2][:], acols[:, h, :], ACT.Square), flow("a_h_sq"))
                for h in range(4):
                    bank[2 * (h % 2) + 1].wait_emptied(act, ("a_norm", l, h))
                    step(fn(a_den[:, h, :], a_den[:, h, :], ACT.Ln, scale=1.0 / P))
                    step(fn(a_den[:, h, :], a_den[:, h, :], ACT.Exp, scale=-0.5), flow("a_r"))

            def b_values(l):
                flow("a_h").wait_next(act, "act")
                bank[0].read(act, "act")
                step(fn(va[:, 0:4, :], mp[0][:].rearrange("p (j d) -> p j d", d=P), ACT.Copy), bank[0].empty["act"])
                bank[2].read(act, "act")
                step(fn(kout[:, 0, :], mp[2][:, 0:P], ACT.Copy))
                step(fn(kout[0:TS, 1, :], mp[2][0:TS, P:2 * P], ACT.Copy))
                step(fn(va[0:TS, 4, :], mp[2][0:TS, 2 * P:3 * P], ACT.Copy), bank[2].empty["act"])

            def b_chunk(l, c):
                sample = c == 8
                n, nt, at = (TS, 2, TP) if sample else (CHUNK, 4, CHUNK * c)
                nk = KEYS_S if sample else CHUNK * min(3, c + 1)
                flow("b_max").wait_next(act, "act")
                for t in range(nt):
                    step(fn(sc[:, t, 0:nk], sc[:, t, 0:nk], ACT.Exp, bias=stats[:, 8 + t:9 + t],
                            accum_out=stats[:, 24 + t:25 + t]))
                step(fn(stats[:, 16:16 + nt], stats[:, 16:16 + nt], ACT.Exp), flow("b_exp"))
                bank[2].read(act, "act")
                step(fn(pt0[0:min(nk, P), 0:nt * P], mp[2][0:min(nk, P), 0:nt * P], ACT.Copy), bank[2].empty["act"])
                bank[0].read(act, "act")
                if c == 0:
                    act.wait_ge(flow("a_state_stored").sem, 96 * (l + 1))
                step(fn(bh[:, :, at:at + n], mp[0][:, 0:4 * n].rearrange("p (m t) -> p m t", t=n), ACT.Copy),
                     bank[0].empty["act"])

            def gate(s):
                l, b, m = s[1:]
                i = 3 * m + b
                if i == 0:
                    act.wait_ge(flow("a_state_stored").sem, 96 * (l + 1))
                    act.wait_ge(flow("b_stored").sem, 96 * (l + 1))
                else:
                    j = i - 2
                    if j >= 0:
                        act.wait_ge(emptied["dve"].sem, tiles[("branch", l, j % 3, j // 3)][2])
                pair = product_done(s)
                step(fn(halves(gate_t[:, i % 2, :]), pair_view(pair), ACT.Tanh, scale=0.5), emptied["act"])

            def merge_split(l):
                for k in range(KD):
                    flow("merged").wait_next(act, "act")
                    xh_ready.inc(fn(xh[:, k, :], merged[:, k, :], ACT.Copy, scale=0.5))

            split_units = [s for s in units if s in split_no]
            split_high(0)
            for s in plan:
                kind = s[0]
                if s in split_no:
                    split_high(split_no[s] + 1)
                if kind == "load_x":
                    load_x()
                elif kind == "norm_pre":
                    norm_pre(*s[1:])
                elif kind == "norm_post":
                    norm_post(*s[1:])
                elif kind == "cols_c":
                    cols_c(s)
                elif kind == "cols_a":
                    cols_a(s)
                elif kind == "cols_b":
                    cols_b(s)
                elif kind == "gate":
                    gate(s)
                elif kind == "mix":
                    pair = product_done(s)
                    step(fn(halves(mixed[:, s[2], :]), pair_view(pair), ACT.Copy), emptied["act"])
                elif kind == "ffn_gate":
                    pair = product_done(s)
                    if s[2] >= 2:
                        act.wait_ge(flow("hidden").sem, KF * s[1] + s[2] - 1)
                    step(fn(halves(ffn_t[:, s[2] % 2, :]), pair_view(pair), ACT.Tanh, scale=0.5), flow("ffn_tanh"))
                elif kind == "ffn_up":
                    act.wait_ge(emptied["dve"].sem, tiles[s][2])
                    step(fn(hid_h[:, s[2], :], ffn_p[:, s[2] % 2, :], ACT.Copy), flow("hidden_high"))
                elif kind == "ffn_out":
                    if s[3] == 2:
                        pair = product_done(s)
                        step(fn(halves(ffn_y[:, s[2], :]), pair_view(pair), ACT.Copy), emptied["act"])
                elif kind == "store_y":
                    for t in range(5):
                        n, at = group(t)
                        b = bank[2 * (t % 2) + 1]
                        b.read(act, "act")
                        step(fn(y_tok[0:n, t, 512:1024], b.t[0:n, :], ACT.Copy), b.empty["act"])
                elif kind in ("branch", "c_gram"):
                    pass
                else:
                    {"c_shift_out": c_shift_out, "c_prep": c_prep, "c_invert": c_invert, "c_chain": c_chain,
                     "c_finish": c_finish, "a_rows": a_rows, "a_chunk": a_chunk, "a_finish": a_finish,
                     "b_values": b_values, "b_chunk": b_chunk, "merge_split": merge_split}[kind](*s[1:])

        @block.vector
        def _(dve):
            step = Lane(dve, chains["dve"])
            tt, stt, ts = dve.tensor_tensor, dve.scalar_tensor_tensor, dve.tensor_scalar
            MUL, ADD, SUB, MAX, MIN = ALU.mult, ALU.add, ALU.subtract, ALU.max, ALU.min

            def product_done(s):
                dve.wait_ge(products.sem, unit_no[s] + 1)
                return tiles[s][0]

            def load_x():
                dve.wait_ge(ld_const.sem, 32)
                bank[1].read(dve, "dve")
                step(dve.tensor_copy(bias_line[:], mp[1][0:8, 0:256]), bank[1].empty["dve"])
                step(dve.tensor_copy(stats[0:1, 61:62], bias_line[0:1, 0:1]), flow("bias_line"))
                for k in range(0, KD, 2):
                    bank[2].read(dve, "dve")
                    step(dve.tensor_copy(x[:, k, 0:TP], mp[2][:]), bank[2].empty["dve"])
                    step(dve.tensor_copy(stats[0:1, 61:62], stats[0:1, 61:62]), flow("x_even"))
                step(dve.memset(stats[:], 0.0))

            def norm_pre(l, w_):
                g0 = PARAM_AT["norm_mix_pre" if w_ == 0 else "norm_ffn_pre"]
                flow("rstd").wait_next(dve, "dve")
                if w_ == 0:
                    step(dve.memset(craw[:, :, 0:1], 0.0))
                if l == 0 and w_ == 0:
                    at = PARAM_AT["c_w0"]
                    step(ts(half_w0a0[:], prm[:, :, at:at + 8], 0.5, None, MUL))

                def low(k):
                    xh_ready.wait_next(dve, "dve")
                    step(tt(xl[:, k, :], squares[:, k, :], xh[:, k, :].bitcast(F32), SUB), xl_ready)

                for k in range(KD):
                    step(stt(out=squares[:, k, :], in0=x[:, k, :], scalar=prm[:, l, g0 + k:g0 + k + 1], in1=rstd[:],
                             op0=MUL, op1=MUL), xn_part)
                    if k:
                        low(k - 1)
                low(KD - 1)

            def norm_post(l, w_):
                g0 = PARAM_AT["norm_mix_post" if w_ == 1 else "norm_ffn_post"]
                src, tmp = (mixed, squares) if w_ == 1 else (ffn_y, sq2)
                flow("rstd").wait_next(dve, "dve")
                for k in range(KD):
                    step(stt(out=tmp[:, k, :], in0=src[:, k, :], scalar=prm[:, l, g0 + k:g0 + k + 1], in1=rstd[:],
                             op0=MUL, op1=MUL))
                    step(tt(x[:, k, :], x[:, k, :], tmp[:, k, :], ADD), flow("x_new"))

            def cols_c(s):
                l, j = s[1:]
                flow("c_raw").wait_next(dve, "dve")
                raw, d = craw[:, j % 2, :], c_diff[:, j % 2, :]
                step(dve.tensor_copy(view(shift_out[:], [[CT, 2]], j), view(raw, [[TS + 1, 2]], TP)),
                     flow("shift_cols") if j == CT - 1 else None)
                step(tt(d, raw[:, 0:CW], raw[:, 1:CW + 1], SUB))
                mu = PARAM_AT["c_mu"] + j
                step(stt(out=cc[:, j, :], in0=d, scalar=prm[:, l, mu:mu + 1], in1=raw[:, 1:CW + 1], op0=MUL, op1=ADD),
                     flow("c_col"))

            C1 = -0.5 * math.exp(-0.5)

            def c_prep(l, g):
                n, at, nch, L = c_group(g)
                r4 = cc[:, 0:4, at:at + n]
                k4 = cc[:, 4:8, at:at + n]
                v4 = cc[:, 8:12, at:at + n]
                f4 = lambda t: t[:, 0:4 * n]
                step(tt(gv(kk, n), k4, view(prm[:, l, PARAM_AT["c_k_k"]:], [[1, 4], [0, n]]), MUL),
                     flow("c_kk_raw"))
                flow("c_sig_raw").wait_next(dve, "dve")
                step(ts(sig_g[:, 0:n], sig_g[:, 0:n], 0.5, 0.5, MUL, ADD), flow("c_gate_in"))
                bank[0].wait_emptied(dve, ("c_lw", l, g))
                step(ts(f4(decay_log), f4(decay_log), C1, C1, MUL, ADD))
                mask = C("scan64") if L == 64 else C("scan32")
                step(dve.tensor_tensor_scan(f4(cum), mask[:, 0:4 * n], f4(decay_log), 0.0, MUL, ADD))
                step(tt(f4(decay_log), f4(cum), f4(decay_log), SUB), flow("c_cum"))
                bank[1].wait_emptied(dve, ("c_la", l, g))
                step(ts(f4(in_rate), f4(in_rate), 0.5, 0.5, MUL, ADD))
                bank[2].read(dve, "dve")
                step(ts(f4(kprime), mp[2][:, 0:4 * n], 1e-24, None, MAX), bank[2].empty["dve"])
                step(dve.tensor_copy(stats[0:1, 61:62], stats[0:1, 61:62]), flow("c_ss"))
                flow("c_rn").wait_next(dve, "dve")
                step(tt(f4(kk), f4(kk), f4(kprime), MUL))
                step(stt(out=gv(kprime, n), in0=gv(in_rate, n), scalar=-1.0, in1=view(prm[:, l, PARAM_AT["c_k_a"]:], [[1, 4], [0, n]]),
                         op0=ADD, op1=MUL))
                step(stt(out=gv(kprime, n), in0=gv(kprime, n), scalar=1.0, in1=k4, op0=ADD, op1=MUL))
                step(tt(f4(in_rate), f4(kk), f4(in_rate), MUL))
                step(tt(gv(scratch, n), r4, view(prm[:, l, PARAM_AT["c_r_k"]:], [[1, 4], [0, n]]), MUL))
                step(tt(f4(scratch), f4(scratch), f4(kprime), MUL), flow("c_rk"))
                flow("c_exps").wait_next(dve, "dve")
                en = rhs_z[:, :, :].rearrange("p a b -> p (a b)")[:, 0:4 * n]
                step(tt(kap_r[:, :, 0, 0:n], gv(kk, n), gv(decay_log, n), MUL))
                step(tt(kap_r[:, :, 1, 0:n], r4, gv(cum, n), MUL))
                step(tt(f4(in_rate), f4(in_rate), en, MUL))
                step(tt(f4(kprime), f4(kprime), en, MUL), flow("c_scaled"))
                bank[3].read(dve, "dve")
                step(tt(v4, gv(mp[3], n), v4, MUL), bank[3].empty["dve"])

            def level_mask(k, n, L):
                return view(C("levels")[0:n], [[0, 8], [1, L]], 64 * k)

            def c_gram(l, g):
                n, at, nch, L = c_group(g)
                masks = view(C("lt_le")[0:n], [[0, 4], [64, 2], [1, L]])

                def masked(b, dst, h0):
                    bank[b].read(dve, "dve")
                    step(tt(dst[0:n, h0:h0 + 4, :, 0:L], mp[b][0:n, 0:8 * L].rearrange("p (h u t) -> p h u t", u=2, t=L),
                            masks, MUL), bank[b].empty["dve"])

                masked(0, a_rb, 0)
                masked(3, a_rb, 4)
                bank[1].read(dve, "dve")
                at_ = a_rb[0:n, :, 0, 0:L]
                i_, it_ = inv[0:n, :, 0:L], invT[0:n, :, 0:L]
                eye = view(C("eye64")[0:n], [[0, 8], [1, L]])
                step(tt(i_, mp[1][0:n, 0:8 * L].rearrange("p (h t) -> p h t", t=L),
                        view(C("level0_neg")[0:n], [[0, 8], [1, L]]), MUL), bank[1].empty["dve"])
                step(tt(i_, i_, eye, ADD))
                step(tt(it_, at_, level_mask(0, n, L), MUL))
                step(tt(it_, eye, it_, SUB))
                step(tt(a_lev[0:n, :, 0:L], at_, level_mask(1, n, L), MUL), flow("c_level"))
                masked(2, b_rk, 0)
                masked(0, b_rk, 4)

            def c_invert(l, g):
                n, at, nch, L = c_group(g)
                levels = 6 if L == 64 else 5
                i_, it_ = inv[0:n, :, 0:L], invT[0:n, :, 0:L]
                for k in range(1, levels):
                    for b, t in ((3, i_), (2, it_)):
                        if b == 3 and k == levels - 1:
                            continue
                        bank[b].read(dve, "dve")
                        step(tt(t, t, mp[b][0:n, 0:8 * L].rearrange("p (h t) -> p h t", t=L), SUB), bank[b].empty["dve"])
                    if k < levels - 1:
                        step(tt(a_lev[0:n, :, 0:L], a_rb[0:n, :, 0, 0:L], level_mask(k + 1, n, L), MUL), flow("c_level"))

            def c_chain(l, g):
                n, at, nch, L = c_group(g)
                if g == 0:
                    step(dve.memset(state[:, 0], 0.0), flow("c_state"))
                if g == 4:
                    bank[0].read(dve, "dve")
                    step(dve.tensor_copy(state[:, 0], mp[0][:, 0:256].rearrange("p (f i) -> p f i", i=64)), bank[0].empty["dve"])
                    step(dve.tensor_copy(stats[0:1, 61:62], stats[0:1, 61:62]), flow("c_state"))
                for c in range(nch):
                    r = slice(64 * c, 64 * c + L)
                    cur = (2 * g + c) % 2
                    bank[0].read(dve, "dve")
                    step(dve.tensor_copy(rhs_z[r], mp[0][r, :].rearrange("p (h i) -> p h i", i=64)), bank[0].empty["dve"])
                    bank[1].read(dve, "dve")
                    step(ts(neg_z[r], mp[1][r, :].rearrange("p (h i) -> p h i", i=64), -1.0, None, MUL), bank[1].empty["dve"])
                    bank[2].read(dve, "dve")
                    nxt = state[:, 1 - cur]
                    step(tt(nxt, state[:, cur], mp[2][:, 0:256].rearrange("p (f i) -> p f i", i=64), ADD), bank[2].empty["dve"])
                    step(tt(nxt, nxt, view(cum[:], [[n, 4], [0, 64]], c * L + L - 1), MUL), flow("c_state"))

            def c_finish(l, g):
                n, at, nch, L = c_group(g)
                f4 = lambda t: t[:, 0:4 * n]
                y4, v4 = cc[:, 0:4, at:at + n], cc[:, 8:12, at:at + n]
                par = lambda name: view(prm[:, l, PARAM_AT[name]:], [[1, 4], [0, n]])
                bank[0].read(dve, "dve")
                step(stt(out=gv(kk, n), in0=gv(mp[0], n), scalar=-1.0 / 64, in1=y4, op0=MUL, op1=ADD), bank[0].empty["dve"])
                step(dve.tensor_copy(stats[0:1, 61:62], stats[0:1, 61:62]), flow("c_dev"))
                flow("c_gn_r").wait_next(dve, "dve")
                step(tt(f4(kk), f4(kk), f4(kprime), MUL))
                step(tt(gv(kk, n), gv(kk, n), par("c_gn_g"), MUL))
                step(tt(gv(kk, n), gv(kk, n), par("c_gn_b"), ADD))
                step(tt(gv(kk, n), gv(kk, n), v4, ADD))
                step(tt(y4, gv(kk, n), gv(cum, n), MUL), flow("c_h"))

            def a_rows(l):
                dve.wait_ge(emptied["act"].sem, tiles[("cols_a", l, 16)][2])
                q = slice(0, 4)
                step(dve.tensor_copy(r_lf[q, :], r_nm[32:36, :]))
                step(stt(out=r_g[q, :], in0=r_lf[q, :], scalar=-1.0, in1=r_lf[q, :], op0=MUL, op1=MIN))
                step(ts(r_in[q, :], r_lf[q, :], 0.0, None, MIN), flow("a_abs"))
                flow("a_ln").wait_next(dve, "dve")
                step(tt(r_lf[q, :], r_in[q, :], r_wk[q, :], SUB))
                step(dve.tensor_tensor_scan(r_f[q, :], C("scan_rows")[q], r_lf[q, :], 0.0, MUL, ADD))
                step(dve.tensor_tensor_scan(r_m[q, 0:TP], r_lf[q, 0:TP], r_li[q, 0:TP], 0.0, ADD, MAX))
                step(dve.tensor_tensor_scan(r_m[q, TP:T], r_lf[q, TP:T], r_li[q, TP:T], m_init[q, :], ADD, MAX))
                step(tt(r_g[q, :], r_f[q, :], r_m[q, :], SUB))
                step(tt(r_li[q, :], r_li[q, :], r_f[q, :], SUB))
                step(dve.memset(m_prev[:], 0.0))
                step(dve.tensor_copy(m_prev[q, 1:4], view(r_m[q, :], [[P, 3]], P - 1)))
                step(dve.tensor_copy(m_prev[q, 4:5], m_init[q, :]))
                step(dve.tensor_copy(g_last[q, 0:4], view(r_g[q, :], [[P, 4]], P - 1)))
                step(dve.tensor_copy(g_last[q, 4:5], r_g[q, T - 1:T]))
                for dst, src, edge in ((r_in, r_g, m_prev), (r_wk, r_li, g_last)):
                    step(tt(dst[q, 0:TP].rearrange("p (c t) -> p c t", t=P), src[q, 0:TP].rearrange("p (c t) -> p c t", t=P),
                            view(edge[q, :], [[1, 4], [0, P]]), ADD))
                    step(tt(dst[q, TP:T], src[q, TP:T], view(edge[q, :], [[0, TS]], 4), ADD))
                step(dve.memset(cn[:], 0.0))
                step(dve.memset(vo[:, :, P:256], 1.0), flow("a_exp_in"))

            def a_chunk(l, g):
                n, at = group(g)
                if g == 4:
                    dve.wait_ge(flow("a_state_in").sem, 32 * (l + 1))
                    step(dve.tensor_copy(cn[:, :, P:256], view(ncol[:], [[1, 4], [0, P]])), flow("a_n_spread"))
                flow("a_cols_t").wait_next(dve, "dve")
                bank[0].read(dve, "dve")
                for h in range(4):
                    step(stt(out=dexp[0:n, h * n:(h + 1) * n], in0=mp[0][0:n, h * n:(h + 1) * n], scalar=a_cols_t[0:n, h:h + 1],
                             in1=C("future_neg")[0:n, 0:n], op0=ADD, op1=ADD), bank[0].empty["dve"] if h == 3 else None)
                bank[1].read(dve, "dve")
                step(tt(gv(qt, n), acols[:, 0:4, at:at + n], gv(mp[1], n), MUL))
                step(dve.tensor_copy(a_dec[:], view(mp[1][:], [[n, 4]], n - 1)), bank[1].empty["dve"])
                flow("a_dexp").wait_next(dve, "dve")
                bank[3].read(dve, "dve")
                step(stt(out=wts[0:n, 0:4 * n], in0=mp[3][0:n, 0:4 * n], scalar=P ** -0.5, in1=dexp[0:n, 0:4 * n],
                         op0=MUL, op1=MUL), bank[3].empty["dve"])
                bank[3].wait_emptied(dve, ("a_den", l, g))
                bank[0].read(dve, "dve")
                step(tt(a_den[:, :, at:at + n], a_den[:, :, at:at + n], gv(mp[0], n), MAX), bank[0].empty["dve"])
                for b in range(2):
                    bank[1 + b].read(dve, "dve")
                    for i in range(2):
                        h = 2 * b + i
                        step(stt(out=cn[:, h, :], in0=cn[:, h, :], scalar=a_dec[:, h:h + 1],
                                 in1=mp[1 + b][:, i * 256:(i + 1) * 256], op0=MUL, op1=ADD),
                             bank[1 + b].empty["dve"] if i else None)

            def a_finish(l):
                step(ts(a_den[:], a_den[:], 4e12, None, MIN), flow("a_den_ok"))
                flow("a_den_sq").wait_next(dve, "dve")
                for h in range(4):
                    for b in range(2):
                        bk = 2 * (h % 2) + b
                        bank[bk].read(dve, "dve")
                        cols_ = a_den[:, h, b * HALF:(b + 1) * HALF]
                        step(stt(out=cols_, in0=cols_, scalar=P * NORM_EPS, in1=mp[bk][:, 0:HALF], op0=MUL, op1=ADD),
                             bank[bk].empty["dve"])
                flow("a_o_tanh").wait_next(dve, "dve")
                g0 = PARAM_AT["a_norm"]
                for h in range(4):
                    flow("a_r").wait_next(dve, "dve")
                    step(tt(acols[:, h, :], acols[:, h, :], a_den[:, h, :], MUL))
                    step(stt(out=acols[:, h, :], in0=acols[:, 12 + h, :], scalar=1.0, in1=acols[:, h, :], op0=ADD, op1=MUL))
                    step(ts(acols[:, h, :], acols[:, h, :], prm[:, l, g0 + h:g0 + h + 1], 0.5, MUL, MUL),
                         flow("a_h") if h == 3 else None)

            def b_values(l):
                bank[1].read(dve, "dve")
                step(dve.tensor_copy(vb[:, 0:3, :], mp[1][:, 0:3 * P].rearrange("p (j d) -> p j d", d=P)))
                step(dve.tensor_copy(vb[0:64, 3, :], mp[1][0:64, 3 * P:4 * P]), bank[1].empty["dve"])
                bank[3].read(dve, "dve")
                step(dve.tensor_copy(ks[:, 0:P], mp[3][:, 0:P]), bank[3].empty["dve"])
                step(dve.tensor_copy(ks[:, P:KEYS_S], bkv[:, 0, TP:T]), flow("b_values"))

            def b_chunk(l, c):
                sample = c == 8
                nt = 2 if sample else 4
                nk = KEYS_S if sample else CHUNK * min(3, c + 1)
                if l == 0 and c == 0:
                    dve.wait_ge(bias_in.sem, 16 * 16)
                per = nt // 2
                for v in range(2):
                    bank[v].read(dve, "dve")
                    bias = bias_s[:, v:v + 1, :] if sample else bias_p[:, 2 * v:2 * v + 2, KEYS - nk:KEYS]
                    step(stt(out=sc[:, per * v:per * v + per, 0:nk], in0=mp[v][:, 0:per * nk].rearrange("p (i k) -> p i k", k=nk),
                             scalar=B_HD ** -0.5, in1=bias, op0=MUL, op1=ADD), bank[v].empty["dve"])
                s0 = 4 if sample else 0
                step(dve.tensor_reduce(stats[:, 0:nt], sc[:, 0:nt, 0:nk], AX.X, MAX))
                step(tt(stats[:, 0:nt], stats[:, 0:nt], sinks[:, s0:s0 + nt], MAX))
                step(tt(stats[:, 16:16 + nt], sinks[:, s0:s0 + nt], stats[:, 0:nt], SUB))
                step(ts(stats[:, 8:8 + nt], stats[:, 0:nt], -1.0, None, MUL), flow("b_max"))
                flow("b_exp").wait_next(dve, "dve")
                step(tt(stats[:, 32:32 + nt], stats[:, 24:24 + nt], stats[:, 16:16 + nt], ADD))
                step(dve.reciprocal(stats[:, 40:40 + nt], stats[:, 32:32 + nt]))
                step(tt(sc[:, 0:nt, 0:nk], sc[:, 0:nt, 0:nk], view(stats[:], [[1, nt], [0, nk]], 40), MUL), flow("b_probs"))
                if nk > P:
                    bank[3].read(dve, "dve")
                    step(dve.tensor_copy(pt1[0:nk - P, 0:nt * P], mp[3][0:nk - P, 0:nt * P]), bank[3].empty["dve"])

            def branch(s):
                l, b, m = s[1:]
                i = 3 * m + b
                if i == 0:
                    dve.wait_ge(flow("a_state_stored").sem, 96 * (l + 1))
                pair = product_done(s)
                dve.wait_ge(emptied["act"].sem, tiles[("gate", l, b, m)][2])
                dst = merged[:, m, :] if b == 0 else prod[:, i % 2, :]
                step(stt(out=halves(dst), in0=halves(gate_t[:, i % 2, :]), scalar=1.0, in1=pair_view(pair), op0=ADD, op1=MUL),
                     emptied["dve"])
                if b:
                    step(tt(merged[:, m, :], merged[:, m, :], dst, ADD), flow("merged") if b == 2 else None)

            def hidden_low(j):
                flow("hidden_high").wait_next(dve, "dve")
                step(tt(hid_l[:, j, :], ffn_p[:, j % 2, :], hid_h[:, j, :].bitcast(F32), SUB), flow("hidden"))

            for s in plan:
                kind = s[0]
                if kind == "load_x":
                    load_x()
                elif kind == "norm_pre":
                    norm_pre(*s[1:])
                elif kind == "norm_post":
                    norm_post(*s[1:])
                elif kind == "cols_c":
                    cols_c(s)
                elif kind == "branch":
                    branch(s)
                elif kind == "merge_split":
                    for k in range(KD):
                        xh_ready.wait_next(dve, "dve")
                        step(stt(out=xl[:, k, :], in0=merged[:, k, :], scalar=0.5, in1=xh[:, k, :].bitcast(F32),
                                 op0=MUL, op1=SUB), xl_ready)
                elif kind == "ffn_gate":
                    j = s[2]
                    pair = tiles[s][0]
                    flow("ffn_tanh").wait_next(dve, "dve")
                    step(stt(out=halves(ffn_p[:, j % 2, :]), in0=halves(ffn_t[:, j % 2, :]), scalar=1.0, in1=pair_view(pair),
                             op0=ADD, op1=MUL), emptied["dve"])
                    if j:
                        hidden_low(j - 1)
                elif kind == "ffn_up":
                    j = s[2]
                    pair = product_done(s)
                    step(stt(out=halves(ffn_p[:, j % 2, :]), in0=halves(ffn_p[:, j % 2, :]), scalar=0.5, in1=pair_view(pair),
                             op0=MUL, op1=MUL), emptied["dve"])
                    if j == KF - 1:
                        hidden_low(j)
                elif kind == "store_y":
                    for t in range(5):
                        n, at = group(t)
                        b = bank[2 * (t % 2)]
                        b.read(dve, "dve")
                        step(dve.tensor_copy(y_tok[0:n, t, 0:512], b.t[0:n, :]), b.empty["dve"])
                elif kind in ("cols_a", "cols_b", "gate", "mix", "ffn_out", "c_shift_out"):
                    pass
                else:
                    {"c_prep": c_prep, "c_gram": c_gram, "c_invert": c_invert, "c_chain": c_chain, "c_finish": c_finish,
                     "a_rows": a_rows, "a_chunk": a_chunk, "a_finish": a_finish, "b_values": b_values,
                     "b_chunk": b_chunk}[kind](*s[1:])

        @block.sync
        def _(sp):
            with nc.allow_non_contiguous_dma(reason="small vectors"):
                def put(c, dst, src):
                    c.inc(sp.dma_start(dst, src), 16)

                put(ld_const, cst[:], consts_dram)
                put(ld_const, table[:], a["rel_bias"])
                for l in range(DEPTH):
                    for name, rows in PARAM_ROWS:
                        src = a[name][l] if name != "state_rwkv_shift" else a[name][l, 0, 0]
                        at = PARAM_AT[name]
                        put(ld_prm, prm_rows[at:at + rows, l, :], src.rearrange("(r c) -> r c", c=P))
                for t in range(4):
                    put(ld_x, x_tok[:, t, :], a["x_prompt"][0, t * P:(t + 1) * P, :])
                put(ld_x, x_tok[0:TS, 4, :], a["x_sample"][0])
                flow("bias_line").wait_next(sp, "sp")
                put(bias_out, bias_dram.rearrange("h (q n) -> h q n", n=256), view(bias_line[:], [[0, 64], [1, 256]]))
                bias_out.wait_next(sp, "sp", 16)
                h0 = bias_dram
                for hh in range(2):
                    for t in range(4):
                        head = 4 * (t // 2) + 2 * (t % 2) + hh
                        src = bass.AP(tensor=h0.tensor, offset=h0.offset + head * 64 * 256 + 63, ap=[[255, 64], [1, KEYS]])
                        put(bias_in, bias_p[64 * hh:64 * hh + 64, t, :], src)
                for kv in range(2):
                    for m in range(4):
                        src = bass.AP(tensor=h0.tensor, offset=h0.offset + (4 * kv + m) * 64 * 256 + 63,
                                      ap=[[255, TS], [1, KEYS_S]])
                        put(bias_in, bias_s[TS * m:TS * m + TS, kv, :], src)

                def free_raw(u):
                    s = units[u]
                    if s in split_no:
                        sp.wait_ge(low_ready.sem, split_no[s] + 1)
                    else:
                        sp.wait_ge(products.sem, unit_no[s] + 1)

                def load_unit(s):
                    u = unit_no[s]
                    if u >= NRAW:
                        free_raw(u - NRAW)
                    for (ps, ks_, ms), src in unit_parts(s):
                        put(landed[u % NRAW], wraw[ps, u % NRAW, ks_, ms], src)

                for s in units[0:NRAW - 1]:
                    load_unit(s)

                def vec(ap):
                    return ap.rearrange("(n u) -> n u", u=1)

                for s in plan:
                    kind, l = s[0], s[1] if len(s) > 1 else 0
                    if kind in GEMMS and unit_no[s] + NRAW - 1 < len(units):
                        load_unit(units[unit_no[s] + NRAW - 1])
                    if kind == "norm_pre" and s[2] == 0:
                        if l > 0:
                            sp.wait_ge(products.sem, unit_no[("mix", l - 1, 0)] + 1)
                        put(ld_layer, lora[0:64, 0:512], a["c_w_w2"][l])
                        put(ld_layer, lora[64:128, 0:512], a["c_w_a2"][l])
                        put(ld_layer, lora[:, 512:1024], a["c_w_g2"][l])
                        sk = a["b_sinks"][l]
                        for hh in range(2):
                            src = bass.AP(tensor=sk.tensor, offset=sk.offset + hh, ap=[[0, 64], [2, 4]])
                            put(ld_layer, sinks[64 * hh:64 * hh + 64, 0:4], src)
                        for m in range(4):
                            src = bass.AP(tensor=sk.tensor, offset=sk.offset + m, ap=[[0, TS], [4, 2]])
                            put(ld_layer, sinks[TS * m:TS * m + TS, 4:6], src)
                        gb = vec(a["a_gate_bias"][l])
                        put(ld_layer, gate_bias[0:4, :], gb[0:4])
                        put(ld_layer, gate_bias[32:36, :], gb[4:8])
                        put(ld_layer, m_init[0:4, :], vec(a["state_mlstm_m"][l, 0]))
                        put(flow("c_state_in"), s_nat[:], a["state_rwkv_s"][l, 0].rearrange("(p q) i j -> (q i) p j", q=2))
                    if kind == "c_shift_out":
                        flow("shift_rows").wait_next(sp, "sp")
                        for i, name in enumerate(("p_rwkv_shift", "s_rwkv_shift")):
                            put(flow("shift_stored"), o[name][l, 0, 0].rearrange("(r c) -> r c", c=P),
                                shift_rows[CT * i:CT * i + CT, :])
                    if kind == "c_finish" and s[2] >= 3:
                        bank[3].wait_emptied(sp, ("c_state", l, s[2]))
                        put(flow("c_state_stored"),
                            o["p_rwkv_s" if s[2] == 3 else "s_rwkv_s"][l, 0].rearrange("(p q) i j -> (q i) p j", q=2), s_out[:])
                    if kind == "a_chunk" and s[2] in (3, 4):
                        pre = "p" if s[2] == 3 else "s"
                        bank[2].wait_emptied(sp, ("a_state", l, s[2]))
                        done = flow("a_state_stored")
                        put(done, o[f"{pre}_mlstm_c"][l, 0].rearrange("h k v -> k h v"), cn[:, :, 0:P])
                        put(done, o[f"{pre}_mlstm_n"][l, 0].rearrange("h k -> k h"), cn[:, :, P])
                        put(done, vec(o[f"{pre}_mlstm_m"][l, 0]), r_m[0:4, TP - 1:TP] if s[2] == 3 else r_m[0:4, T - 1:T])
                        if s[2] == 3:
                            sp.wait_ge(done.sem, done.value)
                            put(flow("a_state_in"), cn[:, :, 0:P], a["state_mlstm_c"][l, 0].rearrange("h k v -> k h v"))
                            put(flow("a_state_in"), ncol[:], a["state_mlstm_n"][l, 0].rearrange("h k -> k h"))
                    if kind == "a_finish":
                        flow("a_h").wait_next(sp, "sp")
                        put(flow("b_cache_in"), kcache[:], a["cache_swa_k"][l, 0].rearrange("t v d -> t (v d)"))
                        put(flow("b_cache_in"), vcache[:], a["cache_swa_v"][l, 0].rearrange("t v d -> t (v d)"))
                    if kind == "b_values":
                        bank[2].wait_emptied(sp, ("b_values", l))
                        pk, pv, sk_, sv = (o[n][l, 0].rearrange("t v d -> t (v d)") for n in
                                           ("p_swa_k", "p_swa_v", "s_swa_k", "s_swa_v"))
                        done = flow("b_stored")
                        put(done, pk, kout[:, 0, :])
                        put(done, pv, va[:, 3, :])
                        sp.wait_ge(flow("b_cache_in").sem, 32 * (l + 1))
                        put(done, sk_[0:WINDOW - TS], kcache[TS:P, :])
                        put(done, sv[0:WINDOW - TS], vcache[TS:P, :])
                        put(done, sk_[WINDOW - TS:], kout[0:TS, 1, :])
                        put(done, sv[WINDOW - TS:], va[0:TS, 4, :])
                for t in range(5):
                    bank[2 * (t % 2)].wait_emptied(sp, ("y", t, 0))
                    bank[2 * (t % 2) + 1].wait_emptied(sp, ("y", t, 1))
                    if t < 4:
                        put(stored, o["y_prompt"][0, t * P:(t + 1) * P, :], y_tok[:, t, :])
                    else:
                        put(stored, o["y_sample"][0], y_tok[0:TS, 4, :])
                for c in (stored, flow("shift_stored"), flow("c_state_stored"), flow("a_state_stored"), flow("b_stored")):
                    sp.wait_ge(c.sem, c.value)

        @block.gpsimd
        def _(pool):
            for s in units:
                if s not in split_no:
                    continue
                n = split_no[s]
                slot = unit_no[s] % NRAW
                nk = nk_of(s)
                pool.wait_ge(high_ready.sem, n + 1)
                low_ready.inc(pool.tensor_tensor(wl[:, n % NSPLIT, 0:nk], wraw[:, slot, 0:nk],
                                                 wh[:, n % NSPLIT, 0:nk].bitcast(F32), ALU.subtract))


_INS = ['x_prompt', 'x_sample', 'cache_swa_k', 'cache_swa_v', 'state_mlstm_c', 'state_mlstm_n', 'state_mlstm_m',
        'state_rwkv_s', 'state_rwkv_shift', 'w_in', 'norm_mix_pre', 'norm_mix_post', 'norm_ffn_pre', 'norm_ffn_post',
        'a_gate_bias', 'a_norm', 'rel_bias', 'b_sinks', 'c_mu', 'c_w0', 'c_w_w2', 'c_a0', 'c_w_a2', 'c_w_g2', 'c_k_k',
        'c_k_a', 'c_r_k', 'c_gn_g', 'c_gn_b', 'w_branch_a', 'w_branch_b', 'w_branch_c', 'w_out', 'w_ffn_in', 'w_ffn_out']
_STATES = [("swa_k", (DEPTH, 1, WINDOW, 2, 64)), ("swa_v", (DEPTH, 1, WINDOW, 2, 64)), ("mlstm_c", (DEPTH, 1, 4, P, P)),
           ("mlstm_n", (DEPTH, 1, 4, P)), ("mlstm_m", (DEPTH, 1, 4)), ("rwkv_s", (DEPTH, 1, 8, 64, 64)),
           ("rwkv_shift", (DEPTH, 1, 1, C_COLS))]
_OUTS = ([("y_prompt", (1, TP, D)), ("y_sample", (1, TS, D))] + [("p_" + n, s) for n, s in _STATES]
         + [("s_" + n, s) for n, s in _STATES])


def kernel(**inputs):
    import concourse.bacc as _bacc
    from concourse.bass_utils import run_bass_kernel_spmd as _run

    nc = _bacc.Bacc("TRN2", target_bir_lowering=False, num_devices=1)
    arrays, a, o = {}, {}, {}
    for name in _INS:
        v = np.ascontiguousarray(inputs[name])
        arrays[f"in_{name}"] = v
        a[name] = nc.dram_tensor(f"in_{name}", v.shape, mybir.dt.from_np(v.dtype), kind="ExternalInput").ap()
    for name, shape in _OUTS:
        o[name] = nc.dram_tensor(f"out_{name}", shape, mybir.dt.float32, kind="ExternalOutput").ap()
    build(nc, a, o)
    r = _run(nc, [arrays], core_ids=[0])
    return tuple(r.results[0][f"out_{name}"] for name, _ in _OUTS)
```

```python
import math
from contextlib import ExitStack

import numpy as np

import concourse.bass as bass
from concourse import mybir

P = 128
D = 1024
TP, TS = 512, 32
T = TP + TS
DEPTH = 2
KD = D // P
A_H, A_W = 4, 512
A_COLS = 4 * A_W + 2 * A_H
B_W, B_HD = 512, 64
B_COLS = 768
C_W, C_H = 512, 8
C_COLS = 1792
CT = C_COLS // P
OFF_B = A_COLS
OFF_C = A_COLS + B_COLS
OFF_G = OFF_C + C_COLS
D_FF = 2816
KF = D_FF // P
WINDOW = 128
CHUNK = 64
NORM_EPS, GN_EPS = 1e-6, 64e-5
HALF = T // 2
SPLIT_C = 256
CW = TP + 1 + TS
KEYS = WINDOW + CHUNK
KEYS_S = WINDOW + TS
NRAW, NSPLIT = 3, 2
GROUPS = 5
PARAM_ROWS = [("norm_mix_pre", KD), ("norm_mix_post", KD), ("norm_ffn_pre", KD), ("norm_ffn_post", KD),
              ("c_mu", CT), ("state_rwkv_shift", CT), ("a_norm", 4), ("c_w0", 4), ("c_a0", 4), ("c_k_k", 4),
              ("c_k_a", 4), ("c_r_k", 4), ("c_gn_g", 4), ("c_gn_b", 4)]
PARAM_AT, _n = {}, 0
for _name, _rows in PARAM_ROWS:
    PARAM_AT[_name] = _n
    _n += _rows
NPARAM = _n


def group(g):
    return (P, P * g) if g < 4 else (TS, TP)


def shape_constants():
    c = {}
    c["ident"] = np.eye(P)
    c["ones"] = np.ones((P, P))
    c["headones"] = np.kron(np.eye(2), np.ones((64, 64)))
    s = np.arange(64)[:, None]
    t = np.arange(64)[None, :]
    both = lambda m: np.tile(m.astype(np.float64), (2, 1))
    c["lt_le"] = np.concatenate([both(s < t), both(s <= t)], axis=1)
    level = []
    for b in (1, 2, 4, 8, 16, 32):
        same = (s // (2 * b)) == (t // (2 * b))
        level.append(both(same & (s % (2 * b) >= b) & (t % (2 * b) < b)))
    c["levels"] = np.concatenate(level, axis=1)
    c["level0_up"] = both((s // 2 == t // 2) & (s % 2 == 0) & (t % 2 == 1))
    c["level0_neg"] = -both((s // 2 == t // 2) & (s % 2 == 1) & (t % 2 == 0))
    c["eye64"] = both(s == t)
    a = np.arange(P)
    c["future_neg"] = np.where(a[:, None] > a[None, :], -1e30, 0.0)
    m = np.ones((P, 512))
    m[:, ::64] = 0
    c["scan64"] = m
    m = np.ones((P, 128))
    m[:, ::32] = 0
    c["scan32"] = m
    sel = np.zeros((P, 4 * P))
    for h in range(4):
        sel[h, h * P:(h + 1) * P] = 1
    c["sel"] = sel
    m = np.ones((P, T))
    m[:, 0:TP:P] = 0
    m[:, TP] = 0
    c["scan_rows"] = m
    rel = np.arange(256) - 63 - WINDOW
    half, exact = 16, 8
    n = np.abs(rel)
    far = exact + (np.log(np.maximum(n, 1).astype(np.float32) / np.float32(exact)) / math.log(256 / exact)
                   * (half - exact)).astype(np.int32)
    bucket = np.where(rel > 0, half, 0) + np.where(n < exact, n, np.minimum(far, half - 1))
    hot = np.zeros((P, 256))
    hot[np.clip(bucket, 0, 31), np.arange(256)] = 1
    c["bucket_hot"] = hot
    v = np.zeros((P, 8))
    v[:, 0] = NORM_EPS
    v[:, 1] = GN_EPS
    v[:, 2] = 10 * math.log(2)
    v[:, 3] = 1.0
    c["scalars"] = v
    at, cols, parts = {}, 0, []
    for k, x in c.items():
        at[k] = (cols, x.shape[1])
        cols += x.shape[1]
        parts.append(x)
    return at, np.concatenate(parts, axis=1).astype(np.float32)


class Count:

    def __init__(self, sem):
        self.sem, self.value, self.seen = sem, 0, {}

    def inc(self, ins, n=1):
        ins.then_inc(self.sem, n)
        self.value += n

    def wait_next(self, eng, who, n=1):
        self.seen[who] = self.seen.get(who, 0) + n
        eng.wait_ge(self.sem, self.seen[who])


class Lane:

    def __init__(self, eng, chain):
        self.eng, self.chain = eng, chain

    def __call__(self, ins, count=None):
        c = count or self.chain
        c.inc(ins)
        self.eng.wait_ge(c.sem, c.value)


class Bank:

    def __init__(self, name, tensor, sem):
        self.t = tensor
        self.full = {r: Count(sem(f"{name}_full_for_{r}")) for r in ("act", "dve")}
        self.empty = {r: Count(sem(f"{name}_emptied_by_{r}")) for r in ("act", "dve")}
        self.last = None
        self.marks = {}

    def claim(self, pe):
        if self.last:
            pe.wait_ge(self.empty[self.last].sem, self.full[self.last].value)

    def filled(self, ins, reader, mark=None):
        self.full[reader].inc(ins)
        self.last = reader
        self.marks[mark] = (self.empty[reader].sem, self.full[reader].value)

    def read(self, eng, reader):
        self.full[reader].wait_next(eng, reader)

    def wait_emptied(self, eng, mark):
        eng.wait_ge(*self.marks[mark])


def weave(items, fillers):
    out, used = [], 0
    for i, item in enumerate(items):
        out.append(item)
        upto = (i + 1) * len(fillers) // len(items)
        out += fillers[used:upto]
        used = upto
    return out


def gate_order():
    return [(b, m) for m in range(KD) for b in range(2)] + [(2, m) for m in range(KD)]


GATES = gate_order()


def make_plan():
    plan = [("load_x",)]
    for l in range(DEPTH):
        plan += [("norm_pre", l, 0)]
        plan += [("cols_a", l, j) for j in (0, 1, 2, 16)] + [("a_rows", l), ("cols_a", l, 3), ("cols_a", l, 4)]
        plan += [("a_rows_exp", l)] + [("cols_a", l, j) for j in range(5, 16)]
        plan += [("cols_b", l, j) for j in range(6)]
        ab = []
        for g in range(GROUPS):
            ab += [("a_chunk", l, g), ("a_chunk_out", l, g)]
        ab += [("a_finish", l), ("b_values", l)] + [("b_chunk", l, c) for c in range(9)]
        plan += weave(ab, [("cols_c", l, j) for j in range(CT)])
        plan += [("c_shift_out", l)]
        c = []
        for g in range(GROUPS):
            c += [("c_prep", l, g), ("c_gram", l, g)]
            c += [("c_level", l, g, k) for k in range(1, 6 if g < 4 else 5)]
            c += [("c_chain", l, g, k) for k in range(2 if g < 4 else 1)]
            c += [("c_finish", l, g)]
        products = []
        for b, m in GATES[:2 * KD]:
            products += [("gate", l, b, m), ("branch", l, b, m)]
        plan += weave(c, products)
        for b, m in GATES[2 * KD:]:
            plan += [("gate", l, b, m), ("branch", l, b, m)]
        plan += [("merge_split", l)]
        plan += [("mix", l, m) for m in range(KD)]
        plan += [("norm_post", l, 1)]
        plan += [("norm_pre", l, 2)]
        for j in range(KF):
            plan += [("ffn_gate", l, j), ("ffn_up", l, j)]
        plan += [("ffn_out", l, m, q) for m in range(KD) for q in range(3)]
        plan += [("norm_post", l, 3)]
    plan += [("store_y",)]
    return plan


GEMMS = {"cols_c": "act", "cols_a": "act", "cols_b": "act", "gate": "act", "branch": "dve", "mix": "act",
         "ffn_gate": "dve", "ffn_up": "dve", "ffn_out": "act"}
UNSPLIT = {"branch"}


def view(ap, free, start=0):
    return bass.AP(tensor=ap.tensor, offset=ap.offset + start, ap=[list(ap.ap[0])] + [list(x) for x in free])


def build(nc, a, o):
    F32, F32R = mybir.dt.float32, mybir.dt.float32r
    ALU, ACT, AX = mybir.AluOpType, mybir.ActivationFunctionType, mybir.AxisListType
    plan = make_plan()
    const_at, const_np = shape_constants()
    NCONST = const_np.shape[1]
    consts_dram = nc.inline_tensor(const_np, name="shape_constants").ap()
    bias_dram = nc.dram_tensor("bias_skewed", (8, 64 * 256), F32, kind="Internal").ap()

    x_dram = nc.dram_tensor("x_kept", (P, KD * T), F32, kind="Internal").ap()

    base = [(nc.sbuf_base + 63) // 64 * 64]
    limit = nc.sbuf_usable_end

    def region(nbytes):
        at = base[0]
        base[0] += (nbytes + 63) // 64 * 64
        assert base[0] <= limit, (base[0], limit)
        return at

    def place(name, shape, at, dt=F32):
        n = 4 * int(np.prod(shape[1:]))
        assert at + n <= limit, (name, at + n, limit)
        return nc.alloc_sbuf_tensor_at(name, shape, dt, offset=at)

    def fixed(name, shape, dt=F32):
        return place(name, shape, region(4 * int(np.prod(shape[1:]))), dt)

    cst = fixed("consts", [P, NCONST])
    prm = fixed("params", [P, DEPTH, NPARAM])
    half_w0a0 = fixed("half_w0a0", [P, DEPTH, 8])
    bias_p = fixed("bias_prompt", [P, 4, KEYS])
    bias_s = fixed("bias_sample", [P, 2, KEYS_S])
    lora = fixed("lora", [P, 1024])
    sinks = fixed("sinks", [P, 8])
    gate_bias = fixed("gate_bias", [P, 1])
    m_init = fixed("m_init", [P, 1])
    shift_out = fixed("shift_out", [P, 2 * CT])
    stats = fixed("stats", [P, 64])
    s_nat = fixed("c_state_natural", [P, 4, 64])
    s_out = fixed("c_state_out", [P, 4, 64])
    shift_rows = fixed("shift_rows", [2 * CT, P])
    x_at = region(4 * KD * T)
    x = place("x", [P, KD, T], x_at)
    xnh_at = region(2 * 4 * KD * T)
    xh = place("xn_high", [P, KD, T], xnh_at, F32R)
    xl = place("xn_low", [P, KD, T], xnh_at + 4 * KD * T, F32R)
    wraw = fixed("w_raw", [P, NRAW, 8, P])
    wh = fixed("w_high", [P, NSPLIT, 8, P], F32R)
    wl = fixed("w_low", [P, NSPLIT, 8, P], F32R)
    arena = base[0]
    cc_at = arena
    craw_at = (cc_at + 4 * CT * CW + 63) // 64 * 64
    a_work = (craw_at + 4 * 2 * (CW + 1) + 63) // 64 * 64
    acols_at = (limit - 4 * 16 * T) // 64 * 64
    cc = place("c_cols", [P, CT, CW], cc_at)
    craw = place("c_raw", [P, 2, CW + 1], craw_at)
    acols = place("a_cols", [P, 16, T], acols_at)
    AK, AV, AO, AQ = 0, 4, 8, 12

    def worker(start):
        at = [start]

        def w(name, shape, dt=F32):
            t = place(name, shape, at[0], dt)
            at[0] += (4 * int(np.prod(shape[1:])) + 31) // 32 * 32
            return t
        w.end = lambda: at[0]
        return w

    w = worker(x_at)
    bq = w("b_queries", [P, 4 * T])
    bkv = w("b_keys_values", [P, 2, T])
    sc = w("b_scores", [P, 4, KEYS])
    ks = w("b_keys_sample", [P, KEYS_S])
    kcache = w("b_k_cache", [P, P])
    merged = place("merged", [P, KD, T], x_at)
    w = worker(craw_at)
    decay_log, in_rate, kk, scratch, kprime, cum = (w(n, [P, 512]) for n in (
        "c_decay_log", "c_in_rate", "c_kk", "c_scratch", "c_kprime", "c_cum"))
    kap_r = w("c_kappa_r", [P, 4, 2, P])
    tanh_w = w("c_tanh_w", [64, P])
    sig_g = w("c_sig_g", [P, P])
    vt, kt, bt = (w(n, [P, 512]) for n in ("c_v_tokens", "c_k_tokens", "c_b_tokens"))
    a_rb = w("c_a_rb", [P, 8, 2, 64])
    b_rk = w("c_b_rk", [P, 8, 2, 64])
    inv, invT, w_lev, neg_z = (t[:].rearrange("p (h t) -> p h t", t=64) for t in (scratch, kk, in_rate, kprime))
    rhs_z = w("c_rhs_z", [P, 8, 64])
    state = w("c_state", [P, 2, 4, 64])
    diag = w("c_block_diagonal", [P, 3, 8, P])
    a_bd, w_bd, invT_bd = diag[:, 0], diag[:, 1], diag[:, 2]
    bh = w("b_heads", [P, 4, T])
    rest = (w.end() + 63) // 64 * 64
    w = worker(rest)
    pt0 = w("b_probsT_first", [P, 512])
    pt1 = w("b_probsT_second", [P, 512])
    va = w("b_values_even", [P, 5, P])
    vb = w("b_values_odd", [P, 4, P])
    vcache = w("b_v_cache", [P, P])
    kout = w("b_k_out", [P, 2, P])
    assert w.end() <= acols_at + 4 * AQ * T
    w = worker(rest)
    gate_t = w("gate_tanh", [P, 2, T])
    prod = w("gate_product", [P, 2, T])
    assert w.end() <= acols_at + 4 * AQ * T
    w = worker(a_work)
    r_li, r_m, r_g, r_in, r_nm, r_wk = (w(n, [P, T]) for n in ("a_li", "a_m", "a_g", "a_inter", "a_negm", "a_wk"))
    a_den = w("a_den", [P, 4, T])
    r_lf, r_f = a_den[:, 0, :], a_den[:, 1, :]
    dexp, qt, kw = (w(n, [P, 512]) for n in ("a_dexp", "a_q_inter", "a_k_weighted"))
    vo = w("a_values_ones", [P, 4, 256])
    cn = w("a_state", [P, 4, 256])
    a_cols_t = w("a_cols_tokens", [P, 8])
    a_dec = w("a_decay", [P, 4])
    m_prev = w("a_m_prev", [P, 8])
    g_last = w("a_g_last", [P, 8])
    ncol = w("a_n_col", [P, 4])
    assert w.end() <= acols_at
    squares = place("squares", [P, KD, T], acols_at)
    mixed = place("mixed", [P, KD, T], acols_at + 4 * KD * T)
    rstd = place("rstd", [P, T], a_work)
    w = worker(arena)
    hid_h = w("hidden_high", [P, KF, T], F32R)
    hid_l = w("hidden_low", [P, KF, T], F32R)
    ffn_t = w("ffn_tanh", [P, 2, T])
    ffn_p = w("ffn_product", [P, 2, T])
    ffn_y = place("ffn_y", [P, KD, T], xnh_at)
    sq2 = place("squares_ffn", [P, KD, T], arena)
    w = worker(arena)
    x_tok = w("x_tokens", [P, 5, D])
    prm_rows = w("param_rows", [P, DEPTH, P])
    bias_line = w("bias_line", [8, 256])
    table = w("bias_table", [32, 8])
    y_tok = place("y_tokens", [P, 5, D], arena)

    ctx = ExitStack()
    with ctx:
        gp = ctx.enter_context(nc.psum_tensor("psum_products", [P, 4, 512], F32))
        mp = [ctx.enter_context(nc.psum_tensor(f"psum_mixer{i}", [P, 512], F32)) for i in range(4)]
        nsem = [0]

        def sem(name):
            nsem[0] += 1
            return ctx.enter_context(nc.semaphore(name))

        def count(name):
            return Count(sem(name))

        def C(name, lo=0, n=None):
            at, width = const_at[name]
            return cst[:, at + lo:at + (width if n is None else lo + n)]

        bank = [Bank(f"bank{i}", mp[i], sem) for i in range(4)]
        landed = [count(f"weights_landed{i}") for i in range(NRAW)]
        high_ready, low_ready = count("w_high_ready"), count("w_low_ready")
        products = count("products_done")
        emptied = {r: count(f"products_emptied_by_{r}") for r in ("act", "dve")}
        xn_part, xh_ready, xl_ready = count("xn_ready"), count("xn_high_ready"), count("xn_low_ready")
        sq_ready = count("squares_ready")
        chains = {e: count(f"{e}_steps") for e in ("act", "dve", "pe", "pool")}
        ld_const, ld_x, ld_prm, ld_layer = (count(n) for n in ("consts_in", "x_in", "params_in", "layer_in"))
        bias_out, bias_in = count("bias_written"), count("bias_read")
        stored = count("outputs_stored")
        flows = {}

        def flow(name):
            if name not in flows:
                flows[name] = count(name)
            return flows[name]

        units = [s for s in plan if s[0] in GEMMS]
        unit_no = {s: i for i, s in enumerate(units)}
        split_no, unsplit_no, n_split, n_unsplit = {}, {}, 0, 0
        for s in units:
            if s[0] in UNSPLIT:
                unsplit_no[s] = n_unsplit
                n_unsplit += 1
            else:
                split_no[s] = n_split
                n_split += 1
        tiles, reads = {}, {"act": 0, "dve": 0}
        order = []
        for s in units:
            key = s[:3] if s[0] == "ffn_out" else s
            if key not in tiles:
                r = GEMMS[s[0]]
                reads[r] += 1
                tiles[key] = (len(order) % 2, r, reads[r])
                order.append(key)
        tile_no = {k: i for i, k in enumerate(order)}

        def unit_parts(s):
            kind, l = s[0], s[1]

            def cols(src, c0, n=P, m0=0, rows=None):
                v = src[l] if rows is None else src[l, rows[0]:rows[1]]
                nk = v.shape[0] // P
                return ((slice(0, P), slice(0, nk), slice(m0, m0 + n)),
                        v[:, c0:c0 + n].rearrange("(k p) m -> p k m", p=P))

            if kind == "cols_c":
                return [cols(a["w_in"], OFF_C + s[2] * P)]
            if kind == "cols_a":
                if s[2] < 16:
                    return [cols(a["w_in"], s[2] * P)]
                return [cols(a["w_in"], 4 * A_W, A_H, 0), cols(a["w_in"], 4 * A_W + A_H, A_H, 32)]
            if kind == "cols_b":
                if s[2] < 4:
                    return [cols(a["w_in"], OFF_B + s[2] * 64, 64, 0), cols(a["w_in"], OFF_B + 256 + s[2] * 64, 64, 64)]
                return [cols(a["w_in"], OFF_B + s[2] * P)]
            if kind == "gate":
                return [cols(a["w_in"], OFF_G + s[2] * D + s[3] * P)]
            if kind == "branch":
                c0 = s[3] * P
                if s[2] == 1:
                    v = a["w_branch_b"][l].rearrange("(v m d) n -> v d m n", v=2, d=64)
                    return [((slice(64 * i, 64 * i + 64), slice(0, 4), slice(0, P)), v[i, :, :, c0:c0 + P])
                            for i in range(2)]
                return [cols(a["w_branch_a" if s[2] == 0 else "w_branch_c"], c0)]
            if kind == "mix":
                return [cols(a["w_out"], s[2] * P)]
            if kind == "ffn_gate":
                return [cols(a["w_ffn_in"], s[2] * P)]
            if kind == "ffn_up":
                return [cols(a["w_ffn_in"], D_FF + s[2] * P)]
            k0 = 8 * s[3]
            return [cols(a["w_ffn_out"], s[2] * P, rows=(k0 * P, min(k0 + 8, KF) * P))]

        landed_at = {}
        tot = [0] * NRAW
        for i, s in enumerate(units):
            tot[i % NRAW] += 16 * len(unit_parts(s))
            landed_at[s] = (i % NRAW, tot[i % NRAW])

        def nk_of(s):
            return 4 if s[0] == "branch" else (min(8, KF - 8 * s[3]) if s[0] == "ffn_out" else 8)

        def pair_view(pair, lo=0, hi=P):
            return gp[lo:hi, 2 * pair:2 * pair + 2, 0:HALF]

        def halves(ap):
            return ap.rearrange("p (b n) -> p b n", b=2)

        def c_group(g):
            return (P, P * g, 2, 64) if g < 4 else (TS, TP + 1, 1, TS)

        def gv(t, n):
            return t[:, 0:4 * n].rearrange("p (f n) -> p f n", n=n)

        def pb(l, name, n, width):
            at = PARAM_AT[name]
            return view(prm[:, l, at:at + n], [[1, n], [0, width]])

        block = ctx.enter_context(nc.Block())

        @block.tensor
        def _(pe):
            def mm(out, lhsT, rhs, start=True, stop=True):
                return pe.matmul(out, lhsT, rhs, start=start, stop=stop, skip_group_check=True)

            def order_after(ins):
                chains["pe"].inc(ins)
                pe.wait_ge(chains["pe"].sem, chains["pe"].value)

            done_k = {}

            def gemm(s, rh=None, rl=None, rhs=None, first=True, last=True, cut=HALF, wait_k=False, k0=0, nk=8, spare=False,
                     steps=8):
                ks = range(done_k.get(s, 0), min(nk, done_k.get(s, 0) + steps))
                if not ks:
                    return
                done_k[s] = ks[-1] + 1
                key = s[:3] if s[0] == "ffn_out" else s
                pair, reader, turn = tiles[key]
                if s in split_no:
                    slot = split_no[s] % NSPLIT
                    if ks[0] == 0:
                        pe.wait_ge(low_ready.sem, split_no[s] + 1)
                else:
                    at, value = landed_at[s]
                    slot = unit_no[s] % NRAW
                    if ks[0] == 0:
                        pe.wait_ge(landed[at].sem, value)
                if first and ks[0] == 0 and tile_no[key] >= 2:
                    _, r, t = tiles[order[tile_no[key] - 2]]
                    pe.wait_ge(emptied[r].sem, t)
                for k in ks:
                    if wait_k:
                        xl_ready.wait_next(pe, "pe")
                    if rhs is None:
                        passes = [(wh[:, slot, k], rh[:, k0 + k]), (wh[:, slot, k], rl[:, k0 + k]),
                                  (wl[:, slot, k], rh[:, k0 + k])]
                    else:
                        passes = [(wraw[:, slot, k], rhs[k])]
                    for i, (wt, act_) in enumerate(passes):
                        pieces = [(0, 0, 0, cut), (1, 0, cut, T - cut)]
                        if spare:
                            pieces = [(0, 0, 0, cut), (1, 0, cut, TP - cut), (1, TP - cut, TP + 1, TS)]
                        for b, to, at, n in pieces:
                            last_mm = mm(gp[:, 2 * pair + b, to:to + n], wt, act_[:, at:at + n],
                                         start=first and k == 0 and i == 0 and to == 0,
                                         stop=last and k == nk - 1 and i == len(passes) - 1)
                if ks[-1] == nk - 1:
                    products.inc(last_mm)

            unit_at = [0]

            def product(s, steps=8):
                kind = s[0]
                if kind == "branch":
                    l, b, m = s[1:]
                    rhs = [(acols[:, AQ + k, :], bh[:, k, :], cc[:, k, :])[b] for k in range(4)]
                    gemm(s, rhs=rhs, nk=4, spare=b == 2, steps=steps)
                else:
                    gemm(s, rh=xh, rl=xl, cut=SPLIT_C if kind == "cols_c" or (kind == "cols_b" and s[2] < 4) else HALF,
                         wait_k=bool(first_user.get("norm")), steps=steps)
                    first_user["norm"] = False

            def fill(steps):
                if unit_at[0] < len(units):
                    s = units[unit_at[0]]
                    if s[0] in ("cols_c", "gate") or (s[0] == "branch" and s[3] > 0):
                        product(s, steps)

            def sum_squares(src):
                bank[0].claim(pe)
                bank[1].claim(pe)
                for k in range(KD):
                    sq_ready.wait_next(pe, "pe")
                    for b in range(2):
                        last = mm(mp[b][:, 0:HALF], C("ones"), src[:, k, b * HALF:(b + 1) * HALF],
                                  start=(k == 0), stop=(k == KD - 1))
                        if k == KD - 1:
                            bank[b].filled(last, "act")

            def load_x():
                pe.wait_ge(ld_const.sem, 32)
                pe.wait_ge(ld_prm.sem, 16 * DEPTH * len(PARAM_ROWS))
                bank[0].claim(pe)
                for l in range(DEPTH):
                    last = pe.transpose(mp[0][:, l * P:l * P + NPARAM], prm_rows[0:NPARAM, l, :], C("ident")[0:NPARAM, 0:NPARAM])
                bank[0].filled(last, "act")
                bank[1].claim(pe)
                bank[1].filled(mm(mp[1][0:8, 0:256], table[:], C("bucket_hot")[0:32]), "dve")
                pe.wait_ge(ld_x.sem, 16 * 5)
                for k in range(KD):
                    b = bank[2 + k % 2]
                    b.claim(pe)
                    for t in range(4):
                        last = pe.transpose(b.t[:, t * P:(t + 1) * P], x_tok[:, t, k * P:(k + 1) * P], C("ident"))
                    b.filled(last, "act" if k % 2 else "dve")
                bank[0].claim(pe)
                for k in range(KD):
                    last = pe.transpose(mp[0][:, k * TS:(k + 1) * TS], x_tok[0:TS, 4, k * P:(k + 1) * P],
                                        C("ident")[0:TS, 0:TS])
                bank[0].filled(last, "act")

            def c_shift_out():
                flow("shift_cols").wait_next(pe, "pe")
                bank[0].claim(pe)
                bank[0].filled(pe.transpose(mp[0][0:2 * CT, 0:P], shift_out[:], C("ident")), "act")

            def c_prep(l, g):
                n, at, nch, L = c_group(g)
                if g == 0:
                    pe.wait_ge(ld_layer.sem, 16 * 12 * (l + 1))
                bank[0].claim(pe)
                flow("c_tanh_w").wait_next(pe, "pe")
                for f in range(4):
                    last = mm(mp[0][:, f * n:(f + 1) * n], lora[0:64, f * P:(f + 1) * P], tanh_w[:, 0:n])
                bank[0].filled(last, "act", ("c_lw", l, g))
                bank[1].claim(pe)
                for f in range(4):
                    last = mm(mp[1][:, f * n:(f + 1) * n], lora[64:128, f * P:(f + 1) * P], cc[64:128, 12, at:at + n])
                bank[1].filled(last, "act", ("c_la", l, g))
                fill(2)
                bank[2].claim(pe)
                flow("c_kk_sq").wait_next(pe, "pe")
                bank[2].filled(mm(mp[2][:, 0:4 * n], C("headones"), scratch[:, 0:4 * n]), "dve")
                bank[0].claim(pe)
                for f in range(4):
                    last = pe.transpose(mp[0][0:n, f * P:(f + 1) * P], cc[:, 8 + f, at:at + n], C("ident"))
                bank[0].filled(last, "act")
                fill(8)
                bank[3].claim(pe)
                flow("c_rk").wait_next(pe, "pe")
                bank[3].filled(mm(mp[3][:, 0:4 * n], C("headones"), scratch[:, 0:4 * n]), "dve")
                flow("c_scaled").wait_next(pe, "pe")
                for b, src in ((1, kprime), (2, in_rate)):
                    bank[b].claim(pe)
                    for f in range(4):
                        last = pe.transpose(mp[b][0:n, f * P:(f + 1) * P], gv(src, n)[:, f, :], C("ident"))
                    bank[b].filled(last, "act")

            def heads():
                for p in range(4):
                    for q in range(2):
                        yield 2 * p + q, p, q

            def c_gram(l, g):
                n, at, nch, L = c_group(g)

                def grams(banks, src, q):
                    for p in range(4):
                        h = 2 * p + q
                        for c in range(nch):
                            out = mp[banks[h // 4]][64 * c:64 * c + L, (h % 4) * 2 * L:(h % 4 + 1) * 2 * L]
                            last = mm(out.rearrange("p (u t) -> p u t", u=2),
                                      gv(src, n)[64 * q:64 * q + 64, p, c * L:c * L + L],
                                      kap_r[64 * q:64 * q + 64, p, :, c * L:c * L + L])
                        if p % 2 == 1:
                            ends.append((banks[h // 4], last))

                ends = []
                for b in (0, 3, 1):
                    bank[b].claim(pe)
                grams((0, 3), in_rate, 0)
                for q in range(2):
                    for p in range(4):
                        for c in range(nch):
                            last = mm(mp[1][64 * c:64 * c + L, (2 * p + q) * L:(2 * p + q + 1) * L],
                                      kap_r[64 * q:64 * q + 64, p, 0, c * L:c * L + L],
                                      gv(in_rate, n)[64 * q:64 * q + 64, p, c * L:c * L + L])
                    if q == 0:
                        order_after(last)
                        ends = []
                        grams((0, 3), in_rate, 1)
                        for b, ins in ends:
                            bank[b].filled(ins, "dve")
                bank[1].filled(last, "dve")
                bank[2].claim(pe)
                bank[0].claim(pe)
                ends = []
                grams((2, 0), kprime, 1)
                order_after(ends[-1][1])
                ends = []
                grams((2, 0), kprime, 0)
                for b, ins in ends:
                    bank[b].filled(ins, "dve")

            def c_level(l, g, k):
                n, at, nch, L = c_group(g)

                def by_head(b, lhsT, rhs, mark=None):
                    bank[b].claim(pe)
                    for h in range(8):
                        last = mm(mp[b][0:n, h * L:(h + 1) * L], lhsT[0:n, h, 0:n], rhs[0:n, h, 0:L])
                    bank[b].filled(last, "dve", mark)

                if k == 1:
                    flow("c_a_bd").wait_next(pe, "pe")
                    flow("c_inv0").wait_next(pe, "pe")
                else:
                    bank[3].wait_emptied(pe, ("c_inv", l, g, k - 1))
                by_head(1, a_bd, inv, ("c_w", l, g, k))
                fill(2)
                if k < (5 if L == 64 else 4):
                    bank[1].claim(pe)
                    flow("c_invT_bd").wait_next(pe, "pe")
                    by_head(3, invT_bd, w_lev, ("c_inv", l, g, k))
                    fill(1)
                flow("c_w_bd").wait_next(pe, "pe")
                by_head(2, w_bd, invT, ("c_invT", l, g, k))
                fill(1)

            def c_chain(l, g, c):
                n, at, nch, L = c_group(g)
                if g == 4:
                    pe.wait_ge(flow("c_state_in").sem, 16 * (l + 1))
                    bank[0].claim(pe)
                    for h, p, q in heads():
                        last = mm(mp[0][64 * q:64 * q + 64, p * 64:(p + 1) * 64], s_nat[64 * q:64 * q + 64, p, :],
                                  C("ident")[64 * q:64 * q + 64, 64 * q:64 * q + 64])
                    bank[0].filled(last, "dve")
                r = slice(64 * c, 64 * c + L)
                cur = (2 * g + c) % 2
                bank[0].claim(pe)
                for h in range(8):
                    last = mm(mp[0][r, h * 64:(h + 1) * 64], b_rk[r, h, 0, 0:L], vt[r, h * 64:(h + 1) * 64],
                              start=h == 0, stop=False)
                order_after(last)
                flow("c_state").wait_next(pe, "pe")
                for q in (c, 1 - c):
                    for p in range(4):
                        last = mm(mp[0][r, (2 * p + q) * 64:(2 * p + q + 1) * 64],
                                  kap_r[64 * q:64 * q + 64, p, 0, c * L:c * L + L],
                                  state[64 * q:64 * q + 64, cur, p, :], start=False, stop=q != c)
                    if q == c:
                        order_after(last)
                bank[0].filled(last, "dve")
                bank[3].claim(pe)
                for h, p, q in heads():
                    last = mm(mp[3][64 * q:64 * q + 64, p * L:(p + 1) * L], state[64 * q:64 * q + 64, cur, p, :],
                              kap_r[64 * q:64 * q + 64, p, 1, c * L:c * L + L], start=p == 0, stop=False)
                order_after(last)
                fill(1)
                bank[1].claim(pe)
                bank[0].claim(pe)
                for h in range(8):
                    last = mm(mp[1][r, h * 64:(h + 1) * 64], invT[r, h, 0:L], rhs_z[r, h, :])
                bank[1].filled(last, "dve")
                fill(1)
                bank[2].claim(pe)
                bank[1].claim(pe)
                for h, p, q in heads():
                    out = mp[2][64 * q:64 * q + 64, p * 64:(p + 1) * 64]
                    mm(out, kt[r, h * 64:(h + 1) * 64], vt[r, h * 64:(h + 1) * 64], stop=False)
                    last = mm(out, bt[r, h * 64:(h + 1) * 64], neg_z[r, h, :], start=False)
                bank[2].filled(last, "dve")
                for h, p, q in heads():
                    out = mp[3][64 * q:64 * q + 64, p * L:(p + 1) * L]
                    mm(out, vt[r, h * 64:(h + 1) * 64], b_rk[r, h, 1, 0:L], start=False, stop=False)
                    last = mm(out, neg_z[r, h, :], a_rb[r, h, 1, 0:L], start=False)
                bank[3].filled(last, "act", ("c_y", l, g, c))
                fill(4)

            def c_finish(l, g):
                n, at, nch, L = c_group(g)
                y = cc[:, 0:4, at:at + n]
                bank[0].claim(pe)
                bank[3].wait_emptied(pe, ("c_y", l, g, nch - 1))
                bank[0].filled(mm(mp[0][:, 0:4 * n], C("headones"), y), "dve")
                bank[1].claim(pe)
                flow("c_gate_in").wait_next(pe, "pe")
                for f in range(4):
                    last = mm(mp[1][:, f * n:(f + 1) * n], lora[:, 512 + f * P:512 + (f + 1) * P], sig_g[:, 0:n])
                bank[1].filled(last, "act")
                fill(3)
                bank[2].claim(pe)
                flow("c_dev_sq").wait_next(pe, "pe")
                bank[2].filled(mm(mp[2][:, 0:4 * n], C("headones"), scratch[:, 0:4 * n]), "act")
                if g >= 3:
                    flow("c_state").wait_next(pe, "pe")
                    cur = 0 if g == 3 else 1
                    bank[3].claim(pe)
                    for h, p, q in heads():
                        last = mm(mp[3][64 * q:64 * q + 64, p * 64:(p + 1) * 64], state[64 * q:64 * q + 64, cur, p, :],
                                  C("ident")[64 * q:64 * q + 64, 64 * q:64 * q + 64])
                    bank[3].filled(last, "act", ("c_state", l, g))

            def a_chunk(l, g):
                n, at = group(g)
                if g == 0:
                    flow("a_rows").wait_next(pe, "pe")
                sel = lambda h, m: C("sel")[0:4, h * P:h * P + m]
                bank[0].claim(pe)
                for h in range(4):
                    last = mm(mp[0][0:n, h * n:(h + 1) * n], sel(h, n), r_g[0:4, at:at + n])
                bank[0].filled(last, "dve", ("a_g", l, g))
                bank[1].claim(pe)
                for h in range(4):
                    last = mm(mp[1][:, h * n:(h + 1) * n], sel(h, P), r_in[0:4, at:at + n])
                bank[1].filled(last, "dve")
                bank[2].claim(pe)
                mm(mp[2][0:n, 0:4], r_li[0:4, at:at + n], C("ident")[0:4, 0:4])
                bank[2].filled(mm(mp[2][0:n, 4:8], r_wk[0:4, at:at + n], C("ident")[0:4, 0:4]), "act")
                bank[3].claim(pe)
                for h in range(4):
                    last = mm(mp[3][0:n, h * n:(h + 1) * n], acols[:, AK + h, at:at + n], acols[:, AQ + h, at:at + n])
                bank[3].filled(last, "dve")
                for b, c0 in ((0, AK), (1, AV)):
                    fill(2)
                    bank[b].claim(pe)
                    for h in range(4):
                        last = pe.transpose(mp[b][0:n, h * P:(h + 1) * P], acols[:, c0 + h, at:at + n], C("ident"))
                    bank[b].filled(last, "act")
                fill(1)

            def a_chunk_out(l, g):
                n, at = group(g)
                sel = lambda h, m: C("sel")[0:4, h * P:h * P + m]
                bank[0].claim(pe)
                for h in range(4):
                    last = mm(mp[0][:, h * n:(h + 1) * n], sel(h, P), r_nm[0:4, at:at + n])
                bank[0].filled(last, "dve")
                bank[3].claim(pe)
                bank[1].claim(pe)
                if g == 4:
                    flow("a_n_spread").wait_next(pe, "pe")
                for b, c0, mark in ((3, P, ("a_den", l, g)), (2, 0, None)):
                    bank[b].claim(pe)
                    for h in range(4):
                        out = mp[b][:, h * n:(h + 1) * n]
                        mm(out, vo[0:n, h, c0:c0 + P], dexp[0:n, h * n:(h + 1) * n], stop=False)
                        last = mm(out, cn[:, h, c0:c0 + P], qt[:, h * n:(h + 1) * n], start=False)
                    bank[b].filled(last, "act", mark)
                for b in range(2):
                    if b:
                        fill(1)
                    bank[1 + b].claim(pe)
                    for i in range(2):
                        h = 2 * b + i
                        last = mm(mp[1 + b][:, i * 256:(i + 1) * 256], kw[0:n, h * P:(h + 1) * P], vo[0:n, h, :])
                    bank[1 + b].filled(last, "dve", ("a_state", l, g))

            def a_finish(l):
                for h in range(4):
                    fill(2)
                    flow("a_h_sq").wait_next(pe, "pe")
                    for b in range(2):
                        bk = 2 * (h % 2) + b
                        bank[bk].claim(pe)
                        bank[bk].filled(mm(mp[bk][:, 0:HALF], C("ones"), (r_li, r_wk)[h % 2][:, b * HALF:(b + 1) * HALF]),
                                        "dve", ("a_norm", l, h))

            def b_values(l):
                pe.wait_ge(emptied["act"].sem, tiles[("cols_b", l, 5)][2])
                bank[0].claim(pe)
                for j in range(4):
                    last = pe.transpose(mp[0][:, j * P:(j + 1) * P], bkv[:, 1, j * P:(j + 1) * P], C("ident"))
                bank[0].filled(last, "act")
                bank[1].claim(pe)
                for j in range(4):
                    m = P if j < 3 else 64
                    last = pe.transpose(mp[1][0:m, j * P:(j + 1) * P], bkv[:, 1, 64 + j * P:64 + j * P + m], C("ident"))
                bank[1].filled(last, "dve")
                bank[2].claim(pe)
                pe.transpose(mp[2][:, 0:P], bkv[:, 0, TP - P:TP], C("ident"))
                pe.transpose(mp[2][0:TS, P:2 * P], bkv[:, 0, TP:T], C("ident"))
                bank[2].filled(pe.transpose(mp[2][0:TS, 2 * P:3 * P], bkv[:, 1, TP:T], C("ident")), "act", ("b_values", l))
                bank[3].claim(pe)
                pe.wait_ge(flow("b_cache_in").sem, 32 * (l + 1))
                bank[3].filled(pe.transpose(mp[3][:, 0:P], kcache[:], C("ident")), "dve")

            def b_chunk(l, c):
                sample = c == 8
                if c == 0:
                    flow("b_values").wait_next(pe, "pe")
                if sample:
                    n, nk, nt, at = TS, KEYS_S, 2, TP
                    keys = ks[:, :]
                else:
                    n, nt, at = CHUNK, 4, CHUNK * c
                    nk = CHUNK * min(3, c + 1)
                    keys = bkv[:, 0, at + CHUNK - nk:at + CHUNK]
                per = nt // 2
                hpt = P // n
                first_n, second_n = min(nk, P), max(nk - P, 0)
                for v in range(2):
                    r = slice(64 * v, 64 * v + 64)
                    bank[v].claim(pe)
                    for i in range(per):
                        last = mm(mp[v][:, i * nk:(i + 1) * nk], bq[r, 4 * at + i * P:4 * at + (i + 1) * P], keys[r, :])
                    bank[v].filled(last, "dve")
                fill(5)
                flow("b_probs").wait_next(pe, "pe")
                bank[2].claim(pe)
                for t in range(nt):
                    last = pe.transpose(mp[2][0:first_n, t * P:(t + 1) * P], sc[:, t, 0:first_n], C("ident"))
                bank[2].filled(last, "act")
                if second_n:
                    bank[3].claim(pe)
                    for t in range(nt):
                        last = pe.transpose(mp[3][0:second_n, t * P:(t + 1) * P], sc[:, t, P:P + second_n], C("ident"))
                    bank[3].filled(last, "dve")
                fill(2)
                if second_n:
                    bank[3].claim(pe)
                bank[2].claim(pe)
                bank[0].claim(pe)
                for t in range(nt):
                    v, i = t // per, t % per
                    r = slice(64 * v, 64 * v + 64)
                    if sample:
                        va0, va1 = vcache[:, r], va[0:TS, 4, r]
                    else:
                        start = at + CHUNK - nk
                        src = va if start % P == 0 else vb
                        j = start // P
                        va0, va1 = src[0:first_n, j, r], (src[0:64, j + 1, r] if second_n else None)
                    out = mp[0][r, i * P:(i + 1) * P]
                    last = mm(out, va0, pt0[0:first_n, t * P:(t + 1) * P], stop=not second_n)
                    if second_n:
                        last = mm(out, va1, pt1[0:second_n, t * P:(t + 1) * P], start=False)
                bank[0].filled(last, "act", ("b_out", l, c))

            def store_y():
                for t in range(5):
                    n, at = group(t)
                    for b in range(2):
                        bk = 2 * (t % 2) + b
                        bank[bk].claim(pe)
                        for k in range(4):
                            last = pe.transpose(mp[bk][0:n, k * P:(k + 1) * P], x[:, 4 * b + k, at:at + n], C("ident"))
                        bank[bk].filled(last, "act" if b else "dve", ("y", t, b))

            first_user = {}
            for s in plan:
                kind = s[0]
                if kind == "load_x":
                    load_x()
                elif kind == "norm_pre":
                    sum_squares(squares if s[2] == 0 or s[2] == 2 else sq2)
                    first_user["norm"] = True
                elif kind == "norm_post":
                    sum_squares(squares if s[2] == 1 else sq2)
                elif kind in ("cols_c", "cols_a", "cols_b", "gate", "ffn_gate", "ffn_up", "branch"):
                    if kind == "branch" and s[3] == 0:
                        if s[2] == 0:
                            flow("a_h").wait_next(pe, "pe")
                        elif s[2] == 1:
                            bank[0].wait_emptied(pe, ("b_out", s[1], 8))
                        else:
                            flow("c_h").wait_next(pe, "pe", GROUPS)
                    product(s)
                elif kind == "merge_split":
                    pass
                elif kind == "mix":
                    gemm(s, rh=xh, rl=xl, wait_k=s[2] == 0)
                elif kind == "ffn_out":
                    l, m, q = s[1:]
                    if m == 0 and q == 0:
                        flow("hidden").wait_next(pe, "pe", KF)
                    gemm(s, rh=hid_h, rl=hid_l, k0=8 * q, nk=nk_of(s), first=q == 0, last=q == 2)
                elif kind == "c_shift_out":
                    c_shift_out()
                elif kind == "store_y":
                    pe.wait_ge(flow("x_new").sem, KD * 2 * DEPTH)
                    store_y()
                else:
                    {"c_prep": c_prep, "c_gram": c_gram, "c_level": c_level, "c_chain": c_chain, "c_finish": c_finish,
                     "a_rows": lambda l: None, "a_rows_exp": lambda l: None, "a_chunk": a_chunk,
                     "a_chunk_out": a_chunk_out, "a_finish": a_finish, "b_values": b_values,
                     "b_chunk": b_chunk}[kind](*s[1:])
                if kind in GEMMS:
                    unit_at[0] += 1

        @block.scalar
        def _(act):
            step = Lane(act, chains["act"])

            def fn(out, in_, f, **kw_):
                return act.activation(out, in_, f, **kw_)

            def split_high(n):
                if n >= n_split:
                    return
                s = split_units[n]
                if n >= NSPLIT:
                    act.wait_ge(products.sem, unit_no[split_units[n - NSPLIT]] + 1)
                at, value = landed_at[s]
                act.wait_ge(landed[at].sem, value)
                nk = nk_of(s)
                high_ready.inc(fn(wh[:, n % NSPLIT, 0:nk], wraw[:, unit_no[s] % NRAW, 0:nk], ACT.Copy))

            def product_done(s):
                act.wait_ge(products.sem, unit_no[s] + 1)
                return tiles[s[:3] if s[0] == "ffn_out" else s][0]

            def load_x():
                act.wait_ge(ld_const.sem, 32)
                bank[0].read(act, "act")
                step(fn(prm[:, :, :], mp[0][:, 0:DEPTH * P].rearrange("p (l n) -> p l n", n=P)[:, :, 0:NPARAM], ACT.Copy),
                     bank[0].empty["act"])
                for k in range(1, KD, 2):
                    bank[3].read(act, "act")
                    step(fn(x[:, k, 0:TP], mp[3][:], ACT.Copy), bank[3].empty["act"])
                bank[0].read(act, "act")
                step(fn(x[:, :, TP:T], mp[0][:, 0:KD * TS].rearrange("p (k n) -> p k n", n=TS), ACT.Copy), bank[0].empty["act"])
                flow("x_even").wait_next(act, "act", 4)

            def norm(src, sq, which):
                for k in range(KD):
                    if which in ("x", "x_new"):
                        if which == "x_new":
                            flow("x_new").wait_next(act, "act")
                    sq_ready.inc(fn(sq[:, k, :], src[:, k, :], ACT.Square))
                for b in range(2):
                    bank[b].read(act, "act")
                    step(fn(rstd[:, b * HALF:(b + 1) * HALF], mp[b][:, 0:HALF], ACT.Ln, scale=1.0 / D,
                            bias=C("scalars", 0, 1)), bank[b].empty["act"])
                step(fn(rstd[:], rstd[:], ACT.Exp, scale=-0.5), flow("rstd"))

            def norm_pre(l, w_):
                norm(x, squares, "x" if l == 0 and w_ == 0 else "x_new")
                for k in range(KD):
                    xn_part.wait_next(act, "act")
                    xh_ready.inc(fn(xh[:, k, :], squares[:, k, :], ACT.Copy))

            def norm_post(l, w_):
                if w_ == 1:
                    norm(mixed, squares, "")
                else:
                    norm(ffn_y, sq2, "")

            def cols_c(s):
                l, j = s[1:]
                i = l * CT + j
                pair = product_done(s)
                if i >= 2:
                    act.wait_ge(flow("c_col").sem, i - 1)
                step(fn(craw[:, j % 2, 1:1 + TP].rearrange("p (b n) -> p b n", b=2),
                        gp[:, 2 * pair:2 * pair + 2, 0:SPLIT_C], ACT.Copy))
                step(fn(craw[:, j % 2, TP + 2:TP + 2 + TS], gp[:, 2 * pair + 1, SPLIT_C:SPLIT_C + TS], ACT.Copy),
                     emptied["act"])
                at = PARAM_AT["state_rwkv_shift"] + j
                step(fn(craw[:, j % 2, TP + 1:TP + 2], prm[:, l, at:at + 1], ACT.Copy), flow("c_raw"))

            def c_shift_out(l):
                bank[0].read(act, "act")
                if l > 0:
                    act.wait_ge(flow("shift_stored").sem, 32 * l)
                step(fn(shift_rows[:], mp[0][0:2 * CT, 0:P], ACT.Copy), bank[0].empty["act"])
                step(fn(stats[0:1, 60:61], stats[0:1, 60:61], ACT.Copy), flow("shift_rows"))

            def c_prep(l, g):
                n, at, nch, L = c_group(g)
                if g == 0:
                    act.wait_ge(flow("c_col").sem, CT * (l + 1))
                    act.wait_ge(flow("a_state_stored").sem, 96 * (l + 1))
                step(fn(tanh_w[:, 0:n], cc[0:64, 12, at:at + n], ACT.Tanh), flow("c_tanh_w"))
                step(fn(sig_g[:, 0:n], cc[:, 13, at:at + n], ACT.Tanh, scale=0.5), flow("c_sig_raw"))
                for b, dst, name in ((0, decay_log, "c_lw"), (1, in_rate, "c_la")):
                    bank[b].read(act, "act")
                    for f in range(4):
                        ins = fn(gv(dst, n)[:, f, :], mp[b][:, f * n:(f + 1) * n], ACT.Tanh, scale=0.5,
                                 bias=half_w0a0[:, l, 4 * b + f:4 * b + f + 1])
                        step(ins, bank[b].empty["act"] if f == 3 else None)
                    if b == 0:
                        flow("c_kk_raw").wait_next(act, "act")
                        step(fn(scratch[:, 0:4 * n], kk[:, 0:4 * n], ACT.Square), flow("c_kk_sq"))
                flow("c_ss").wait_next(act, "act")
                step(fn(kprime[:, 0:4 * n], kprime[:, 0:4 * n], ACT.Ln, scale=float(2 ** 20)))
                step(fn(kprime[:, 0:4 * n], kprime[:, 0:4 * n], ACT.Exp, scale=-0.5, bias=C("scalars", 2, 1)), flow("c_rn"))
                bank[0].read(act, "act")
                step(fn(vt[0:n, :], mp[0][0:n, :], ACT.Copy), bank[0].empty["act"])
                flow("c_cum").wait_next(act, "act")
                en = rhs_z[:, :, :].rearrange("p a b -> p (a b)")[:, 0:4 * n]
                step(fn(en, cum[:, 0:4 * n], ACT.Exp, scale=-1.0))
                step(fn(cum[:, 0:4 * n], cum[:, 0:4 * n], ACT.Exp))
                step(fn(decay_log[:, 0:4 * n], decay_log[:, 0:4 * n], ACT.Exp), flow("c_exps"))
                for b, dst in ((1, kt), (2, bt)):
                    bank[b].read(act, "act")
                    step(fn(dst[0:n, :], mp[b][0:n, :], ACT.Copy), bank[b].empty["act"])

            def diagonal(dst, src, L, flow_name):
                step(fn(dst[0:L, :, 0:L], src[0:L, :, 0:L], ACT.Copy), flow(flow_name) if L < 64 else None)
                if L == 64:
                    step(fn(dst[64:128, :, 64:128], src[64:128, :, 0:64], ACT.Copy), flow(flow_name))

            def c_gram(l, g):
                n, at, nch, L = c_group(g)
                flow("c_a_masked").wait_next(act, "act")
                diagonal(a_bd, a_rb[:, :, 0, :], L, "c_a_bd")
                flow("c_invT0").wait_next(act, "act")
                diagonal(invT_bd, invT, L, "c_invT_bd")

            def c_level(l, g, k):
                n, at, nch, L = c_group(g)
                bank[1].wait_emptied(act, ("c_w", l, g, k))
                diagonal(w_bd, w_lev, L, "c_w_bd")
                if k < (5 if L == 64 else 4) - 1:
                    bank[2].wait_emptied(act, ("c_invT", l, g, k))
                    diagonal(invT_bd, invT, L, "c_invT_bd")

            def c_chain(l, g, c):
                n, at, nch, L = c_group(g)
                bank[3].read(act, "act")
                step(fn(cc[:, 0:4, at + c * L:at + c * L + L], mp[3][:, 0:4 * L].rearrange("p (f t) -> p f t", t=L),
                        ACT.Copy), bank[3].empty["act"])

            def c_finish(l, g):
                n, at, nch, L = c_group(g)
                flow("c_dev").wait_next(act, "act")
                step(fn(scratch[:, 0:4 * n], kk[:, 0:4 * n], ACT.Square), flow("c_dev_sq"))
                bank[1].read(act, "act")
                step(fn(cum[:, 0:4 * n], mp[1][:, 0:4 * n], ACT.Copy), bank[1].empty["act"])
                bank[2].read(act, "act")
                step(fn(kprime[:, 0:4 * n], mp[2][:, 0:4 * n], ACT.Ln, scale=1.0 / 64, bias=C("scalars", 1, 1)),
                     bank[2].empty["act"])
                step(fn(kprime[:, 0:4 * n], kprime[:, 0:4 * n], ACT.Exp, scale=-0.5), flow("c_gn_r"))
                if g >= 3:
                    bank[3].read(act, "act")
                    before = 2 * l + g - 3
                    if before:
                        act.wait_ge(flow("c_state_stored").sem, 16 * before)
                    step(fn(s_out[:, :, :], mp[3][:, 0:256].rearrange("p (f t) -> p f t", t=64), ACT.Copy),
                         bank[3].empty["act"])

            def cols_a(s):
                l, j = s[1:]
                pair = product_done(s)
                if j < 16:
                    step(fn(halves(acols[:, (j + AQ) % 16, :]), pair_view(pair), ACT.Copy), emptied["act"])
                    return
                step(fn(halves(r_li[0:4, :]), pair_view(pair, 0, 4), ACT.Identity, bias=gate_bias[0:4, :]))
                step(fn(halves(r_nm[32:36, :]), pair_view(pair, 32, 36), ACT.Identity, bias=gate_bias[32:36, :]),
                     emptied["act"])

            def cols_b(s):
                l, j = s[1:]
                pair = product_done(s)
                if j == 0:
                    act.wait_ge(flow("x_kept").sem, 16 * (l + 1))
                if j < 4:
                    step(fn(view(bq[:], [[4 * SPLIT_C, 2], [SPLIT_C, 4], [1, CHUNK]], CHUNK * j),
                            gp[:, 2 * pair:2 * pair + 2, 0:SPLIT_C].rearrange("p b (c t) -> p b c t", t=CHUNK), ACT.Copy))
                    step(fn(bq[:, 4 * TP + TS * j:4 * TP + TS * (j + 1)], gp[:, 2 * pair + 1, SPLIT_C:SPLIT_C + TS], ACT.Copy),
                         emptied["act"])
                    return
                step(fn(halves(bkv[:, j - 4, :]), pair_view(pair), ACT.Copy), emptied["act"])

            def a_rows(l):
                flow("a_abs").wait_next(act, "act")
                step(fn(r_wk[0:4, :], r_g[0:4, :], ACT.Exp))
                step(fn(r_wk[0:4, :], r_wk[0:4, :], ACT.Ln, bias=C("scalars", 3, 1)[0:4]), flow("a_ln"))

            def a_rows_exp(l):
                flow("a_exp_in").wait_next(act, "act")
                step(fn(r_in[0:4, :], r_in[0:4, :], ACT.Exp))
                step(fn(r_wk[0:4, :], r_wk[0:4, :], ACT.Exp))
                step(fn(r_nm[0:4, :], r_m[0:4, :], ACT.Exp, scale=-1.0), flow("a_rows"))

            def a_chunk(l, g):
                n, at = group(g)
                bank[2].read(act, "act")
                step(fn(a_cols_t[0:n, :], mp[2][0:n, 0:8], ACT.Copy), bank[2].empty["act"])
                step(fn(a_cols_t[0:n, 4:8], a_cols_t[0:n, 4:8], ACT.Copy, scale=P ** -0.5), flow("a_cols_t"))
                bank[0].wait_emptied(act, ("a_g", l, g))
                step(fn(dexp[0:n, 0:4 * n], dexp[0:n, 0:4 * n], ACT.Exp), flow("a_dexp"))
                bank[0].read(act, "act")
                for h in range(4):
                    step(fn(kw[0:n, h * P:(h + 1) * P], mp[0][0:n, h * P:(h + 1) * P], ACT.Copy,
                            scale=a_cols_t[0:n, 4 + h:5 + h]), bank[0].empty["act"] if h == 3 else None)
                bank[1].read(act, "act")
                step(fn(vo[0:n, :, 0:P], mp[1][0:n, :].rearrange("p (h v) -> p h v", v=P), ACT.Copy), bank[1].empty["act"])

            def a_chunk_out(l, g):
                n, at = group(g)
                bank[3].read(act, "act")
                step(fn(a_den[:, :, at:at + n], gv(mp[3], n), ACT.Abs), bank[3].empty["act"])
                bank[2].read(act, "act")
                step(fn(acols[:, AQ:AQ + 4, at:at + n], mp[2][:, 0:4 * n].rearrange("p (h t) -> p h t", t=n), ACT.Copy),
                     bank[2].empty["act"])

            def a_finish(l):
                step(fn(acols[:, AO:AO + 4, :], acols[:, AO:AO + 4, :], ACT.Tanh, scale=0.5), flow("a_o_tanh"))
                flow("a_den_ok").wait_next(act, "act")
                step(fn(a_den[:], a_den[:], ACT.Square), flow("a_den_sq"))
                for h in range(4):
                    if h >= 2:
                        bank[2 * (h % 2) + 1].wait_emptied(act, ("a_norm", l, h - 2))
                    step(fn((r_li, r_wk)[h % 2][:], acols[:, AQ + h, :], ACT.Square), flow("a_h_sq"))
                for h in range(4):
                    bank[2 * (h % 2) + 1].wait_emptied(act, ("a_norm", l, h))
                    step(fn(a_den[:, h, :], a_den[:, h, :], ACT.Ln, scale=1.0 / P))
                    step(fn(a_den[:, h, :], a_den[:, h, :], ACT.Exp, scale=-0.5), flow("a_r"))

            def b_values(l):
                flow("a_h").wait_next(act, "act")
                bank[0].read(act, "act")
                step(fn(va[:, 0:4, :], mp[0][:].rearrange("p (j d) -> p j d", d=P), ACT.Copy), bank[0].empty["act"])
                bank[2].read(act, "act")
                step(fn(kout[:, 0, :], mp[2][:, 0:P], ACT.Copy))
                step(fn(kout[0:TS, 1, :], mp[2][0:TS, P:2 * P], ACT.Copy))
                step(fn(va[0:TS, 4, :], mp[2][0:TS, 2 * P:3 * P], ACT.Copy), bank[2].empty["act"])

            def b_chunk(l, c):
                sample = c == 8
                n, nt, at = (TS, 2, TP) if sample else (CHUNK, 4, CHUNK * c)
                nk = KEYS_S if sample else CHUNK * min(3, c + 1)
                flow("b_max").wait_next(act, "act")
                for t in range(nt):
                    step(fn(sc[:, t, 0:nk], sc[:, t, 0:nk], ACT.Exp, bias=stats[:, 8 + t:9 + t],
                            accum_out=stats[:, 24 + t:25 + t]))
                step(fn(stats[:, 16:16 + nt], stats[:, 16:16 + nt], ACT.Exp), flow("b_exp"))
                bank[2].read(act, "act")
                step(fn(pt0[0:min(nk, P), 0:nt * P], mp[2][0:min(nk, P), 0:nt * P], ACT.Copy), bank[2].empty["act"])
                bank[0].read(act, "act")
                step(fn(bh[:, :, at:at + n], mp[0][:, 0:4 * n].rearrange("p (m t) -> p m t", t=n), ACT.Copy),
                     bank[0].empty["act"])

            def gate(s):
                l, b, m = s[1:]
                i = GATES.index((b, m))
                if i == 0:
                    act.wait_ge(flow("b_stored").sem, 96 * (l + 1))
                if i >= 2:
                    act.wait_ge(emptied["dve"].sem, tiles[("branch", l) + GATES[i - 2]][2])
                pair = product_done(s)
                step(fn(halves(gate_t[:, i % 2, :]), pair_view(pair), ACT.Tanh, scale=0.5), emptied["act"])

            def merge_split(l):
                for k in range(KD):
                    flow("merged").wait_next(act, "act")
                    xh_ready.inc(fn(xh[:, k, :], merged[:, k, :], ACT.Copy, scale=0.5))

            split_units = [s for s in units if s in split_no]
            split_high(0)
            for s in plan:
                kind = s[0]
                if s in split_no:
                    split_high(split_no[s] + 1)
                if kind == "load_x":
                    load_x()
                elif kind == "norm_pre":
                    norm_pre(*s[1:])
                elif kind == "norm_post":
                    norm_post(*s[1:])
                elif kind == "cols_c":
                    cols_c(s)
                elif kind == "cols_a":
                    cols_a(s)
                elif kind == "cols_b":
                    cols_b(s)
                elif kind == "gate":
                    gate(s)
                elif kind == "mix":
                    pair = product_done(s)
                    step(fn(halves(mixed[:, s[2], :]), pair_view(pair), ACT.Copy), emptied["act"])
                elif kind == "ffn_gate":
                    pair = product_done(s)
                    if s[2] >= 2:
                        act.wait_ge(flow("hidden").sem, KF * s[1] + s[2] - 1)
                    step(fn(halves(ffn_t[:, s[2] % 2, :]), pair_view(pair), ACT.Tanh, scale=0.5), flow("ffn_tanh"))
                elif kind == "ffn_up":
                    act.wait_ge(emptied["dve"].sem, tiles[s][2])
                    step(fn(hid_h[:, s[2], :], ffn_p[:, s[2] % 2, :], ACT.Copy), flow("hidden_high"))
                elif kind == "ffn_out":
                    if s[3] == 2:
                        pair = product_done(s)
                        step(fn(halves(ffn_y[:, s[2], :]), pair_view(pair), ACT.Copy), emptied["act"])
                elif kind == "store_y":
                    for t in range(5):
                        n, at = group(t)
                        b = bank[2 * (t % 2) + 1]
                        b.read(act, "act")
                        step(fn(y_tok[0:n, t, 512:1024], b.t[0:n, :], ACT.Copy), b.empty["act"])
                elif kind == "branch":
                    pass
                else:
                    {"c_shift_out": c_shift_out, "c_prep": c_prep, "c_gram": c_gram, "a_rows_exp": a_rows_exp,
                     "a_chunk_out": a_chunk_out, "c_level": c_level, "c_chain": c_chain,
                     "c_finish": c_finish, "a_rows": a_rows, "a_chunk": a_chunk, "a_finish": a_finish,
                     "b_values": b_values, "b_chunk": b_chunk, "merge_split": merge_split}[kind](*s[1:])

        @block.vector
        def _(dve):
            step = Lane(dve, chains["dve"])
            tt, stt, ts = dve.tensor_tensor, dve.scalar_tensor_tensor, dve.tensor_scalar
            MUL, ADD, SUB, MAX, MIN = ALU.mult, ALU.add, ALU.subtract, ALU.max, ALU.min

            def product_done(s):
                dve.wait_ge(products.sem, unit_no[s] + 1)
                return tiles[s][0]

            def load_x():
                dve.wait_ge(ld_const.sem, 32)
                bank[1].read(dve, "dve")
                step(dve.tensor_copy(bias_line[:], mp[1][0:8, 0:256]), bank[1].empty["dve"])
                step(dve.tensor_copy(stats[0:1, 61:62], bias_line[0:1, 0:1]), flow("bias_line"))
                for k in range(0, KD, 2):
                    bank[2].read(dve, "dve")
                    step(dve.tensor_copy(x[:, k, 0:TP], mp[2][:]), bank[2].empty["dve"])
                    step(dve.tensor_copy(stats[0:1, 61:62], stats[0:1, 61:62]), flow("x_even"))
                step(dve.memset(stats[:], 0.0))

            def norm_pre(l, w_):
                g0 = PARAM_AT["norm_mix_pre" if w_ == 0 else "norm_ffn_pre"]
                flow("rstd").wait_next(dve, "dve")
                if w_ == 0:
                    step(dve.memset(craw[:, :, 0:1], 0.0))
                if l == 0 and w_ == 0:
                    at = PARAM_AT["c_w0"]
                    step(ts(half_w0a0[:], prm[:, :, at:at + 8], 0.5, None, MUL))

                def low(k):
                    xh_ready.wait_next(dve, "dve")
                    step(tt(xl[:, k, :], squares[:, k, :], xh[:, k, :].bitcast(F32), SUB), xl_ready)

                for k in range(KD):
                    step(stt(out=squares[:, k, :], in0=x[:, k, :], scalar=prm[:, l, g0 + k:g0 + k + 1], in1=rstd[:],
                             op0=MUL, op1=MUL), xn_part)
                    if k:
                        low(k - 1)
                low(KD - 1)

            def norm_post(l, w_):
                g0 = PARAM_AT["norm_mix_post" if w_ == 1 else "norm_ffn_post"]
                src, tmp = (mixed, squares) if w_ == 1 else (ffn_y, sq2)
                flow("rstd").wait_next(dve, "dve")
                if w_ == 1:
                    dve.wait_ge(flow("x_back").sem, 16 * (l + 1))
                for k in range(KD):
                    step(stt(out=tmp[:, k, :], in0=src[:, k, :], scalar=prm[:, l, g0 + k:g0 + k + 1], in1=rstd[:],
                             op0=MUL, op1=MUL))
                    step(tt(x[:, k, :], x[:, k, :], tmp[:, k, :], ADD), flow("x_new"))

            def cols_c(s):
                l, j = s[1:]
                flow("c_raw").wait_next(dve, "dve")
                raw, d = craw[:, j % 2, :], cc[:, j, :]
                step(dve.tensor_copy(view(shift_out[:], [[CT, 2]], j), view(raw, [[TS + 1, 2]], TP)),
                     flow("shift_cols") if j == CT - 1 else None)
                step(tt(d, raw[:, 0:CW], raw[:, 1:CW + 1], SUB))
                mu = PARAM_AT["c_mu"] + j
                step(stt(out=cc[:, j, :], in0=d, scalar=prm[:, l, mu:mu + 1], in1=raw[:, 1:CW + 1], op0=MUL, op1=ADD),
                     flow("c_col"))

            C1 = -0.5 * math.exp(-0.5)

            def c_prep(l, g):
                n, at, nch, L = c_group(g)
                r4 = cc[:, 0:4, at:at + n]
                k4 = cc[:, 4:8, at:at + n]
                v4 = cc[:, 8:12, at:at + n]
                f4 = lambda t: t[:, 0:4 * n]
                if g == 0:
                    dve.wait_ge(flow("a_state_stored").sem, 96 * (l + 1))
                    step(dve.memset(diag[:], 0.0))
                step(tt(gv(kk, n), k4, view(prm[:, l, PARAM_AT["c_k_k"]:], [[1, 4], [0, n]]), MUL),
                     flow("c_kk_raw"))
                flow("c_sig_raw").wait_next(dve, "dve")
                step(ts(sig_g[:, 0:n], sig_g[:, 0:n], 0.5, 0.5, MUL, ADD), flow("c_gate_in"))
                bank[0].wait_emptied(dve, ("c_lw", l, g))
                step(ts(f4(decay_log), f4(decay_log), C1, C1, MUL, ADD))
                mask = C("scan64") if L == 64 else C("scan32")
                step(dve.tensor_tensor_scan(f4(cum), mask[:, 0:4 * n], f4(decay_log), 0.0, MUL, ADD))
                step(tt(f4(decay_log), f4(cum), f4(decay_log), SUB), flow("c_cum"))
                bank[1].wait_emptied(dve, ("c_la", l, g))
                step(ts(f4(in_rate), f4(in_rate), 0.5, 0.5, MUL, ADD))
                bank[2].read(dve, "dve")
                step(ts(f4(kprime), mp[2][:, 0:4 * n], 1e-24, None, MAX), bank[2].empty["dve"])
                step(dve.tensor_copy(stats[0:1, 61:62], stats[0:1, 61:62]), flow("c_ss"))
                flow("c_rn").wait_next(dve, "dve")
                step(tt(f4(kk), f4(kk), f4(kprime), MUL))
                step(stt(out=gv(kprime, n), in0=gv(in_rate, n), scalar=-1.0, in1=view(prm[:, l, PARAM_AT["c_k_a"]:], [[1, 4], [0, n]]),
                         op0=ADD, op1=MUL))
                step(stt(out=gv(kprime, n), in0=gv(kprime, n), scalar=1.0, in1=k4, op0=ADD, op1=MUL))
                step(tt(f4(in_rate), f4(kk), f4(in_rate), MUL))
                step(tt(gv(scratch, n), r4, view(prm[:, l, PARAM_AT["c_r_k"]:], [[1, 4], [0, n]]), MUL))
                step(tt(f4(scratch), f4(scratch), f4(kprime), MUL), flow("c_rk"))
                flow("c_exps").wait_next(dve, "dve")
                en = rhs_z[:, :, :].rearrange("p a b -> p (a b)")[:, 0:4 * n]
                step(tt(kap_r[:, :, 0, 0:n], gv(kk, n), gv(decay_log, n), MUL))
                step(tt(kap_r[:, :, 1, 0:n], r4, gv(cum, n), MUL))
                step(tt(f4(in_rate), f4(in_rate), en, MUL))
                step(tt(f4(kprime), f4(kprime), en, MUL), flow("c_scaled"))
                bank[3].read(dve, "dve")
                step(tt(v4, gv(mp[3], n), v4, MUL), bank[3].empty["dve"])

            def level_mask(k, n, L):
                return view(C("levels")[0:n], [[0, 8], [1, L]], 64 * k)

            def c_gram(l, g):
                n, at, nch, L = c_group(g)
                masks = view(C("lt_le")[0:n], [[0, 4], [64, 2], [1, L]])

                def masked(b, dst, h0):
                    bank[b].read(dve, "dve")
                    step(tt(dst[0:n, h0:h0 + 4, :, 0:L], mp[b][0:n, 0:8 * L].rearrange("p (h u t) -> p h u t", u=2, t=L),
                            masks, MUL), bank[b].empty["dve"])

                masked(0, a_rb, 0)
                masked(3, a_rb, 4)
                step(dve.tensor_copy(stats[0:1, 61:62], stats[0:1, 61:62]), flow("c_a_masked"))
                bank[1].read(dve, "dve")
                i_, it_ = inv[0:n, :, 0:L], invT[0:n, :, 0:L]
                eye = view(C("eye64")[0:n], [[0, 8], [1, L]])
                step(tt(it_, a_rb[0:n, :, 0, 0:L], view(C("level0_up")[0:n], [[0, 8], [1, L]]), MUL))
                step(tt(it_, eye, it_, SUB), flow("c_invT0"))
                step(tt(i_, mp[1][0:n, 0:8 * L].rearrange("p (h t) -> p h t", t=L),
                        view(C("level0_neg")[0:n], [[0, 8], [1, L]]), MUL), bank[1].empty["dve"])
                step(tt(i_, i_, eye, ADD), flow("c_inv0"))
                masked(2, b_rk, 0)
                masked(0, b_rk, 4)

            def c_level(l, g, k):
                n, at, nch, L = c_group(g)
                by_head = lambda b: mp[b][0:n, 0:8 * L].rearrange("p (h t) -> p h t", t=L)
                i_, it_ = inv[0:n, :, 0:L], invT[0:n, :, 0:L]
                bank[1].read(dve, "dve")
                step(tt(w_lev[0:n, :, 0:L], by_head(1), level_mask(k, n, L), MUL), bank[1].empty["dve"])
                if k < (5 if L == 64 else 4):
                    bank[3].read(dve, "dve")
                    step(tt(i_, i_, by_head(3), SUB), bank[3].empty["dve"])
                bank[2].read(dve, "dve")
                step(tt(it_, it_, by_head(2), SUB), bank[2].empty["dve"])

            def c_chain(l, g, c):
                n, at, nch, L = c_group(g)
                if g == 0 and c == 0:
                    step(dve.memset(state[:, 0], 0.0), flow("c_state"))
                if g == 4:
                    bank[0].read(dve, "dve")
                    step(dve.tensor_copy(state[:, 0], mp[0][:, 0:256].rearrange("p (f i) -> p f i", i=64)), bank[0].empty["dve"])
                    step(dve.tensor_copy(stats[0:1, 61:62], stats[0:1, 61:62]), flow("c_state"))
                r = slice(64 * c, 64 * c + L)
                cur = (2 * g + c) % 2
                bank[0].read(dve, "dve")
                step(dve.tensor_copy(rhs_z[r], mp[0][r, :].rearrange("p (h i) -> p h i", i=64)), bank[0].empty["dve"])
                bank[1].read(dve, "dve")
                step(ts(neg_z[r], mp[1][r, :].rearrange("p (h i) -> p h i", i=64), -1.0, None, MUL), bank[1].empty["dve"])
                bank[2].read(dve, "dve")
                nxt = state[:, 1 - cur]
                step(tt(nxt, state[:, cur], mp[2][:, 0:256].rearrange("p (f i) -> p f i", i=64), ADD), bank[2].empty["dve"])
                step(tt(nxt, nxt, view(cum[:], [[n, 4], [0, 64]], c * L + L - 1), MUL), flow("c_state"))

            def c_finish(l, g):
                n, at, nch, L = c_group(g)
                f4 = lambda t: t[:, 0:4 * n]
                y4, v4 = cc[:, 0:4, at:at + n], cc[:, 8:12, at:at + n]
                par = lambda name: view(prm[:, l, PARAM_AT[name]:], [[1, 4], [0, n]])
                bank[0].read(dve, "dve")
                step(stt(out=gv(kk, n), in0=gv(mp[0], n), scalar=-1.0 / 64, in1=y4, op0=MUL, op1=ADD), bank[0].empty["dve"])
                step(dve.tensor_copy(stats[0:1, 61:62], stats[0:1, 61:62]), flow("c_dev"))
                flow("c_gn_r").wait_next(dve, "dve")
                step(tt(f4(kk), f4(kk), f4(kprime), MUL))
                step(tt(gv(kk, n), gv(kk, n), par("c_gn_g"), MUL))
                step(tt(gv(kk, n), gv(kk, n), par("c_gn_b"), ADD))
                step(tt(gv(kk, n), gv(kk, n), v4, ADD))
                step(tt(y4, gv(kk, n), gv(cum, n), MUL), flow("c_h"))

            def a_rows(l):
                dve.wait_ge(emptied["act"].sem, tiles[("cols_a", l, 16)][2])
                q = slice(0, 4)
                step(dve.tensor_copy(r_lf[q, :], r_nm[32:36, :]))
                step(stt(out=r_g[q, :], in0=r_lf[q, :], scalar=-1.0, in1=r_lf[q, :], op0=MUL, op1=MIN))
                step(ts(r_in[q, :], r_lf[q, :], 0.0, None, MIN), flow("a_abs"))
                flow("a_ln").wait_next(dve, "dve")
                step(tt(r_lf[q, :], r_in[q, :], r_wk[q, :], SUB))
                step(dve.tensor_tensor_scan(r_f[q, :], C("scan_rows")[q], r_lf[q, :], 0.0, MUL, ADD))
                step(dve.tensor_tensor_scan(r_m[q, 0:TP], r_lf[q, 0:TP], r_li[q, 0:TP], 0.0, ADD, MAX))
                step(dve.tensor_tensor_scan(r_m[q, TP:T], r_lf[q, TP:T], r_li[q, TP:T], m_init[q, :], ADD, MAX))
                step(tt(r_g[q, :], r_f[q, :], r_m[q, :], SUB))
                step(tt(r_li[q, :], r_li[q, :], r_f[q, :], SUB))
                step(dve.memset(m_prev[:], 0.0))
                step(dve.tensor_copy(m_prev[q, 1:4], view(r_m[q, :], [[P, 3]], P - 1)))
                step(dve.tensor_copy(m_prev[q, 4:5], m_init[q, :]))
                step(dve.tensor_copy(g_last[q, 0:4], view(r_g[q, :], [[P, 4]], P - 1)))
                step(dve.tensor_copy(g_last[q, 4:5], r_g[q, T - 1:T]))
                for dst, src, edge in ((r_in, r_g, m_prev), (r_wk, r_li, g_last)):
                    step(tt(dst[q, 0:TP].rearrange("p (c t) -> p c t", t=P), src[q, 0:TP].rearrange("p (c t) -> p c t", t=P),
                            view(edge[q, :], [[1, 4], [0, P]]), ADD))
                    step(tt(dst[q, TP:T], src[q, TP:T], view(edge[q, :], [[0, TS]], 4), ADD))
                step(dve.memset(cn[:], 0.0))
                step(dve.memset(vo[:, :, P:256], 1.0), flow("a_exp_in"))

            def a_chunk(l, g):
                n, at = group(g)
                if g == 4:
                    dve.wait_ge(flow("a_state_in").sem, 32 * (l + 1))
                    step(dve.tensor_copy(cn[:, :, P:256], view(ncol[:], [[1, 4], [0, P]])), flow("a_n_spread"))
                flow("a_cols_t").wait_next(dve, "dve")
                bank[0].read(dve, "dve")
                for h in range(4):
                    step(stt(out=dexp[0:n, h * n:(h + 1) * n], in0=mp[0][0:n, h * n:(h + 1) * n], scalar=a_cols_t[0:n, h:h + 1],
                             in1=C("future_neg")[0:n, 0:n], op0=ADD, op1=ADD), bank[0].empty["dve"] if h == 3 else None)
                bank[1].read(dve, "dve")
                step(tt(gv(qt, n), acols[:, AQ:AQ + 4, at:at + n], gv(mp[1], n), MUL))
                step(dve.tensor_copy(a_dec[:], view(mp[1][:], [[n, 4]], n - 1)), bank[1].empty["dve"])
                flow("a_dexp").wait_next(dve, "dve")
                bank[3].read(dve, "dve")
                step(stt(out=dexp[0:n, 0:4 * n], in0=mp[3][0:n, 0:4 * n], scalar=P ** -0.5, in1=dexp[0:n, 0:4 * n],
                         op0=MUL, op1=MUL), bank[3].empty["dve"])

            def a_chunk_out(l, g):
                n, at = group(g)
                bank[3].wait_emptied(dve, ("a_den", l, g))
                bank[0].read(dve, "dve")
                step(tt(a_den[:, :, at:at + n], a_den[:, :, at:at + n], gv(mp[0], n), MAX), bank[0].empty["dve"])
                for b in range(2):
                    bank[1 + b].read(dve, "dve")
                    for i in range(2):
                        h = 2 * b + i
                        step(stt(out=cn[:, h, :], in0=cn[:, h, :], scalar=a_dec[:, h:h + 1],
                                 in1=mp[1 + b][:, i * 256:(i + 1) * 256], op0=MUL, op1=ADD),
                             bank[1 + b].empty["dve"] if i else None)

            def a_finish(l):
                step(ts(a_den[:], a_den[:], 4e12, None, MIN), flow("a_den_ok"))
                flow("a_den_sq").wait_next(dve, "dve")
                for h in range(4):
                    for b in range(2):
                        bk = 2 * (h % 2) + b
                        bank[bk].read(dve, "dve")
                        cols_ = a_den[:, h, b * HALF:(b + 1) * HALF]
                        step(stt(out=cols_, in0=cols_, scalar=P * NORM_EPS, in1=mp[bk][:, 0:HALF], op0=MUL, op1=ADD),
                             bank[bk].empty["dve"])
                flow("a_o_tanh").wait_next(dve, "dve")
                g0 = PARAM_AT["a_norm"]
                for h in range(4):
                    flow("a_r").wait_next(dve, "dve")
                    hh = acols[:, AQ + h, :]
                    step(tt(hh, hh, a_den[:, h, :], MUL))
                    step(stt(out=hh, in0=acols[:, AO + h, :], scalar=1.0, in1=hh, op0=ADD, op1=MUL))
                    step(ts(hh, hh, prm[:, l, g0 + h:g0 + h + 1], 0.5, MUL, MUL),
                         flow("a_h") if h == 3 else None)

            def b_values(l):
                bank[1].read(dve, "dve")
                step(dve.tensor_copy(vb[:, 0:3, :], mp[1][:, 0:3 * P].rearrange("p (j d) -> p j d", d=P)))
                step(dve.tensor_copy(vb[0:64, 3, :], mp[1][0:64, 3 * P:4 * P]), bank[1].empty["dve"])
                bank[3].read(dve, "dve")
                step(dve.tensor_copy(ks[:, 0:P], mp[3][:, 0:P]), bank[3].empty["dve"])
                step(dve.tensor_copy(ks[:, P:KEYS_S], bkv[:, 0, TP:T]), flow("b_values"))

            def b_chunk(l, c):
                sample = c == 8
                nt = 2 if sample else 4
                nk = KEYS_S if sample else CHUNK * min(3, c + 1)
                if l == 0 and c == 0:
                    dve.wait_ge(bias_in.sem, 16 * 16)
                per = nt // 2
                for v in range(2):
                    bank[v].read(dve, "dve")
                    bias = bias_s[:, v:v + 1, :] if sample else bias_p[:, 2 * v:2 * v + 2, KEYS - nk:KEYS]
                    step(stt(out=sc[:, per * v:per * v + per, 0:nk], in0=mp[v][:, 0:per * nk].rearrange("p (i k) -> p i k", k=nk),
                             scalar=B_HD ** -0.5, in1=bias, op0=MUL, op1=ADD), bank[v].empty["dve"])
                s0 = 4 if sample else 0
                step(dve.tensor_reduce(stats[:, 0:nt], sc[:, 0:nt, 0:nk], AX.X, MAX))
                step(tt(stats[:, 0:nt], stats[:, 0:nt], sinks[:, s0:s0 + nt], MAX))
                step(tt(stats[:, 16:16 + nt], sinks[:, s0:s0 + nt], stats[:, 0:nt], SUB))
                step(ts(stats[:, 8:8 + nt], stats[:, 0:nt], -1.0, None, MUL), flow("b_max"))
                flow("b_exp").wait_next(dve, "dve")
                step(tt(stats[:, 32:32 + nt], stats[:, 24:24 + nt], stats[:, 16:16 + nt], ADD))
                step(dve.reciprocal(stats[:, 40:40 + nt], stats[:, 32:32 + nt]))
                step(tt(sc[:, 0:nt, 0:nk], sc[:, 0:nt, 0:nk], view(stats[:], [[1, nt], [0, nk]], 40), MUL), flow("b_probs"))
                if nk > P:
                    bank[3].read(dve, "dve")
                    step(dve.tensor_copy(pt1[0:nk - P, 0:nt * P], mp[3][0:nk - P, 0:nt * P]), bank[3].empty["dve"])

            def branch(s):
                l, b, m = s[1:]
                i = GATES.index((b, m))
                if i == 0:
                    dve.wait_ge(flow("b_stored").sem, 96 * (l + 1))
                pair = product_done(s)
                dve.wait_ge(emptied["act"].sem, tiles[("gate", l, b, m)][2])
                dst = merged[:, m, :] if b == 0 else prod[:, i % 2, :]
                step(stt(out=halves(dst), in0=halves(gate_t[:, i % 2, :]), scalar=1.0, in1=pair_view(pair), op0=ADD, op1=MUL),
                     emptied["dve"])
                if b:
                    step(tt(merged[:, m, :], merged[:, m, :], dst, ADD), flow("merged") if b == 2 else None)

            def hidden_low(j):
                flow("hidden_high").wait_next(dve, "dve")
                step(tt(hid_l[:, j, :], ffn_p[:, j % 2, :], hid_h[:, j, :].bitcast(F32), SUB), flow("hidden"))

            for s in plan:
                kind = s[0]
                if kind == "load_x":
                    load_x()
                elif kind == "norm_pre":
                    norm_pre(*s[1:])
                elif kind == "norm_post":
                    norm_post(*s[1:])
                elif kind == "cols_c":
                    cols_c(s)
                elif kind == "branch":
                    branch(s)
                elif kind == "merge_split":
                    for k in range(KD):
                        xh_ready.wait_next(dve, "dve")
                        step(stt(out=xl[:, k, :], in0=merged[:, k, :], scalar=0.5, in1=xh[:, k, :].bitcast(F32),
                                 op0=MUL, op1=SUB), xl_ready)
                elif kind == "ffn_gate":
                    j = s[2]
                    pair = tiles[s][0]
                    flow("ffn_tanh").wait_next(dve, "dve")
                    step(stt(out=halves(ffn_p[:, j % 2, :]), in0=halves(ffn_t[:, j % 2, :]), scalar=1.0, in1=pair_view(pair),
                             op0=ADD, op1=MUL), emptied["dve"])
                    if j:
                        hidden_low(j - 1)
                elif kind == "ffn_up":
                    j = s[2]
                    pair = product_done(s)
                    step(stt(out=halves(ffn_p[:, j % 2, :]), in0=halves(ffn_p[:, j % 2, :]), scalar=0.5, in1=pair_view(pair),
                             op0=MUL, op1=MUL), emptied["dve"])
                    if j == KF - 1:
                        hidden_low(j)
                elif kind == "store_y":
                    for t in range(5):
                        n, at = group(t)
                        b = bank[2 * (t % 2)]
                        b.read(dve, "dve")
                        step(dve.tensor_copy(y_tok[0:n, t, 0:512], b.t[0:n, :]), b.empty["dve"])
                elif kind in ("cols_a", "cols_b", "gate", "mix", "ffn_out", "c_shift_out", "a_rows_exp"):
                    pass
                else:
                    {"c_prep": c_prep, "c_gram": c_gram, "c_level": c_level, "c_chain": c_chain, "c_finish": c_finish,
                     "a_chunk_out": a_chunk_out,
                     "a_rows": a_rows, "a_chunk": a_chunk, "a_finish": a_finish, "b_values": b_values,
                     "b_chunk": b_chunk}[kind](*s[1:])

        @block.sync
        def _(sp):
            with nc.allow_non_contiguous_dma(reason="small vectors"):
                def put(c, dst, src):
                    c.inc(sp.dma_start(dst, src), 16)

                put(ld_const, cst[:], consts_dram)
                put(ld_const, table[:], a["rel_bias"])
                for l in range(DEPTH):
                    for name, rows in PARAM_ROWS:
                        src = a[name][l] if name != "state_rwkv_shift" else a[name][l, 0, 0]
                        at = PARAM_AT[name]
                        put(ld_prm, prm_rows[at:at + rows, l, :], src.rearrange("(r c) -> r c", c=P))
                for t in range(4):
                    put(ld_x, x_tok[:, t, :], a["x_prompt"][0, t * P:(t + 1) * P, :])
                put(ld_x, x_tok[0:TS, 4, :], a["x_sample"][0])
                flow("bias_line").wait_next(sp, "sp")
                put(bias_out, bias_dram.rearrange("h (q n) -> h q n", n=256), view(bias_line[:], [[0, 64], [1, 256]]))
                bias_out.wait_next(sp, "sp", 16)
                h0 = bias_dram
                for hh in range(2):
                    for t in range(4):
                        head = 4 * (t // 2) + 2 * (t % 2) + hh
                        src = bass.AP(tensor=h0.tensor, offset=h0.offset + head * 64 * 256 + 63, ap=[[255, 64], [1, KEYS]])
                        put(bias_in, bias_p[64 * hh:64 * hh + 64, t, :], src)
                for kv in range(2):
                    for m in range(4):
                        src = bass.AP(tensor=h0.tensor, offset=h0.offset + (4 * kv + m) * 64 * 256 + 63,
                                      ap=[[255, TS], [1, KEYS_S]])
                        put(bias_in, bias_s[TS * m:TS * m + TS, kv, :], src)

                def free_raw(u):
                    s = units[u]
                    if s in split_no:
                        sp.wait_ge(low_ready.sem, split_no[s] + 1)
                    else:
                        sp.wait_ge(products.sem, unit_no[s] + 1)

                def load_unit(s):
                    u = unit_no[s]
                    if u >= NRAW:
                        free_raw(u - NRAW)
                    for (ps, ks_, ms), src in unit_parts(s):
                        put(landed[u % NRAW], wraw[ps, u % NRAW, ks_, ms], src)

                for s in units[0:NRAW - 1]:
                    load_unit(s)

                def vec(ap):
                    return ap.rearrange("(n u) -> n u", u=1)

                for s in plan:
                    kind, l = s[0], s[1] if len(s) > 1 else 0
                    if kind in GEMMS and unit_no[s] + NRAW - 1 < len(units):
                        load_unit(units[unit_no[s] + NRAW - 1])
                    if kind == "norm_pre" and s[2] == 0:
                        sp.wait_ge(sq_ready.sem, KD * (4 * l + 1))
                        put(flow("x_kept"), x_dram, x[:].rearrange("p k t -> p (k t)"))
                        if l > 0:
                            sp.wait_ge(products.sem, unit_no[("mix", l - 1, 0)] + 1)
                        put(ld_layer, lora[0:64, 0:512], a["c_w_w2"][l])
                        put(ld_layer, lora[64:128, 0:512], a["c_w_a2"][l])
                        put(ld_layer, lora[:, 512:1024], a["c_w_g2"][l])
                        sk = a["b_sinks"][l]
                        for hh in range(2):
                            src = bass.AP(tensor=sk.tensor, offset=sk.offset + hh, ap=[[0, 64], [2, 4]])
                            put(ld_layer, sinks[64 * hh:64 * hh + 64, 0:4], src)
                        for m in range(4):
                            src = bass.AP(tensor=sk.tensor, offset=sk.offset + m, ap=[[0, TS], [4, 2]])
                            put(ld_layer, sinks[TS * m:TS * m + TS, 4:6], src)
                        gb = vec(a["a_gate_bias"][l])
                        put(ld_layer, gate_bias[0:4, :], gb[0:4])
                        put(ld_layer, gate_bias[32:36, :], gb[4:8])
                        put(ld_layer, m_init[0:4, :], vec(a["state_mlstm_m"][l, 0]))
                        put(flow("c_state_in"), s_nat[:], a["state_rwkv_s"][l, 0].rearrange("(p q) i j -> (q i) p j", q=2))
                    if kind == "c_shift_out":
                        flow("shift_rows").wait_next(sp, "sp")
                        for i, name in enumerate(("p_rwkv_shift", "s_rwkv_shift")):
                            put(flow("shift_stored"), o[name][l, 0, 0].rearrange("(r c) -> r c", c=P),
                                shift_rows[CT * i:CT * i + CT, :])
                    if kind == "c_finish" and s[2] >= 3:
                        bank[3].wait_emptied(sp, ("c_state", l, s[2]))
                        put(flow("c_state_stored"),
                            o["p_rwkv_s" if s[2] == 3 else "s_rwkv_s"][l, 0].rearrange("(p q) i j -> (q i) p j", q=2), s_out[:])
                    if kind == "mix" and s[2] == 0:
                        sp.wait_ge(products.sem, unit_no[s] + 1)
                        sp.wait_ge(flow("x_kept").sem, 16 * (l + 1))
                        put(flow("x_back"), x[:].rearrange("p k t -> p (k t)"), x_dram)
                    if kind == "a_chunk_out" and s[2] in (3, 4):
                        pre = "p" if s[2] == 3 else "s"
                        bank[2].wait_emptied(sp, ("a_state", l, s[2]))
                        done = flow("a_state_stored")
                        put(done, o[f"{pre}_mlstm_c"][l, 0].rearrange("h k v -> k h v"), cn[:, :, 0:P])
                        put(done, o[f"{pre}_mlstm_n"][l, 0].rearrange("h k -> k h"), cn[:, :, P])
                        put(done, vec(o[f"{pre}_mlstm_m"][l, 0]), r_m[0:4, TP - 1:TP] if s[2] == 3 else r_m[0:4, T - 1:T])
                        if s[2] == 3:
                            sp.wait_ge(done.sem, done.value)
                            put(flow("a_state_in"), cn[:, :, 0:P], a["state_mlstm_c"][l, 0].rearrange("h k v -> k h v"))
                            put(flow("a_state_in"), ncol[:], a["state_mlstm_n"][l, 0].rearrange("h k -> k h"))
                    if kind == "a_finish":
                        flow("a_h").wait_next(sp, "sp")
                        sp.wait_ge(flow("x_kept").sem, 16 * (l + 1))
                        put(flow("b_cache_in"), kcache[:], a["cache_swa_k"][l, 0].rearrange("t v d -> t (v d)"))
                        put(flow("b_cache_in"), vcache[:], a["cache_swa_v"][l, 0].rearrange("t v d -> t (v d)"))
                    if kind == "b_values":
                        bank[2].wait_emptied(sp, ("b_values", l))
                        pk, pv, sk_, sv = (o[n][l, 0].rearrange("t v d -> t (v d)") for n in
                                           ("p_swa_k", "p_swa_v", "s_swa_k", "s_swa_v"))
                        done = flow("b_stored")
                        put(done, pk, kout[:, 0, :])
                        put(done, pv, va[:, 3, :])
                        sp.wait_ge(flow("b_cache_in").sem, 32 * (l + 1))
                        put(done, sk_[0:WINDOW - TS], kcache[TS:P, :])
                        put(done, sv[0:WINDOW - TS], vcache[TS:P, :])
                        put(done, sk_[WINDOW - TS:], kout[0:TS, 1, :])
                        put(done, sv[WINDOW - TS:], va[0:TS, 4, :])
                for t in range(5):
                    bank[2 * (t % 2)].wait_emptied(sp, ("y", t, 0))
                    bank[2 * (t % 2) + 1].wait_emptied(sp, ("y", t, 1))
                    if t < 4:
                        put(stored, o["y_prompt"][0, t * P:(t + 1) * P, :], y_tok[:, t, :])
                    else:
                        put(stored, o["y_sample"][0], y_tok[0:TS, 4, :])
                for c in (stored, flow("shift_stored"), flow("c_state_stored"), flow("a_state_stored"), flow("b_stored")):
                    sp.wait_ge(c.sem, c.value)

        @block.gpsimd
        def _(pool):
            for s in units:
                if s not in split_no:
                    continue
                n = split_no[s]
                slot = unit_no[s] % NRAW
                nk = nk_of(s)
                pool.wait_ge(high_ready.sem, n + 1)
                low_ready.inc(pool.tensor_tensor(wl[:, n % NSPLIT, 0:nk], wraw[:, slot, 0:nk],
                                                 wh[:, n % NSPLIT, 0:nk].bitcast(F32), ALU.subtract))


_INS = ['x_prompt', 'x_sample', 'cache_swa_k', 'cache_swa_v', 'state_mlstm_c', 'state_mlstm_n', 'state_mlstm_m',
        'state_rwkv_s', 'state_rwkv_shift', 'w_in', 'norm_mix_pre', 'norm_mix_post', 'norm_ffn_pre', 'norm_ffn_post',
        'a_gate_bias', 'a_norm', 'rel_bias', 'b_sinks', 'c_mu', 'c_w0', 'c_w_w2', 'c_a0', 'c_w_a2', 'c_w_g2', 'c_k_k',
        'c_k_a', 'c_r_k', 'c_gn_g', 'c_gn_b', 'w_branch_a', 'w_branch_b', 'w_branch_c', 'w_out', 'w_ffn_in', 'w_ffn_out']
_STATES = [("swa_k", (DEPTH, 1, WINDOW, 2, 64)), ("swa_v", (DEPTH, 1, WINDOW, 2, 64)), ("mlstm_c", (DEPTH, 1, 4, P, P)),
           ("mlstm_n", (DEPTH, 1, 4, P)), ("mlstm_m", (DEPTH, 1, 4)), ("rwkv_s", (DEPTH, 1, 8, 64, 64)),
           ("rwkv_shift", (DEPTH, 1, 1, C_COLS))]
_OUTS = ([("y_prompt", (1, TP, D)), ("y_sample", (1, TS, D))] + [("p_" + n, s) for n, s in _STATES]
         + [("s_" + n, s) for n, s in _STATES])


def kernel(**inputs):
    import concourse.bacc as _bacc
    from concourse.bass_utils import run_bass_kernel_spmd as _run

    nc = _bacc.Bacc("TRN2", target_bir_lowering=False, num_devices=1)
    arrays, a, o = {}, {}, {}
    for name in _INS:
        v = np.ascontiguousarray(inputs[name])
        arrays[f"in_{name}"] = v
        a[name] = nc.dram_tensor(f"in_{name}", v.shape, mybir.dt.from_np(v.dtype), kind="ExternalInput").ap()
    for name, shape in _OUTS:
        o[name] = nc.dram_tensor(f"out_{name}", shape, mybir.dt.float32, kind="ExternalOutput").ap()
    build(nc, a, o)
    r = _run(nc, [arrays], core_ids=[0])
    return tuple(r.results[0][f"out_{name}"] for name, _ in _OUTS)
```

```python
import math
from contextlib import ExitStack

import numpy as np

import concourse.bass as bass
from concourse import mybir

P = 128
D = 1024
TP, TS = 512, 32
T = TP + TS
DEPTH = 2
KD = D // P
A_H, A_W = 4, 512
A_COLS = 4 * A_W + 2 * A_H
B_W, B_HD = 512, 64
B_COLS = 768
C_W, C_H = 512, 8
C_COLS = 1792
CT = C_COLS // P
OFF_B = A_COLS
OFF_C = A_COLS + B_COLS
OFF_G = OFF_C + C_COLS
D_FF = 2816
KF = D_FF // P
WINDOW = 128
CHUNK = 64
NORM_EPS, GN_EPS = 1e-6, 64e-5
HALF = T // 2
SPLIT_C = 256
CW = TP + 1 + TS
Y_CUT = 273
KEYS = WINDOW + CHUNK
KEYS_S = WINDOW + TS
NRAW, NSPLIT = 3, 2
GROUPS = 5
PARAM_ROWS = [("norm_mix_pre", KD), ("norm_mix_post", KD), ("norm_ffn_pre", KD), ("norm_ffn_post", KD),
              ("c_mu", CT), ("state_rwkv_shift", CT), ("a_norm", 4), ("c_w0", 4), ("c_a0", 4), ("c_k_k", 4),
              ("c_k_a", 4), ("c_r_k", 4), ("c_gn_g", 4), ("c_gn_b", 4)]
PARAM_AT, _n = {}, 0
for _name, _rows in PARAM_ROWS:
    PARAM_AT[_name] = _n
    _n += _rows
NPARAM = _n


def group(g):
    return (P, P * g) if g < 4 else (TS, TP)


def shape_constants():
    c = {}
    c["ident"] = np.eye(P)
    c["ones"] = np.ones((P, P))
    c["headones"] = np.kron(np.eye(2), np.ones((64, 64)))
    s = np.arange(64)[:, None]
    t = np.arange(64)[None, :]
    both = lambda m: np.tile(m.astype(np.float64), (2, 1))
    c["lt_le"] = np.concatenate([both(s < t), both(s <= t)], axis=1)
    level = []
    for b in (1, 2, 4, 8, 16, 32):
        same = (s // (2 * b)) == (t // (2 * b))
        level.append(both(same & (s % (2 * b) >= b) & (t % (2 * b) < b)))
    c["levels"] = np.concatenate(level, axis=1)
    c["level0_up"] = both((s // 2 == t // 2) & (s % 2 == 0) & (t % 2 == 1))
    c["level0_neg"] = -both((s // 2 == t // 2) & (s % 2 == 1) & (t % 2 == 0))
    c["eye64"] = both(s == t)
    a = np.arange(P)
    c["future_neg"] = np.where(a[:, None] > a[None, :], -1e30, 0.0)
    m = np.ones((P, 512))
    m[:, ::64] = 0
    c["scan64"] = m
    sel = np.zeros((P, 4 * P))
    for h in range(4):
        sel[h, h * P:(h + 1) * P] = 1
    c["sel"] = sel
    m = np.ones((P, T))
    m[:, 0:TP:P] = 0
    m[:, TP] = 0
    c["scan_rows"] = m
    rel = np.arange(256) - 63 - WINDOW
    half, exact = 16, 8
    n = np.abs(rel)
    far = exact + (np.log(np.maximum(n, 1).astype(np.float32) / np.float32(exact)) / math.log(256 / exact)
                   * (half - exact)).astype(np.int32)
    bucket = np.where(rel > 0, half, 0) + np.where(n < exact, n, np.minimum(far, half - 1))
    hot = np.zeros((P, 256))
    hot[np.clip(bucket, 0, 31), np.arange(256)] = 1
    c["bucket_hot"] = hot
    v = np.zeros((P, 8))
    v[:, 0] = NORM_EPS
    v[:, 1] = GN_EPS
    v[:, 2] = 10 * math.log(2)
    v[:, 3] = 1.0
    c["scalars"] = v
    at, cols, parts = {}, 0, []
    for k, x in c.items():
        at[k] = (cols, x.shape[1])
        cols += x.shape[1]
        parts.append(x)
    return at, np.concatenate(parts, axis=1).astype(np.float32)


class Count:

    def __init__(self, sem):
        self.sem, self.value, self.seen = sem, 0, {}

    def inc(self, ins, n=1):
        ins.then_inc(self.sem, n)
        self.value += n

    def wait_next(self, eng, who, n=1):
        self.seen[who] = self.seen.get(who, 0) + n
        eng.wait_ge(self.sem, self.seen[who])


class Lane:

    def __init__(self, eng, chain):
        self.eng, self.chain = eng, chain

    def __call__(self, ins, count=None):
        c = count or self.chain
        c.inc(ins)
        self.eng.wait_ge(c.sem, c.value)


class Bank:

    def __init__(self, name, tensor, sem):
        self.t = tensor
        self.full = {r: Count(sem(f"{name}_full_for_{r}")) for r in ("act", "dve")}
        self.empty = {r: Count(sem(f"{name}_emptied_by_{r}")) for r in ("act", "dve")}
        self.last = None
        self.marks = {}

    def claim(self, pe):
        if self.last:
            pe.wait_ge(self.empty[self.last].sem, self.full[self.last].value)

    def filled(self, ins, reader, mark=None):
        self.full[reader].inc(ins)
        self.last = reader
        self.marks[mark] = (self.empty[reader].sem, self.full[reader].value)

    def read(self, eng, reader):
        self.full[reader].wait_next(eng, reader)

    def wait_emptied(self, eng, mark):
        eng.wait_ge(*self.marks[mark])


WEIGHT = {"c_prep": 1.0, "c_keys": 1.0, "c_scaled": 0.3, "c_scale": 1.0, "c_gram": 0.7, "c_level": 0.3, "c_chain": 0.5,
          "c_state_out": 0.0, "a_chunk": 0.65, "a_chunk_out": 0.2, "a_finish": 1.0, "a_norm": 1.0, "b_values": 0.1,
          "b_chunk": 0.9}


def weave(items, fillers):
    total = sum(WEIGHT.get(i[0], 1.0) for i in items)
    out, used, at = [], 0, 0.0
    for item in items:
        out.append(item)
        at += WEIGHT.get(item[0], 1.0)
        upto = min(len(fillers), int(at * len(fillers) / total + 1e-6))
        out += fillers[used:upto]
        used = upto
    return out


def gate_order():
    return [(b, m) for m in range(KD) for b in range(2)] + [(2, m) for m in range(KD)]


GATES = gate_order()


def make_plan():
    plan = [("load_x",)]
    for l in range(DEPTH):
        plan += [("norm_pre", l, 0)]
        plan += [("cols_a", l, j) for j in (0, 1, 2, 16)] + [("a_rows", l), ("cols_a", l, 3), ("cols_a", l, 4)]
        plan += [("a_rows_exp", l)] + [("cols_a", l, j) for j in range(5, 16)]
        plan += [("cols_b", l, j) for j in range(6)]
        ab = []
        for g in range(GROUPS):
            ab += [("a_chunk", l, g), ("a_chunk_out", l, g)]
        ab += [("a_finish", l), ("a_norm", l), ("b_values", l)] + [("b_chunk", l, c) for c in range(9)]
        plan += weave(ab, [("cols_c", l, j) for j in range(CT)])
        plan += [("c_shift_out", l)]
        c = []
        for g in range(GROUPS):
            c += [("c_prep", l, g), ("c_keys", l, g), ("c_scale", l, g), ("c_scaled", l, g), ("c_gram", l, g)]
            c += [("c_level", l, g, k) for k in range(1, 6 if g < 4 else 5)]
            c += [("c_chain", l, g, k) for k in range(2 if g < 4 else 1)]
            c += [("c_state_out", l, g)] if g >= 3 else []
        products = []
        for b, m in GATES[:2 * KD]:
            products += [("gate", l, b, m), ("branch", l, b, m)]
        plan += weave(c, products)
        finish = [("c_gate_in", l)] + [("c_variance", l, f) for f in range(4)]
        finish += [("c_rsqrt", l)] + [("c_finish", l, f) for f in range(4)]
        plan += weave(finish, [("gate", l, 2, m) for m in range(KD)])
        plan += [("branch", l, 2, m) for m in range(KD)]
        plan += [("merge_split", l)]
        plan += [("mix", l, m) for m in range(KD)]
        plan += [("norm_post", l, 1)]
        plan += [("norm_pre", l, 2)]
        for j in range(KF):
            plan += [("ffn_gate", l, j), ("ffn_up", l, j)]
        plan += [("ffn_out", l, m, q) for m in range(KD) for q in range(3)]
        plan += [("norm_post", l, 3)]
    plan += [("store_y",)]
    return plan


GEMMS = {"cols_c": "act", "cols_a": "act", "cols_b": "act", "gate": "act", "branch": "dve", "mix": "act",
         "ffn_gate": "dve", "ffn_up": "dve", "ffn_out": "act"}
UNSPLIT = {"branch"}


def view(ap, free, start=0):
    return bass.AP(tensor=ap.tensor, offset=ap.offset + start, ap=[list(ap.ap[0])] + [list(x) for x in free])


def build(nc, a, o):
    F32, F32R = mybir.dt.float32, mybir.dt.float32r
    ALU, ACT, AX = mybir.AluOpType, mybir.ActivationFunctionType, mybir.AxisListType
    plan = make_plan()
    const_at, const_np = shape_constants()
    NCONST = const_np.shape[1]
    consts_dram = nc.inline_tensor(const_np, name="shape_constants").ap()
    bias_dram = nc.dram_tensor("bias_skewed", (8, 64 * 256), F32, kind="Internal").ap()

    x_dram = nc.dram_tensor("x_kept", (P, KD * T), F32, kind="Internal").ap()

    base = [(nc.sbuf_base + 63) // 64 * 64]
    limit = nc.sbuf_usable_end

    def region(nbytes):
        at = base[0]
        base[0] += (nbytes + 63) // 64 * 64
        assert base[0] <= limit, (base[0], limit)
        return at

    def place(name, shape, at, dt=F32):
        n = 4 * int(np.prod(shape[1:]))
        assert at + n <= limit, (name, at + n, limit)
        return nc.alloc_sbuf_tensor_at(name, shape, dt, offset=at)

    def fixed(name, shape, dt=F32):
        return place(name, shape, region(4 * int(np.prod(shape[1:]))), dt)

    cst = fixed("consts", [P, NCONST])
    prm = fixed("params", [P, DEPTH, NPARAM])
    half_w0a0 = fixed("half_w0a0", [P, DEPTH, 8])
    bias_p = fixed("bias_prompt", [P, 4, KEYS])
    bias_s = fixed("bias_sample", [P, 2, KEYS_S])
    lora = fixed("lora", [P, 1024])
    sinks = fixed("sinks", [P, 8])
    gate_bias = fixed("gate_bias", [P, 1])
    m_init = fixed("m_init", [P, 1])
    shift_out = fixed("shift_out", [P, 2 * CT])
    stats = fixed("stats", [P, 64])
    s_nat = fixed("c_state_natural", [P, 4, 64])
    s_out = fixed("c_state_out", [P, 4, 64])
    shift_rows = fixed("shift_rows", [2 * CT, P])
    x_at = region(4 * KD * T)
    x = place("x", [P, KD, T], x_at)
    xnh_at = region(2 * 4 * KD * T)
    xh = place("xn_high", [P, KD, T], xnh_at, F32R)
    xl = place("xn_low", [P, KD, T], xnh_at + 4 * KD * T, F32R)
    wraw = fixed("w_raw", [P, NRAW, 8, P])
    wh = fixed("w_high", [P, NSPLIT, 8, P], F32R)
    wl = fixed("w_low", [P, NSPLIT, 8, P], F32R)
    arena = base[0]
    cc_at = arena
    craw_at = (cc_at + 4 * CT * CW + 63) // 64 * 64
    a_work = (craw_at + 4 * 2 * (CW + 1) + 63) // 64 * 64
    acols_at = (limit - 4 * 16 * T) // 64 * 64
    cc = place("c_cols", [P, CT, CW], cc_at)
    craw = place("c_raw", [P, 2, CW + 1], craw_at)
    acols = place("a_cols", [P, 16, T], acols_at)
    AK, AV, AO, AQ = 0, 4, 8, 12

    def worker(start):
        at = [start]

        def w(name, shape, dt=F32):
            t = place(name, shape, at[0], dt)
            at[0] += (4 * int(np.prod(shape[1:])) + 31) // 32 * 32
            return t
        w.end = lambda: at[0]
        return w

    w = worker(x_at)
    bq = w("b_queries", [P, 4 * T])
    bkv = w("b_keys_values", [P, 2, T])
    sc = w("b_scores", [P, 4, KEYS])
    ks = w("b_keys_sample", [P, KEYS_S])
    kcache = w("b_k_cache", [P, P])
    merged = place("merged", [P, KD, T], x_at)
    w = worker(craw_at)
    decay_log, in_rate, kk, scratch, kprime, cum = (w(n, [P, 512]) for n in (
        "c_decay_log", "c_in_rate", "c_kk", "c_scratch", "c_kprime", "c_cum"))
    kap_r = w("c_kappa_r", [P, 4, 2, P])
    tanh_w = w("c_tanh_w", [64, P])
    vt, kt, bt = (w(n, [P, 512]) for n in ("c_v_tokens", "c_k_tokens", "c_b_tokens"))
    a_rb_at = w.end()
    a_rb = w("c_a_rb", [P, 8, 2, 64])
    b_rk = w("c_b_rk", [P, 8, 2, 64])
    inv, invT, w_lev, neg_z = (t[:].rearrange("p (h t) -> p h t", t=64) for t in (scratch, kk, in_rate, kprime))
    rhs_z = w("c_rhs_z", [P, 8, 64])
    state = w("c_state", [P, 2, 4, P])
    diag = w("c_block_diagonal", [P, 3, 8, P])
    a_bd, w_bd, invT_bd = diag[:, 0], diag[:, 1], diag[:, 2]
    bh_at = w.end()
    bh = w("b_heads", [P, 4, T])
    rest = (w.end() + 63) // 64 * 64
    w = worker(rest)
    pt0 = w("b_probsT_first", [P, 512])
    pt1 = w("b_probsT_second", [P, 512])
    va = w("b_values_even", [P, 5, P])
    vb = w("b_values_odd", [P, 4, P])
    assert w.end() <= acols_at + 4 * AQ * T
    w = worker(rest)
    gate_t = w("gate_tanh", [P, 2, T])
    prod = w("gate_product", [P, 2, T])
    assert w.end() <= acols_at + 4 * AQ * T
    w = worker(craw_at)
    y_dev = w("c_y_deviation", [P, 4, CW])
    y_rn = w("c_y_rsqrt", [P, 4, CW])
    y_sq = w("c_y_squares", [P, 2, CW])
    assert w.end() <= a_rb_at
    gate_c = place("gate_tanh_c", [P, KD, T], a_rb_at)
    assert a_rb_at + 4 * KD * T <= bh_at
    w = worker(a_work)
    r_li, r_m, r_g, r_in, r_nm, r_wk = (w(n, [P, T]) for n in ("a_li", "a_m", "a_g", "a_inter", "a_negm", "a_wk"))
    a_den = w("a_den", [P, 4, T])
    r_lf, r_f = a_den[:, 0, :], a_den[:, 1, :]
    vcache = place("b_v_cache", [P, P], w.end())
    kout = place("b_k_out", [P, 2, P], w.end() + 4 * P)
    dexp, qt, kw = (w(n, [P, 512]) for n in ("a_dexp", "a_q_inter", "a_k_weighted"))
    vo = w("a_values_ones", [P, 4, 256])
    cn = w("a_state", [P, 4, 256])
    a_cols_t = w("a_cols_tokens", [P, 8])
    a_dec = w("a_decay", [P, 4])
    m_prev = w("a_m_prev", [P, 8])
    g_last = w("a_g_last", [P, 8])
    ncol = w("a_n_col", [P, 4])
    assert w.end() <= acols_at
    squares = place("squares", [P, KD, T], acols_at)
    mixed = place("mixed", [P, KD, T], acols_at + 4 * KD * T)
    rstd = place("rstd", [P, T], a_work)
    w = worker(arena)
    hid_h = w("hidden_high", [P, KF, T], F32R)
    hid_l = w("hidden_low", [P, KF, T], F32R)
    ffn_t = w("ffn_tanh", [P, 2, T])
    ffn_p = w("ffn_product", [P, 2, T])
    ffn_y = place("ffn_y", [P, KD, T], xnh_at)
    sq2 = place("squares_ffn", [P, KD, T], xnh_at + 4 * KD * T)
    w = worker(arena)
    x_tok = w("x_tokens", [P, 5, D])
    prm_rows = w("param_rows", [P, DEPTH, P])
    bias_line = w("bias_line", [8, 256])
    table = w("bias_table", [32, 8])
    y_tok = place("y_tokens", [P, 5, D], arena)

    ctx = ExitStack()
    with ctx:
        gp = ctx.enter_context(nc.psum_tensor("psum_products", [P, 4, 512], F32))
        mp = [ctx.enter_context(nc.psum_tensor(f"psum_mixer{i}", [P, 512], F32)) for i in range(4)]
        nsem = [0]

        def sem(name):
            nsem[0] += 1
            return ctx.enter_context(nc.semaphore(name))

        def count(name):
            return Count(sem(name))

        def C(name, lo=0, n=None):
            at, width = const_at[name]
            return cst[:, at + lo:at + (width if n is None else lo + n)]

        bank = [Bank(f"bank{i}", mp[i], sem) for i in range(4)]
        landed = [count(f"weights_landed{i}") for i in range(NRAW)]
        high_ready, low_ready = count("w_high_ready"), count("w_low_ready")
        products = count("products_done")
        emptied = {r: count(f"products_emptied_by_{r}") for r in ("act", "dve")}
        xn_part, xh_ready, xl_ready = count("xn_ready"), count("xn_high_ready"), count("xn_low_ready")
        xl_odd = count("xn_low_odd_ready")
        sq_ready = count("squares_ready")
        chains = {e: count(f"{e}_steps") for e in ("act", "dve", "pe", "pool")}
        ld_const, ld_x, ld_prm, ld_layer = (count(n) for n in ("consts_in", "x_in", "params_in", "layer_in"))
        bias_out, bias_in = count("bias_written"), count("bias_read")
        stored = count("outputs_stored")
        flows = {}

        def flow(name):
            if name not in flows:
                flows[name] = count(name)
            return flows[name]

        units = [s for s in plan if s[0] in GEMMS]
        unit_no = {s: i for i, s in enumerate(units)}
        split_no, unsplit_no, n_split, n_unsplit = {}, {}, 0, 0
        for s in units:
            if s[0] in UNSPLIT:
                unsplit_no[s] = n_unsplit
                n_unsplit += 1
            else:
                split_no[s] = n_split
                n_split += 1
        tiles, reads = {}, {"act": 0, "dve": 0}
        order = []
        for s in units:
            key = s[:3] if s[0] == "ffn_out" else s
            if key not in tiles:
                r = GEMMS[s[0]]
                reads[r] += 1
                tiles[key] = (len(order) % 2, r, reads[r])
                order.append(key)
        tile_no = {k: i for i, k in enumerate(order)}

        def unit_parts(s):
            kind, l = s[0], s[1]

            def cols(src, c0, n=P, m0=0, rows=None):
                v = src[l] if rows is None else src[l, rows[0]:rows[1]]
                nk = v.shape[0] // P
                return ((slice(0, P), slice(0, nk), slice(m0, m0 + n)),
                        v[:, c0:c0 + n].rearrange("(k p) m -> p k m", p=P))

            if kind == "cols_c":
                return [cols(a["w_in"], OFF_C + s[2] * P)]
            if kind == "cols_a":
                if s[2] < 16:
                    return [cols(a["w_in"], s[2] * P)]
                return [cols(a["w_in"], 4 * A_W, A_H, 0), cols(a["w_in"], 4 * A_W + A_H, A_H, 32)]
            if kind == "cols_b":
                if s[2] < 4:
                    return [cols(a["w_in"], OFF_B + s[2] * 64, 64, 0), cols(a["w_in"], OFF_B + 256 + s[2] * 64, 64, 64)]
                return [cols(a["w_in"], OFF_B + s[2] * P)]
            if kind == "gate":
                return [cols(a["w_in"], OFF_G + s[2] * D + s[3] * P)]
            if kind == "branch":
                c0 = s[3] * P
                if s[2] == 1:
                    v = a["w_branch_b"][l].rearrange("(v m d) n -> v d m n", v=2, d=64)
                    return [((slice(64 * i, 64 * i + 64), slice(0, 4), slice(0, P)), v[i, :, :, c0:c0 + P])
                            for i in range(2)]
                return [cols(a["w_branch_a" if s[2] == 0 else "w_branch_c"], c0)]
            if kind == "mix":
                return [cols(a["w_out"], s[2] * P)]
            if kind == "ffn_gate":
                return [cols(a["w_ffn_in"], s[2] * P)]
            if kind == "ffn_up":
                return [cols(a["w_ffn_in"], D_FF + s[2] * P)]
            k0 = 8 * s[3]
            return [cols(a["w_ffn_out"], s[2] * P, rows=(k0 * P, min(k0 + 8, KF) * P))]

        landed_at = {}
        tot = [0] * NRAW
        for i, s in enumerate(units):
            tot[i % NRAW] += 16 * len(unit_parts(s))
            landed_at[s] = (i % NRAW, tot[i % NRAW])

        def nk_of(s):
            return 4 if s[0] == "branch" else (min(8, KF - 8 * s[3]) if s[0] == "ffn_out" else 8)

        def pair_view(pair, lo=0, hi=P):
            return gp[lo:hi, 2 * pair:2 * pair + 2, 0:HALF]

        def halves(ap):
            return ap.rearrange("p (b n) -> p b n", b=2)

        def norm_base(l, w_):
            return KD * (4 * l + w_)

        def split_base(l, i):
            return KD * (3 * l + i)

        def c_group(g):
            return (P, P * g, 2, 64) if g < 4 else (TS, TP + 1, 1, TS)

        def gv(t, n):
            return t[:, 0:4 * n].rearrange("p (f n) -> p f n", n=n)

        block = ctx.enter_context(nc.Block())

        @block.tensor
        def _(pe):
            def mm(out, lhsT, rhs, start=True, stop=True):
                return pe.matmul(out, lhsT, rhs, start=start, stop=stop, skip_group_check=True)

            def order_after(ins):
                chains["pe"].inc(ins)
                pe.wait_ge(chains["pe"].sem, chains["pe"].value)

            done_k = {}

            def gemm(s, rh=None, rl=None, rhs=None, first=True, last=True, cut=HALF, wait_k=False, k0=0, nk=8, steps=8):
                ks = range(done_k.get(s, 0), min(nk, done_k.get(s, 0) + steps))
                if not ks:
                    return
                done_k[s] = ks[-1] + 1
                key = s[:3] if s[0] == "ffn_out" else s
                pair, reader, turn = tiles[key]
                if s in split_no:
                    slot = split_no[s] % NSPLIT
                    if ks[0] == 0:
                        pe.wait_ge(low_ready.sem, split_no[s] + 1)
                else:
                    at, value = landed_at[s]
                    slot = unit_no[s] % NRAW
                    if ks[0] == 0:
                        pe.wait_ge(landed[at].sem, value)
                if first and ks[0] == 0 and tile_no[key] >= 2:
                    _, r, t = tiles[order[tile_no[key] - 2]]
                    pe.wait_ge(emptied[r].sem, t)
                for k in ks:
                    if wait_k:
                        (xl_odd if k % 2 and s[0] != "mix" else xl_ready).wait_next(pe, "pe")
                    if rhs is None:
                        passes = [(wh[:, slot, k], rh[:, k0 + k]), (wh[:, slot, k], rl[:, k0 + k]),
                                  (wl[:, slot, k], rh[:, k0 + k])]
                    else:
                        passes = [(wraw[:, slot, k], rhs[k])]
                    for i, (wt, act_) in enumerate(passes):
                        pieces = [(0, 0, 0, cut), (1, 0, cut, T - cut)]
                        for b, to, at, n in pieces:
                            last_mm = mm(gp[:, 2 * pair + b, to:to + n], wt, act_[:, at:at + n],
                                         start=first and k == 0 and i == 0 and to == 0,
                                         stop=last and k == nk - 1 and i == len(passes) - 1)
                if ks[-1] == nk - 1:
                    products.inc(last_mm)

            unit_at = [0]

            def product(s, steps=8):
                kind = s[0]
                if kind == "branch":
                    l, b, m = s[1:]
                    rhs = [(acols[:, AQ + k, :], bh[:, k, :], cc[:, k, :])[b] for k in range(4)]
                    gemm(s, rhs=rhs, nk=4, steps=steps)
                else:
                    gemm(s, rh=xh, rl=xl, cut=SPLIT_C if kind == "cols_c" or (kind == "cols_b" and s[2] < 4) else HALF,
                         wait_k=bool(first_user.get("norm")), steps=steps)
                    first_user["norm"] = False

            def fill(steps):
                if unit_at[0] < len(units):
                    s = units[unit_at[0]]
                    if s[0] in ("cols_c", "gate") or (s[0] == "branch" and s[3] > 0):
                        product(s, steps)

            def sum_squares(l, w_):
                bank[0].claim(pe)
                bank[1].claim(pe)
                for k in range(KD):
                    pe.wait_ge(sq_ready.sem, norm_base(l, w_) + k + 1)
                    for b in range(2):
                        last = mm(mp[b][:, 0:HALF], C("ones"), squares[:, k, b * HALF:(b + 1) * HALF],
                                  start=(k == 0), stop=(k == KD - 1))
                        if k == KD - 1:
                            bank[b].filled(last, "act")

            def load_x():
                pe.wait_ge(ld_const.sem, 16)
                pe.wait_ge(ld_x.sem, 16 * 5)
                for k in range(KD):
                    b = bank[2 + k % 2]
                    b.claim(pe)
                    for t in range(4):
                        last = pe.transpose(b.t[:, t * P:(t + 1) * P], x_tok[:, t, k * P:(k + 1) * P], C("ident"))
                    b.filled(last, "act" if k % 2 else "dve")
                bank[0].claim(pe)
                for k in range(KD):
                    last = pe.transpose(mp[0][:, k * TS:(k + 1) * TS], x_tok[0:TS, 4, k * P:(k + 1) * P],
                                        C("ident")[0:TS, 0:TS])
                bank[0].filled(last, "act")
                pe.wait_ge(ld_prm.sem, 16 * (1 + DEPTH * len(PARAM_ROWS)))
                bank[0].claim(pe)
                for l in range(DEPTH):
                    last = pe.transpose(mp[0][:, l * P:l * P + NPARAM], prm_rows[0:NPARAM, l, :], C("ident")[0:NPARAM, 0:NPARAM])
                bank[0].filled(last, "act")
                bank[1].claim(pe)
                bank[1].filled(mm(mp[1][0:8, 0:256], table[:], C("bucket_hot")[0:32]), "dve")

            def c_shift_out():
                flow("shift_cols").wait_next(pe, "pe")
                bank[0].claim(pe)
                bank[0].filled(pe.transpose(mp[0][0:2 * CT, 0:P], shift_out[:], C("ident")), "act")

            def c_prep(l, g):
                n, at, nch, L = c_group(g)
                if g == 0:
                    pe.wait_ge(ld_layer.sem, 16 * 12 * (l + 1))
                bank[0].claim(pe)
                flow("c_tanh_w").wait_next(pe, "pe")
                for f in range(4):
                    last = mm(mp[0][:, f * n:(f + 1) * n], lora[0:64, f * P:(f + 1) * P], tanh_w[:, 0:n])
                bank[0].filled(last, "act", ("c_lw", l, g))
                fill(2)
                bank[2].claim(pe)
                flow("c_kk_sq").wait_next(pe, "pe")
                bank[2].filled(mm(mp[2][:, 0:4 * n], C("headones"), scratch[:, 0:4 * n]), "dve")
                bank[1].claim(pe)
                for f in range(4):
                    last = mm(mp[1][:, f * n:(f + 1) * n], lora[64:128, f * P:(f + 1) * P], cc[64:128, 12, at:at + n])
                bank[1].filled(last, "act", ("c_la", l, g))
                bank[0].claim(pe)
                for f in range(4):
                    last = pe.transpose(mp[0][0:n, f * P:(f + 1) * P], cc[:, 8 + f, at:at + n], C("ident"))
                bank[0].filled(last, "act")
                fill(4)

            def c_keys(l, g):
                fill(8)

            def c_scaled(l, g):
                n, at, nch, L = c_group(g)
                fill(2)
                bank[3].claim(pe)
                flow("c_rk").wait_next(pe, "pe")
                bank[3].filled(mm(mp[3][:, 0:4 * n], C("headones"), scratch[:, 0:4 * n]), "dve")
                flow("c_scaled").wait_next(pe, "pe")
                for b, src in ((1, kprime), (2, in_rate)):
                    bank[b].claim(pe)
                    for f in range(4):
                        last = pe.transpose(mp[b][0:n, f * P:(f + 1) * P], gv(src, n)[:, f, :], C("ident"))
                    bank[b].filled(last, "act")

            def heads():
                for p in range(4):
                    for q in range(2):
                        yield 2 * p + q, p, q

            def c_gram(l, g):
                n, at, nch, L = c_group(g)

                def grams(banks, src, q):
                    for p in range(4):
                        h = 2 * p + q
                        for c in range(nch):
                            out = mp[banks[h // 4]][64 * c:64 * c + L, (h % 4) * 2 * L:(h % 4 + 1) * 2 * L]
                            last = mm(out.rearrange("p (u t) -> p u t", u=2),
                                      gv(src, n)[64 * q:64 * q + 64, p, c * L:c * L + L],
                                      kap_r[64 * q:64 * q + 64, p, :, c * L:c * L + L])
                        if p % 2 == 1:
                            ends.append((banks[h // 4], last))

                ends = []
                for b in (0, 3, 1):
                    bank[b].claim(pe)
                grams((0, 3), in_rate, 0)
                for q in range(2):
                    for p in range(4):
                        for c in range(nch):
                            last = mm(mp[1][64 * c:64 * c + L, (2 * p + q) * L:(2 * p + q + 1) * L],
                                      kap_r[64 * q:64 * q + 64, p, 0, c * L:c * L + L],
                                      gv(in_rate, n)[64 * q:64 * q + 64, p, c * L:c * L + L])
                    if q == 0:
                        order_after(last)
                        ends = []
                        grams((0, 3), in_rate, 1)
                        for b, ins in ends:
                            bank[b].filled(ins, "dve")
                bank[1].filled(last, "dve")
                bank[2].claim(pe)
                fill(1)
                bank[0].claim(pe)
                ends = []
                grams((2, 0), kprime, 1)
                order_after(ends[-1][1])
                ends = []
                grams((2, 0), kprime, 0)
                for b, ins in ends:
                    bank[b].filled(ins, "dve")
                fill(3)

            def c_level(l, g, k):
                n, at, nch, L = c_group(g)

                def by_head(b, lhsT, rhs, mark=None):
                    bank[b].claim(pe)
                    for h in range(8):
                        last = mm(mp[b][0:n, h * L:(h + 1) * L], lhsT[0:n, h, 0:n], rhs[0:n, h, 0:L])
                    bank[b].filled(last, "dve", mark)

                if k == 1:
                    flow("c_a_bd").wait_next(pe, "pe")
                    flow("c_inv0").wait_next(pe, "pe")
                else:
                    bank[3].wait_emptied(pe, ("c_inv", l, g, k - 1))
                by_head(1, a_bd, inv, ("c_w", l, g, k))
                fill(2)
                if k < (5 if L == 64 else 4):
                    bank[1].claim(pe)
                    flow("c_invT_bd").wait_next(pe, "pe")
                    by_head(3, invT_bd, w_lev, ("c_inv", l, g, k))
                flow("c_w_bd").wait_next(pe, "pe")
                by_head(2, w_bd, invT, ("c_invT", l, g, k))

            def c_chain(l, g, c):
                n, at, nch, L = c_group(g)
                if g == 4:
                    pe.wait_ge(flow("c_state_in").sem, 16 * (l + 1))
                    bank[0].claim(pe)
                    for h, p, q in heads():
                        last = mm(mp[0][64 * q:64 * q + 64, p * 64:(p + 1) * 64], s_nat[64 * q:64 * q + 64, p, :],
                                  C("ident")[64 * q:64 * q + 64, 64 * q:64 * q + 64])
                    bank[0].filled(last, "dve")
                r = slice(64 * c, 64 * c + L)
                cur = (2 * g + c) % 2
                bank[0].claim(pe)
                for h in range(8):
                    last = mm(mp[0][r, h * 64:(h + 1) * 64], b_rk[r, h, 0, 0:L], vt[r, h * 64:(h + 1) * 64],
                              start=h == 0, stop=False)
                order_after(last)
                flow("c_state").wait_next(pe, "pe")
                for p in range(4):
                    last = mm(mp[0][r, p * P:(p + 1) * P], kap_r[:, p, 0, c * L:c * L + L], state[:, cur, p, :], start=False)
                bank[0].filled(last, "dve")
                bank[3].claim(pe)
                for p in range(4):
                    rates = kap_r[:, p, 1, c * L:c * L + L]
                    last = mm(mp[3][:, p * 2 * L:(p + 1) * 2 * L], state[:, cur, p, :], view(rates, [[0, 2], [1, L]]),
                              start=p == 0, stop=False)
                order_after(last)
                bank[1].claim(pe)
                bank[0].claim(pe)
                for h in range(8):
                    last = mm(mp[1][r, h * 64:(h + 1) * 64], invT[r, h, 0:L], rhs_z[r, h, :])
                bank[1].filled(last, "dve")
                bank[2].claim(pe)
                for p in range(4):
                    mm(mp[2][:, p * P:(p + 1) * P], kt[r, p * P:(p + 1) * P], vt[r, p * P:(p + 1) * P], start=p == 0, stop=False)
                bank[1].claim(pe)
                for p in range(4):
                    last = mm(mp[2][:, p * P:(p + 1) * P], bt[r, p * P:(p + 1) * P], view(neg_z[r, 2 * p, :], [[1, P]]), start=False)
                bank[2].filled(last, "dve")
                for p in range(4):
                    out = mp[3][:, p * 2 * L:(p + 1) * 2 * L].rearrange("p (q t) -> p q t", q=2)
                    mm(out, vt[r, p * P:(p + 1) * P], b_rk[r, 2 * p:2 * p + 2, 1, 0:L], start=False, stop=False)
                    last = mm(out, view(neg_z[r, 2 * p, :], [[1, P]]), a_rb[r, 2 * p:2 * p + 2, 1, 0:L], start=False)
                bank[3].filled(last, "act", ("c_y", l, g, c))
                fill(4)

            def c_state_out(l, g):
                flow("c_state").wait_next(pe, "pe")
                cur = 0 if g == 3 else 1
                bank[3].claim(pe)
                for h, p, q in heads():
                    last = mm(mp[3][64 * q:64 * q + 64, p * 64:(p + 1) * 64], state[64 * q:64 * q + 64, cur, p, 64 * q:64 * q + 64],
                              C("ident")[64 * q:64 * q + 64, 64 * q:64 * q + 64])
                bank[3].filled(last, "act", ("c_state", l, g))

            def over_sequence(first, weights, src, reader, mark=None):
                for b in range(2):
                    bank[first + b].claim(pe)
                    c0, c1 = (0, Y_CUT) if b == 0 else (Y_CUT, CW)
                    bank[first + b].filled(mm(mp[first + b][:, 0:c1 - c0], weights, src[:, c0:c1]), reader, mark)

            def c_variance(l, f):
                if f == 0:
                    bank[3].wait_emptied(pe, ("c_state", l, 4))
                over_sequence(0, C("headones"), cc[:, f, :], "dve")
                fill(3)
                flow("c_dev_sq").wait_next(pe, "pe")
                over_sequence(2, C("headones"), y_sq[:, f % 2, :], "act", ("c_var", l, f))

            def c_finish(l, f):
                if f == 0:
                    flow("c_gate_in").wait_next(pe, "pe")
                over_sequence(2 * (f % 2), lora[:, 512 + f * P:512 + (f + 1) * P], cc[:, 13, :], "dve")
                fill(2)

            def a_chunk(l, g):
                n, at = group(g)
                if g == 0:
                    flow("a_rows").wait_next(pe, "pe")
                sel = lambda h, m: C("sel")[0:4, h * P:h * P + m]
                bank[0].claim(pe)
                for h in range(4):
                    last = mm(mp[0][0:n, h * n:(h + 1) * n], sel(h, n), r_g[0:4, at:at + n])
                bank[0].filled(last, "dve", ("a_g", l, g))
                bank[1].claim(pe)
                for h in range(4):
                    last = mm(mp[1][:, h * n:(h + 1) * n], sel(h, P), r_in[0:4, at:at + n])
                bank[1].filled(last, "dve")
                bank[2].claim(pe)
                mm(mp[2][0:n, 0:4], r_li[0:4, at:at + n], C("ident")[0:4, 0:4])
                bank[2].filled(mm(mp[2][0:n, 4:8], r_wk[0:4, at:at + n], C("ident")[0:4, 0:4]), "act")
                bank[3].claim(pe)
                for h in range(4):
                    last = mm(mp[3][0:n, h * n:(h + 1) * n], acols[:, AK + h, at:at + n], acols[:, AQ + h, at:at + n])
                bank[3].filled(last, "dve")
                for b, c0 in ((0, AK), (1, AV)):
                    fill(2)
                    bank[b].claim(pe)
                    for h in range(4):
                        last = pe.transpose(mp[b][0:n, h * P:(h + 1) * P], acols[:, c0 + h, at:at + n], C("ident"))
                    bank[b].filled(last, "act")
                fill(1)

            def a_chunk_out(l, g):
                n, at = group(g)
                sel = lambda h, m: C("sel")[0:4, h * P:h * P + m]
                bank[0].claim(pe)
                for h in range(4):
                    last = mm(mp[0][:, h * n:(h + 1) * n], sel(h, P), r_nm[0:4, at:at + n])
                bank[0].filled(last, "dve")
                bank[3].claim(pe)
                bank[1].claim(pe)
                if g == 4:
                    flow("a_n_spread").wait_next(pe, "pe")
                for b, c0, mark in ((3, P, ("a_den", l, g)), (2, 0, None)):
                    bank[b].claim(pe)
                    for h in range(4):
                        out = mp[b][:, h * n:(h + 1) * n]
                        mm(out, vo[0:n, h, c0:c0 + P], dexp[0:n, h * n:(h + 1) * n], stop=False)
                        last = mm(out, cn[:, h, c0:c0 + P], qt[:, h * n:(h + 1) * n], start=False)
                    bank[b].filled(last, "act", mark)
                for b in range(2):
                    if b:
                        fill(1)
                    bank[1 + b].claim(pe)
                    for i in range(2):
                        h = 2 * b + i
                        last = mm(mp[1 + b][:, i * 256:(i + 1) * 256], kw[0:n, h * P:(h + 1) * P], vo[0:n, h, :])
                    bank[1 + b].filled(last, "dve", ("a_state", l, g))

            def a_finish(l):
                for h in range(4):
                    fill(2)
                    flow("a_h_sq").wait_next(pe, "pe")
                    for b in range(2):
                        bk = 2 * (h % 2) + b
                        bank[bk].claim(pe)
                        bank[bk].filled(mm(mp[bk][:, 0:HALF], C("ones"), (r_li, r_wk)[h % 2][:, b * HALF:(b + 1) * HALF]),
                                        "dve", ("a_norm", l, h))

            def b_values(l):
                pe.wait_ge(emptied["act"].sem, tiles[("cols_b", l, 5)][2])
                bank[0].claim(pe)
                for j in range(4):
                    last = pe.transpose(mp[0][:, j * P:(j + 1) * P], bkv[:, 1, j * P:(j + 1) * P], C("ident"))
                bank[0].filled(last, "act")
                bank[1].claim(pe)
                for j in range(4):
                    m = P if j < 3 else 64
                    last = pe.transpose(mp[1][0:m, j * P:(j + 1) * P], bkv[:, 1, 64 + j * P:64 + j * P + m], C("ident"))
                bank[1].filled(last, "dve")
                bank[2].claim(pe)
                pe.transpose(mp[2][:, 0:P], bkv[:, 0, TP - P:TP], C("ident"))
                pe.transpose(mp[2][0:TS, P:2 * P], bkv[:, 0, TP:T], C("ident"))
                bank[2].filled(pe.transpose(mp[2][0:TS, 2 * P:3 * P], bkv[:, 1, TP:T], C("ident")), "act", ("b_values", l))
                bank[3].claim(pe)
                pe.wait_ge(flow("b_cache_in").sem, 32 * (l + 1))
                bank[3].filled(pe.transpose(mp[3][:, 0:P], kcache[:], C("ident")), "dve")

            def b_chunk(l, c):
                sample = c == 8
                if c == 0:
                    flow("b_values").wait_next(pe, "pe")
                if sample:
                    n, nk, nt, at = TS, KEYS_S, 2, TP
                    keys = ks[:, :]
                else:
                    n, nt, at = CHUNK, 4, CHUNK * c
                    nk = CHUNK * min(3, c + 1)
                    keys = bkv[:, 0, at + CHUNK - nk:at + CHUNK]
                per = nt // 2
                first_n, second_n = min(nk, P), max(nk - P, 0)
                for v in range(2):
                    r = slice(64 * v, 64 * v + 64)
                    bank[v].claim(pe)
                    for i in range(per):
                        last = mm(mp[v][:, i * nk:(i + 1) * nk], bq[r, 4 * at + i * P:4 * at + (i + 1) * P], keys[r, :])
                    bank[v].filled(last, "dve")
                fill(5)
                flow("b_probs").wait_next(pe, "pe")
                bank[2].claim(pe)
                for t in range(nt):
                    last = pe.transpose(mp[2][0:first_n, t * P:(t + 1) * P], sc[:, t, 0:first_n], C("ident"))
                bank[2].filled(last, "act")
                if second_n:
                    bank[3].claim(pe)
                    for t in range(nt):
                        last = pe.transpose(mp[3][0:second_n, t * P:(t + 1) * P], sc[:, t, P:P + second_n], C("ident"))
                    bank[3].filled(last, "dve")
                fill(2)
                if second_n:
                    bank[3].claim(pe)
                bank[2].claim(pe)
                bank[0].claim(pe)
                for t in range(nt):
                    v, i = t // per, t % per
                    r = slice(64 * v, 64 * v + 64)
                    if sample:
                        va0, va1 = vcache[:, r], va[0:TS, 4, r]
                    else:
                        start = at + CHUNK - nk
                        src = va if start % P == 0 else vb
                        j = start // P
                        va0, va1 = src[0:first_n, j, r], (src[0:64, j + 1, r] if second_n else None)
                    out = mp[0][r, i * P:(i + 1) * P]
                    last = mm(out, va0, pt0[0:first_n, t * P:(t + 1) * P], stop=not second_n)
                    if second_n:
                        last = mm(out, va1, pt1[0:second_n, t * P:(t + 1) * P], start=False)
                bank[0].filled(last, "act", ("b_out", l, c))

            def store_y():
                for t in range(5):
                    n, at = group(t)
                    for b in range(2):
                        bk = 2 * (t % 2) + b
                        bank[bk].claim(pe)
                        for k in range(4):
                            last = pe.transpose(mp[bk][0:n, k * P:(k + 1) * P], x[:, 4 * b + k, at:at + n], C("ident"))
                        bank[bk].filled(last, "act" if b else "dve", ("y", t, b))

            first_user = {}
            for s in plan:
                kind = s[0]
                if kind == "load_x":
                    load_x()
                elif kind == "norm_pre":
                    sum_squares(s[1], s[2])
                    first_user["norm"] = True
                elif kind == "norm_post":
                    flow("squares_added").wait_next(pe, "pe")
                    for b in range(2):
                        bank[b].claim(pe)
                        src = squares if s[2] == 1 else sq2
                        bank[b].filled(mm(mp[b][:, 0:HALF], C("ones"), src[:, 0, b * HALF:(b + 1) * HALF]), "act")
                elif kind in ("cols_c", "cols_a", "cols_b", "gate", "ffn_gate", "ffn_up", "branch"):
                    if kind == "branch" and s[3] == 0:
                        if s[2] == 0:
                            flow("a_h").wait_next(pe, "pe")
                        elif s[2] == 1:
                            bank[0].wait_emptied(pe, ("b_out", s[1], 8))
                        else:
                            flow("c_h").wait_next(pe, "pe")
                    product(s)
                elif kind == "merge_split":
                    pass
                elif kind == "mix":
                    gemm(s, rh=xh, rl=xl, wait_k=s[2] == 0)
                elif kind == "ffn_out":
                    l, m, q = s[1:]
                    if m == 0 and q == 0:
                        flow("hidden").wait_next(pe, "pe", KF)
                    gemm(s, rh=hid_h, rl=hid_l, k0=8 * q, nk=nk_of(s), first=q == 0, last=q == 2)
                elif kind == "c_shift_out":
                    c_shift_out()
                elif kind == "store_y":
                    pe.wait_ge(flow("x_new").sem, KD * DEPTH)
                    pe.wait_ge(flow("x_new_odd").sem, KD * DEPTH)
                    store_y()
                else:
                    {"c_prep": c_prep, "c_gram": c_gram, "c_level": c_level, "c_chain": c_chain, "c_finish": c_finish,
                     "c_state_out": c_state_out, "c_gate_in": lambda l: None, "c_rsqrt": lambda l: None,
                     "c_variance": c_variance,
                     "c_keys": c_keys, "c_scale": c_keys, "c_scaled": c_scaled, "a_norm": lambda l: fill(8),
                     "a_rows": lambda l: None, "a_rows_exp": lambda l: None, "a_chunk": a_chunk,
                     "a_chunk_out": a_chunk_out, "a_finish": a_finish, "b_values": b_values,
                     "b_chunk": b_chunk}[kind](*s[1:])
                if kind in GEMMS:
                    unit_at[0] += 1

        @block.scalar
        def _(act):
            step = Lane(act, chains["act"])

            def fn(out, in_, f, **kw_):
                return act.activation(out, in_, f, **kw_)

            def split_high(n):
                if n >= n_split:
                    return
                s = split_units[n]
                if n >= NSPLIT:
                    act.wait_ge(products.sem, unit_no[split_units[n - NSPLIT]] + 1)
                at, value = landed_at[s]
                act.wait_ge(landed[at].sem, value)
                nk = nk_of(s)
                high_ready.inc(fn(wh[:, n % NSPLIT, 0:nk], wraw[:, unit_no[s] % NRAW, 0:nk], ACT.Copy))

            def product_done(s):
                act.wait_ge(products.sem, unit_no[s] + 1)
                return tiles[s[:3] if s[0] == "ffn_out" else s][0]

            def load_x():
                for k in range(1, KD, 2):
                    bank[3].read(act, "act")
                    step(fn(x[:, k, 0:TP], mp[3][:], ACT.Copy), bank[3].empty["act"])
                bank[0].read(act, "act")
                step(fn(x[:, :, TP:T], mp[0][:, 0:KD * TS].rearrange("p (k n) -> p k n", n=TS), ACT.Copy), bank[0].empty["act"])
                bank[0].read(act, "act")
                step(fn(prm[:, :, :], mp[0][:, 0:DEPTH * P].rearrange("p (l n) -> p l n", n=P)[:, :, 0:NPARAM], ACT.Copy),
                     bank[0].empty["act"])
                act.wait_ge(ld_const.sem, 16)
                flow("x_even").wait_next(act, "act", 4)

            squared = [0]

            def norm(src, sq, which):
                for k in range(KD if src is x else 0):
                    if which == "x_new":
                        flow("x_new_odd" if k % 2 else "x_new").wait_next(act, "act")
                    sq_ready.inc(fn(sq[:, k, :], src[:, k, :], ACT.Square))
                    if squared[0] == 0:
                        split_high(0)
                    squared[0] += 1
                step(fn(stats[0:1, 56:57], C("scalars", 3, 1)[0:1], ACT.Ln))
                for b in range(2):
                    bank[b].read(act, "act")
                    step(fn(rstd[:, b * HALF:(b + 1) * HALF], mp[b][:, 0:HALF], ACT.Ln, scale=1.0 / D,
                            bias=C("scalars", 0, 1)), bank[b].empty["act"])
                step(fn(rstd[:], rstd[:], ACT.Exp, scale=-0.5), flow("rstd"))

            def norm_pre(l, w_):
                norm(x, squares, "x" if l == 0 and w_ == 0 else "x_new")
                for k in range(KD):
                    xn_part.wait_next(act, "act")
                    xh_ready.inc(fn(xh[:, k, :], squares[:, k, :], ACT.Copy))

            def norm_post(l, w_):
                if w_ == 1:
                    norm(mixed, squares, "")
                else:
                    norm(ffn_y, sq2, "")

            def cols_c(s):
                l, j = s[1:]
                i = l * CT + j
                pair = product_done(s)
                if i >= 2:
                    act.wait_ge(flow("c_col").sem, i - 1)
                step(fn(craw[:, j % 2, 1:1 + TP].rearrange("p (b n) -> p b n", b=2),
                        gp[:, 2 * pair:2 * pair + 2, 0:SPLIT_C], ACT.Copy))
                step(fn(craw[:, j % 2, TP + 2:TP + 2 + TS], gp[:, 2 * pair + 1, SPLIT_C:SPLIT_C + TS], ACT.Copy),
                     emptied["act"])
                at = PARAM_AT["state_rwkv_shift"] + j
                step(fn(craw[:, j % 2, TP + 1:TP + 2], prm[:, l, at:at + 1], ACT.Copy), flow("c_raw"))

            def c_shift_out(l):
                bank[0].read(act, "act")
                if l > 0:
                    act.wait_ge(flow("shift_stored").sem, 32 * l)
                step(fn(shift_rows[:], mp[0][0:2 * CT, 0:P], ACT.Copy), bank[0].empty["act"])
                step(fn(stats[0:1, 60:61], stats[0:1, 60:61], ACT.Copy), flow("shift_rows"))

            def c_prep(l, g):
                n, at, nch, L = c_group(g)
                if g == 0:
                    act.wait_ge(flow("c_col").sem, CT * (l + 1))
                    act.wait_ge(flow("a_state_stored").sem, 96 * (l + 1))
                    act.wait_ge(flow("b_stored").sem, 96 * (l + 1))
                step(fn(tanh_w[:, 0:n], cc[0:64, 12, at:at + n], ACT.Tanh), flow("c_tanh_w"))
                flow("c_kk_raw").wait_next(act, "act")
                step(fn(scratch[:, 0:4 * n], kk[:, 0:4 * n], ACT.Square), flow("c_kk_sq"))
                for b, dst in ((0, decay_log), (1, in_rate)):
                    bank[b].read(act, "act")
                    for f in range(4):
                        ins = fn(gv(dst, n)[:, f, :], mp[b][:, f * n:(f + 1) * n], ACT.Tanh, scale=0.5,
                                 bias=half_w0a0[:, l, 4 * b + f:4 * b + f + 1])
                        step(ins, bank[b].empty["act"] if f == 3 else None)
                bank[0].read(act, "act")
                step(fn(vt[0:n, :], mp[0][0:n, :], ACT.Copy), bank[0].empty["act"])
                step(fn(stats[0:1, 56:57], C("scalars", 3, 1)[0:1], ACT.Ln))

            def c_keys(l, g):
                n, at, nch, L = c_group(g)
                flow("c_ss").wait_next(act, "act")
                step(fn(kprime[:, 0:4 * n], kprime[:, 0:4 * n], ACT.Ln, scale=float(2 ** 20)))
                step(fn(kprime[:, 0:4 * n], kprime[:, 0:4 * n], ACT.Exp, scale=-0.5, bias=C("scalars", 2, 1)), flow("c_rn"))
                flow("c_cum").wait_next(act, "act")
                en = rhs_z[:, :, :].rearrange("p a b -> p (a b)")[:, 0:4 * n]
                step(fn(en, cum[:, 0:4 * n], ACT.Exp, scale=-1.0))
                step(fn(cum[:, 0:4 * n], cum[:, 0:4 * n], ACT.Exp))
                step(fn(decay_log[:, 0:4 * n], decay_log[:, 0:4 * n], ACT.Exp), flow("c_exps"))

            def c_scaled(l, g):
                n, at, nch, L = c_group(g)
                for b, dst in ((1, kt), (2, bt)):
                    bank[b].read(act, "act")
                    step(fn(dst[0:n, :], mp[b][0:n, :], ACT.Copy), bank[b].empty["act"])

            def diagonal(dst, src, L, flow_name):
                step(fn(dst[0:L, :, 0:L], src[0:L, :, 0:L], ACT.Copy), flow(flow_name) if L < 64 else None)
                if L == 64:
                    step(fn(dst[64:128, :, 64:128], src[64:128, :, 0:64], ACT.Copy), flow(flow_name))

            def c_gram(l, g):
                n, at, nch, L = c_group(g)
                flow("c_a_masked").wait_next(act, "act")
                diagonal(a_bd, a_rb[:, :, 0, :], L, "c_a_bd")

            def c_level(l, g, k):
                n, at, nch, L = c_group(g)
                bank[1].wait_emptied(act, ("c_w", l, g, k))
                diagonal(w_bd, w_lev, L, "c_w_bd")

            def c_chain(l, g, c):
                n, at, nch, L = c_group(g)
                bank[3].read(act, "act")
                for q in range(2):
                    rows = slice(64 * q, 64 * q + 64)
                    step(fn(cc[rows, 0:4, at + c * L:at + c * L + L], view(mp[3][rows, :], [[2 * L, 4], [1, L]], q * L), ACT.Copy),
                         bank[3].empty["act"] if q else None)

            def c_state_out(l, g):
                bank[3].read(act, "act")
                before = 2 * l + g - 3
                if before:
                    act.wait_ge(flow("c_state_stored").sem, 16 * before)
                step(fn(s_out[:, :, :], mp[3][:, 0:256].rearrange("p (f t) -> p f t", t=64), ACT.Copy),
                     bank[3].empty["act"])

            def c_gate_in(l):
                step(fn(cc[:, 13, :], cc[:, 13, :], ACT.Tanh, scale=0.5), flow("c_gate_tanh"))

            def c_variance(l, f):
                flow("c_dev").wait_next(act, "act")
                if f >= 2:
                    bank[3].wait_emptied(act, ("c_var", l, f - 2))
                step(fn(y_sq[:, f % 2, :], y_dev[:, f, :], ACT.Square), flow("c_dev_sq"))
                for b in range(2):
                    bank[2 + b].read(act, "act")
                    c0, c1 = (0, Y_CUT) if b == 0 else (Y_CUT, CW)
                    step(fn(y_rn[:, f, c0:c1], mp[2 + b][:, 0:c1 - c0], ACT.Ln, scale=1.0 / 64, bias=C("scalars", 1, 1)),
                         bank[2 + b].empty["act"])

            def c_rsqrt(l):
                step(fn(y_rn[:], y_rn[:], ACT.Exp, scale=-0.5), flow("c_gn_r"))

            def cols_a(s):
                l, j = s[1:]
                pair = product_done(s)
                if j < 16:
                    step(fn(halves(acols[:, (j + AQ) % 16, :]), pair_view(pair), ACT.Copy), emptied["act"])
                    return
                step(fn(halves(r_li[0:4, :]), pair_view(pair, 0, 4), ACT.Identity, bias=gate_bias[0:4, :]))
                step(fn(halves(r_nm[32:36, :]), pair_view(pair, 32, 36), ACT.Identity, bias=gate_bias[32:36, :]),
                     emptied["act"])

            def cols_b(s):
                l, j = s[1:]
                pair = product_done(s)
                if j == 0:
                    act.wait_ge(flow("x_kept").sem, 16 * (l + 1))
                if j < 4:
                    step(fn(view(bq[:], [[4 * SPLIT_C, 2], [SPLIT_C, 4], [1, CHUNK]], CHUNK * j),
                            gp[:, 2 * pair:2 * pair + 2, 0:SPLIT_C].rearrange("p b (c t) -> p b c t", t=CHUNK), ACT.Copy))
                    step(fn(bq[:, 4 * TP + TS * j:4 * TP + TS * (j + 1)], gp[:, 2 * pair + 1, SPLIT_C:SPLIT_C + TS], ACT.Copy),
                         emptied["act"])
                    return
                step(fn(halves(bkv[:, j - 4, :]), pair_view(pair), ACT.Copy), emptied["act"])

            def a_rows(l):
                flow("a_abs").wait_next(act, "act")
                step(fn(r_wk[0:4, :], r_g[0:4, :], ACT.Exp))
                step(fn(r_wk[0:4, :], r_wk[0:4, :], ACT.Ln, bias=C("scalars", 3, 1)[0:4]), flow("a_ln"))

            def a_rows_exp(l):
                flow("a_exp_in").wait_next(act, "act")
                step(fn(r_in[0:4, :], r_in[0:4, :], ACT.Exp))
                step(fn(r_wk[0:4, :], r_wk[0:4, :], ACT.Exp))
                step(fn(r_nm[0:4, :], r_m[0:4, :], ACT.Exp, scale=-1.0), flow("a_rows"))

            def a_chunk(l, g):
                n, at = group(g)
                bank[2].read(act, "act")
                step(fn(a_cols_t[0:n, :], mp[2][0:n, 0:8], ACT.Copy), bank[2].empty["act"])
                step(fn(a_cols_t[0:n, 4:8], a_cols_t[0:n, 4:8], ACT.Copy, scale=P ** -0.5), flow("a_cols_t"))
                bank[0].wait_emptied(act, ("a_g", l, g))
                step(fn(dexp[0:n, 0:4 * n], dexp[0:n, 0:4 * n], ACT.Exp), flow("a_dexp"))
                bank[0].read(act, "act")
                for h in range(4):
                    step(fn(kw[0:n, h * P:(h + 1) * P], mp[0][0:n, h * P:(h + 1) * P], ACT.Copy,
                            scale=a_cols_t[0:n, 4 + h:5 + h]), bank[0].empty["act"] if h == 3 else None)
                bank[1].read(act, "act")
                step(fn(vo[0:n, :, 0:P], mp[1][0:n, :].rearrange("p (h v) -> p h v", v=P), ACT.Copy), bank[1].empty["act"])

            def a_chunk_out(l, g):
                n, at = group(g)
                bank[3].read(act, "act")
                step(fn(a_den[:, :, at:at + n], gv(mp[3], n), ACT.Abs), bank[3].empty["act"])
                bank[2].read(act, "act")
                step(fn(acols[:, AQ:AQ + 4, at:at + n], mp[2][:, 0:4 * n].rearrange("p (h t) -> p h t", t=n), ACT.Copy),
                     bank[2].empty["act"])

            def a_finish(l):
                step(fn(acols[:, AO:AO + 4, :], acols[:, AO:AO + 4, :], ACT.Tanh, scale=0.5), flow("a_o_tanh"))
                flow("a_den_ok").wait_next(act, "act")
                step(fn(a_den[:], a_den[:], ACT.Square), flow("a_den_sq"))
                for h in range(4):
                    if h >= 2:
                        bank[2 * (h % 2) + 1].wait_emptied(act, ("a_norm", l, h - 2))
                    step(fn((r_li, r_wk)[h % 2][:], acols[:, AQ + h, :], ACT.Square), flow("a_h_sq"))

            def a_norm(l):
                for h in range(4):
                    bank[2 * (h % 2) + 1].wait_emptied(act, ("a_norm", l, h))
                    step(fn(a_den[:, h, :], a_den[:, h, :], ACT.Ln, scale=1.0 / P))
                for h in range(4):
                    step(fn(a_den[:, h, :], a_den[:, h, :], ACT.Exp, scale=-0.5), flow("a_r"))

            def b_values(l):
                flow("a_h").wait_next(act, "act")
                bank[0].read(act, "act")
                step(fn(va[:, 0:4, :], mp[0][:].rearrange("p (j d) -> p j d", d=P), ACT.Copy), bank[0].empty["act"])
                bank[2].read(act, "act")
                step(fn(kout[:, 0, :], mp[2][:, 0:P], ACT.Copy))
                step(fn(kout[0:TS, 1, :], mp[2][0:TS, P:2 * P], ACT.Copy))
                step(fn(va[0:TS, 4, :], mp[2][0:TS, 2 * P:3 * P], ACT.Copy), bank[2].empty["act"])

            def b_chunk(l, c):
                sample = c == 8
                n, nt, at = (TS, 2, TP) if sample else (CHUNK, 4, CHUNK * c)
                nk = KEYS_S if sample else CHUNK * min(3, c + 1)
                flow("b_max").wait_next(act, "act")
                for t in range(nt):
                    step(fn(sc[:, t, 0:nk], sc[:, t, 0:nk], ACT.Exp, bias=stats[:, 8 + t:9 + t],
                            accum_out=stats[:, 24 + t:25 + t]))
                step(fn(stats[:, 16:16 + nt], stats[:, 16:16 + nt], ACT.Exp), flow("b_exp"))
                bank[2].read(act, "act")
                step(fn(pt0[0:min(nk, P), 0:nt * P], mp[2][0:min(nk, P), 0:nt * P], ACT.Copy), bank[2].empty["act"])
                bank[0].read(act, "act")
                step(fn(bh[:, :, at:at + n], mp[0][:, 0:4 * n].rearrange("p (m t) -> p m t", t=n), ACT.Copy),
                     bank[0].empty["act"])

            def gate(s):
                l, b, m = s[1:]
                i = GATES.index((b, m))
                if i == 0:
                    act.wait_ge(flow("b_stored").sem, 96 * (l + 1))
                if 2 <= i < 2 * KD:
                    act.wait_ge(emptied["dve"].sem, tiles[("branch", l) + GATES[i - 2]][2])
                pair = product_done(s)
                dst = gate_c[:, m, :] if b == 2 else gate_t[:, i % 2, :]
                step(fn(halves(dst), pair_view(pair), ACT.Tanh, scale=0.5), emptied["act"])

            def merge_split(l):
                for k in range(KD):
                    flow("merged").wait_next(act, "act")
                    xh_ready.inc(fn(xh[:, k, :], merged[:, k, :], ACT.Copy, scale=0.5))

            split_units = [s for s in units if s in split_no]
            high_made = {0}
            for s in plan:
                kind = s[0]
                if kind in GEMMS:
                    for s2 in units[unit_no[s] + 1:unit_no[s] + 3]:
                        if s2 in split_no:
                            if split_no[s2] not in high_made:
                                high_made.add(split_no[s2])
                                split_high(split_no[s2])
                            break
                if kind == "load_x":
                    load_x()
                elif kind == "norm_pre":
                    norm_pre(*s[1:])
                elif kind == "norm_post":
                    norm_post(*s[1:])
                elif kind == "cols_c":
                    cols_c(s)
                elif kind == "cols_a":
                    cols_a(s)
                elif kind == "cols_b":
                    cols_b(s)
                elif kind == "gate":
                    gate(s)
                elif kind == "mix":
                    pair = product_done(s)
                    step(fn(halves(mixed[:, s[2], :]), pair_view(pair), ACT.Copy), emptied["act"])
                    sq_ready.inc(fn(squares[:, s[2], :], mixed[:, s[2], :], ACT.Square))
                elif kind == "ffn_gate":
                    pair = product_done(s)
                    if s[2] >= 2:
                        act.wait_ge(flow("hidden").sem, KF * s[1] + s[2] - 1)
                    step(fn(halves(ffn_t[:, s[2] % 2, :]), pair_view(pair), ACT.Tanh, scale=0.5), flow("ffn_tanh"))
                elif kind == "ffn_up":
                    act.wait_ge(emptied["dve"].sem, tiles[s][2])
                    step(fn(hid_h[:, s[2], :], ffn_p[:, s[2] % 2, :], ACT.Copy), flow("hidden_high"))
                elif kind == "ffn_out":
                    if s[3] == 2:
                        pair = product_done(s)
                        step(fn(halves(ffn_y[:, s[2], :]), pair_view(pair), ACT.Copy), emptied["act"])
                        sq_ready.inc(fn(sq2[:, s[2], :], ffn_y[:, s[2], :], ACT.Square))
                elif kind == "store_y":
                    for t in range(5):
                        n, at = group(t)
                        b = bank[2 * (t % 2) + 1]
                        b.read(act, "act")
                        step(fn(y_tok[0:n, t, 512:1024], b.t[0:n, :], ACT.Copy), b.empty["act"])
                elif kind in ("branch", "c_finish", "c_scale"):
                    pass
                else:
                    {"c_shift_out": c_shift_out, "c_prep": c_prep, "c_gram": c_gram, "a_rows_exp": a_rows_exp,
                     "c_keys": c_keys, "c_scaled": c_scaled, "a_norm": a_norm,
                     "c_state_out": c_state_out, "c_gate_in": c_gate_in, "c_variance": c_variance, "c_rsqrt": c_rsqrt,
                     "a_chunk_out": a_chunk_out, "c_level": c_level, "c_chain": c_chain,
                     "a_rows": a_rows, "a_chunk": a_chunk, "a_finish": a_finish,
                     "b_values": b_values, "b_chunk": b_chunk, "merge_split": merge_split}[kind](*s[1:])

        @block.vector
        def _(dve):
            step = Lane(dve, chains["dve"])

            def signal(count):
                step(dve.tensor_copy(stats[0:1, 61:62], stats[0:1, 61:62]), count)

            tt, stt, ts = dve.tensor_tensor, dve.scalar_tensor_tensor, dve.tensor_scalar
            MUL, ADD, SUB, MAX, MIN = ALU.mult, ALU.add, ALU.subtract, ALU.max, ALU.min

            def product_done(s):
                dve.wait_ge(products.sem, unit_no[s] + 1)
                return tiles[s][0]

            def load_x():
                step(dve.memset(stats[:], 0.0))
                for k in range(0, KD, 2):
                    bank[2].read(dve, "dve")
                    step(dve.tensor_copy(x[:, k, 0:TP], mp[2][:]), bank[2].empty["dve"])
                    signal(flow("x_even"))
                dve.wait_ge(ld_const.sem, 16)
                bank[1].read(dve, "dve")
                step(dve.tensor_copy(bias_line[:], mp[1][0:8, 0:256]), bank[1].empty["dve"])
                signal(flow("bias_line"))

            def norm_pre(l, w_):
                g0 = PARAM_AT["norm_mix_pre" if w_ == 0 else "norm_ffn_pre"]
                flow("rstd").wait_next(dve, "dve")
                if w_ == 0:
                    step(dve.memset(craw[:, :, 0:1], 0.0))
                if l == 0 and w_ == 0:
                    at = PARAM_AT["c_w0"]
                    step(ts(half_w0a0[:], prm[:, :, at:at + 8], 0.5, None, MUL))

                def low(k):
                    if k % 2:
                        return
                    dve.wait_ge(xh_ready.sem, split_base(l, w_) + k + 1)
                    step(tt(xl[:, k, :], squares[:, k, :], xh[:, k, :].bitcast(F32), SUB), xl_ready)

                for k in range(KD):
                    step(stt(out=squares[:, k, :], in0=x[:, k, :], scalar=prm[:, l, g0 + k:g0 + k + 1], in1=rstd[:],
                             op0=MUL, op1=MUL), xn_part)
                    if k:
                        low(k - 1)
                low(KD - 1)

            def norm_post(l, w_):
                g0 = PARAM_AT["norm_mix_post" if w_ == 1 else "norm_ffn_post"]
                src, tmp = (mixed, squares) if w_ == 1 else (ffn_y, sq2)
                flow("rstd").wait_next(dve, "dve")
                if w_ == 1:
                    dve.wait_ge(flow("x_back").sem, 16 * (l + 1))
                for k in range(KD):
                    step(stt(out=tmp[:, k, :], in0=src[:, k, :], scalar=prm[:, l, g0 + k:g0 + k + 1], in1=rstd[:],
                             op0=MUL, op1=MUL), flow("x_step_odd") if k % 2 else None)
                    if k % 2 == 0:
                        step(tt(x[:, k, :], x[:, k, :], tmp[:, k, :], ADD), flow("x_new"))

            def cols_c(s):
                l, j = s[1:]
                flow("c_raw").wait_next(dve, "dve")
                raw, d = craw[:, j % 2, :], cc[:, j, :]
                step(dve.tensor_copy(view(shift_out[:], [[CT, 2]], j), view(raw, [[TS + 1, 2]], TP)),
                     flow("shift_cols") if j == CT - 1 else None)
                step(tt(d, raw[:, 0:CW], raw[:, 1:CW + 1], SUB))
                mu = PARAM_AT["c_mu"] + j
                step(stt(out=cc[:, j, :], in0=d, scalar=prm[:, l, mu:mu + 1], in1=raw[:, 1:CW + 1], op0=MUL, op1=ADD),
                     flow("c_col"))

            C1 = -0.5 * math.exp(-0.5)

            def c_prep(l, g):
                n, at, nch, L = c_group(g)
                r4 = cc[:, 0:4, at:at + n]
                k4 = cc[:, 4:8, at:at + n]
                v4 = cc[:, 8:12, at:at + n]
                f4 = lambda t: t[:, 0:4 * n]
                if g == 0:
                    dve.wait_ge(flow("a_state_stored").sem, 96 * (l + 1))
                    dve.wait_ge(flow("b_stored").sem, 96 * (l + 1))
                    step(dve.memset(diag[:], 0.0))
                step(tt(gv(kk, n), k4, view(prm[:, l, PARAM_AT["c_k_k"]:], [[1, 4], [0, n]]), MUL),
                     flow("c_kk_raw"))
                bank[2].read(dve, "dve")
                step(ts(f4(kprime), mp[2][:, 0:4 * n], 1e-24, None, MAX), bank[2].empty["dve"])
                signal(flow("c_ss"))
                bank[0].wait_emptied(dve, ("c_lw", l, g))
                step(ts(f4(decay_log), f4(decay_log), C1, C1, MUL, ADD))
                if L == 64:
                    step(dve.tensor_tensor_scan(f4(cum), C("scan64")[:, 0:4 * n], f4(decay_log), 0.0, MUL, ADD))
                for f in range(4 if L < 64 else 0):
                    step(dve.tensor_tensor_scan(gv(cum, n)[:, f, :], C("ones", 0, L), gv(decay_log, n)[:, f, :], 0.0, MUL, ADD))
                step(tt(f4(decay_log), f4(cum), f4(decay_log), SUB), flow("c_cum"))
                bank[1].wait_emptied(dve, ("c_la", l, g))
                step(ts(f4(in_rate), f4(in_rate), 0.5, 0.5, MUL, ADD))

            def c_keys(l, g):
                n, at, nch, L = c_group(g)
                r4 = cc[:, 0:4, at:at + n]
                k4 = cc[:, 4:8, at:at + n]
                f4 = lambda t: t[:, 0:4 * n]
                flow("c_rn").wait_next(dve, "dve")
                step(tt(f4(kk), f4(kk), f4(kprime), MUL))
                step(stt(out=gv(kprime, n), in0=gv(in_rate, n), scalar=-1.0, in1=view(prm[:, l, PARAM_AT["c_k_a"]:], [[1, 4], [0, n]]),
                         op0=ADD, op1=MUL))
                step(stt(out=gv(kprime, n), in0=gv(kprime, n), scalar=1.0, in1=k4, op0=ADD, op1=MUL), flow("c_kprime"))
                step(tt(f4(in_rate), f4(kk), f4(in_rate), MUL))

            def c_scale(l, g):
                n, at, nch, L = c_group(g)
                r4 = cc[:, 0:4, at:at + n]
                f4 = lambda t: t[:, 0:4 * n]
                flow("c_exps").wait_next(dve, "dve")
                en = rhs_z[:, :, :].rearrange("p a b -> p (a b)")[:, 0:4 * n]
                step(tt(kap_r[:, :, 0, 0:n], gv(kk, n), gv(decay_log, n), MUL))
                step(tt(kap_r[:, :, 1, 0:n], r4, gv(cum, n), MUL))
                step(tt(f4(in_rate), f4(in_rate), en, MUL))
                flow("c_rk").wait_next(dve, "dve")
                step(tt(f4(kprime), f4(kprime), en, MUL), flow("c_scaled"))

            def c_scaled(l, g):
                n, at, nch, L = c_group(g)
                v4 = cc[:, 8:12, at:at + n]
                bank[3].read(dve, "dve")
                step(tt(v4, gv(mp[3], n), v4, MUL), bank[3].empty["dve"])

            def level_mask(k, n, L):
                return view(C("levels")[0:n], [[0, 8], [1, L]], 64 * k)

            def c_gram(l, g):
                n, at, nch, L = c_group(g)
                masks = view(C("lt_le")[0:n], [[0, 4], [64, 2], [1, L]])

                def masked(b, dst, h0):
                    bank[b].read(dve, "dve")
                    step(tt(dst[0:n, h0:h0 + 4, :, 0:L], mp[b][0:n, 0:8 * L].rearrange("p (h u t) -> p h u t", u=2, t=L),
                            masks, MUL), bank[b].empty["dve"])

                masked(0, a_rb, 0)
                masked(3, a_rb, 4)
                signal(flow("c_a_masked"))
                bank[1].read(dve, "dve")
                i_, it_ = inv[0:n, :, 0:L], invT[0:n, :, 0:L]
                eye = view(C("eye64")[0:n], [[0, 8], [1, L]])
                step(tt(it_, a_rb[0:n, :, 0, 0:L], view(C("level0_up")[0:n], [[0, 8], [1, L]]), MUL))
                step(tt(it_, eye, it_, SUB))
                step(tt(i_, mp[1][0:n, 0:8 * L].rearrange("p (h t) -> p h t", t=L),
                        view(C("level0_neg")[0:n], [[0, 8], [1, L]]), MUL), bank[1].empty["dve"])
                step(tt(i_, i_, eye, ADD), flow("c_inv0"))
                transposed_diagonal(L)
                masked(2, b_rk, 0)
                masked(0, b_rk, 4)

            def transposed_diagonal(L):
                step(dve.tensor_copy(invT_bd[0:L, :, 0:L], invT[0:L, :, 0:L]), flow("c_invT_bd") if L < 64 else None)
                if L == 64:
                    step(dve.tensor_copy(invT_bd[64:128, :, 64:128], invT[64:128, :, 0:64]), flow("c_invT_bd"))

            def c_level(l, g, k):
                n, at, nch, L = c_group(g)
                by_head = lambda b: mp[b][0:n, 0:8 * L].rearrange("p (h t) -> p h t", t=L)
                i_, it_ = inv[0:n, :, 0:L], invT[0:n, :, 0:L]
                bank[1].read(dve, "dve")
                step(tt(w_lev[0:n, :, 0:L], by_head(1), level_mask(k, n, L), MUL), bank[1].empty["dve"])
                if k < (5 if L == 64 else 4):
                    bank[3].read(dve, "dve")
                    step(tt(i_, i_, by_head(3), SUB), bank[3].empty["dve"])
                bank[2].read(dve, "dve")
                step(tt(it_, it_, by_head(2), SUB), bank[2].empty["dve"])
                if k < (5 if L == 64 else 4) - 1:
                    transposed_diagonal(L)

            def c_chain(l, g, c):
                n, at, nch, L = c_group(g)
                if g == 0 and c == 0:
                    step(dve.memset(state[:], 0.0), flow("c_state"))
                if g == 4:
                    bank[0].read(dve, "dve")
                    for q in range(2):
                        rows = slice(64 * q, 64 * q + 64)
                        step(dve.tensor_copy(state[rows, 0, :, 64 * q:64 * q + 64], mp[0][rows, 0:256].rearrange("p (f i) -> p f i", i=64)),
                             bank[0].empty["dve"] if q else None)
                    signal(flow("c_state"))
                r = slice(64 * c, 64 * c + L)
                cur = (2 * g + c) % 2
                bank[0].read(dve, "dve")
                step(dve.tensor_copy(rhs_z[r], mp[0][r, :].rearrange("p (h i) -> p h i", i=64)), bank[0].empty["dve"])
                bank[1].read(dve, "dve")
                step(ts(neg_z[r], mp[1][r, :].rearrange("p (h i) -> p h i", i=64), -1.0, None, MUL), bank[1].empty["dve"])
                bank[2].read(dve, "dve")
                for q in range(2):
                    rows = slice(64 * q, 64 * q + 64)
                    old, new = (state[rows, u, :, 64 * q:64 * q + 64] for u in (cur, 1 - cur))
                    step(tt(new, old, view(mp[2][rows, :], [[P, 4], [1, 64]], 64 * q), ADD), bank[2].empty["dve"] if q else None)
                for q in range(2):
                    rows = slice(64 * q, 64 * q + 64)
                    new = state[rows, 1 - cur, :, 64 * q:64 * q + 64]
                    step(tt(new, new, view(cum[rows, :], [[n, 4], [0, 64]], c * L + L - 1), MUL), flow("c_state") if q else None)

            def c_gate_in(l):
                flow("c_gate_tanh").wait_next(dve, "dve")
                step(ts(cc[:, 13, :], cc[:, 13, :], 0.5, 0.5, MUL, ADD), flow("c_gate_in"))

            def c_variance(l, f):
                for b in range(2):
                    bank[b].read(dve, "dve")
                    c0, c1 = (0, Y_CUT) if b == 0 else (Y_CUT, CW)
                    step(stt(out=y_dev[:, f, c0:c1], in0=mp[b][:, 0:c1 - c0], scalar=-1.0 / 64, in1=cc[:, f, c0:c1],
                             op0=MUL, op1=ADD), bank[b].empty["dve"])
                signal(flow("c_dev"))

            def c_finish(l, f):
                if f == 0:
                    flow("c_gn_r").wait_next(dve, "dve")
                d = y_dev[:, f, :]
                gain, offset = (prm[:, l, PARAM_AT[name] + f:PARAM_AT[name] + f + 1] for name in ("c_gn_g", "c_gn_b"))
                step(stt(out=d, in0=d, scalar=gain, in1=y_rn[:, f, :], op0=MUL, op1=MUL))
                step(stt(out=d, in0=d, scalar=offset, in1=cc[:, 8 + f, :], op0=ADD, op1=ADD))
                bk = 2 * (f % 2)
                bank[bk].read(dve, "dve")
                step(tt(cc[:, f, 0:Y_CUT], d[:, 0:Y_CUT], mp[bk][:, 0:Y_CUT], MUL), bank[bk].empty["dve"])
                bank[bk + 1].read(dve, "dve")
                step(tt(cc[:, f, Y_CUT:TP], d[:, Y_CUT:TP], mp[bk + 1][:, 0:TP - Y_CUT], MUL))
                step(tt(cc[:, f, TP:T], d[:, TP + 1:CW], mp[bk + 1][:, TP + 1 - Y_CUT:CW - Y_CUT], MUL), bank[bk + 1].empty["dve"])
                if f == 3:
                    signal(flow("c_h"))

            def a_rows(l):
                dve.wait_ge(emptied["act"].sem, tiles[("cols_a", l, 16)][2])
                q = slice(0, 4)
                step(dve.tensor_copy(r_lf[q, :], r_nm[32:36, :]))
                step(stt(out=r_g[q, :], in0=r_lf[q, :], scalar=-1.0, in1=r_lf[q, :], op0=MUL, op1=MIN))
                step(ts(r_in[q, :], r_lf[q, :], 0.0, None, MIN), flow("a_abs"))
                flow("a_ln").wait_next(dve, "dve")
                step(tt(r_lf[q, :], r_in[q, :], r_wk[q, :], SUB))
                step(dve.tensor_tensor_scan(r_f[q, :], C("scan_rows")[q], r_lf[q, :], 0.0, MUL, ADD))
                step(dve.tensor_tensor_scan(r_m[q, 0:TP], r_lf[q, 0:TP], r_li[q, 0:TP], 0.0, ADD, MAX))
                step(dve.tensor_tensor_scan(r_m[q, TP:T], r_lf[q, TP:T], r_li[q, TP:T], m_init[q, :], ADD, MAX))
                step(tt(r_g[q, :], r_f[q, :], r_m[q, :], SUB))
                step(tt(r_li[q, :], r_li[q, :], r_f[q, :], SUB))
                step(dve.memset(m_prev[:], 0.0))
                step(dve.tensor_copy(m_prev[q, 1:4], view(r_m[q, :], [[P, 3]], P - 1)))
                step(dve.tensor_copy(m_prev[q, 4:5], m_init[q, :]))
                step(dve.tensor_copy(g_last[q, 0:4], view(r_g[q, :], [[P, 4]], P - 1)))
                step(dve.tensor_copy(g_last[q, 4:5], r_g[q, T - 1:T]))
                for dst, src, edge in ((r_in, r_g, m_prev), (r_wk, r_li, g_last)):
                    step(tt(dst[q, 0:TP].rearrange("p (c t) -> p c t", t=P), src[q, 0:TP].rearrange("p (c t) -> p c t", t=P),
                            view(edge[q, :], [[1, 4], [0, P]]), ADD))
                    step(tt(dst[q, TP:T], src[q, TP:T], view(edge[q, :], [[0, TS]], 4), ADD))
                step(dve.memset(cn[:], 0.0))
                step(dve.memset(vo[:, :, P:256], 1.0), flow("a_exp_in"))

            def a_chunk(l, g):
                n, at = group(g)
                if g == 4:
                    dve.wait_ge(flow("a_state_in").sem, 32 * (l + 1))
                    step(dve.tensor_copy(cn[:, :, P:256], view(ncol[:], [[1, 4], [0, P]])), flow("a_n_spread"))
                flow("a_cols_t").wait_next(dve, "dve")
                bank[0].read(dve, "dve")
                for h in range(4):
                    step(stt(out=dexp[0:n, h * n:(h + 1) * n], in0=mp[0][0:n, h * n:(h + 1) * n], scalar=a_cols_t[0:n, h:h + 1],
                             in1=C("future_neg")[0:n, 0:n], op0=ADD, op1=ADD), bank[0].empty["dve"] if h == 3 else None)
                bank[1].read(dve, "dve")
                step(tt(gv(qt, n), acols[:, AQ:AQ + 4, at:at + n], gv(mp[1], n), MUL))
                step(dve.tensor_copy(a_dec[:], view(mp[1][:], [[n, 4]], n - 1)), bank[1].empty["dve"])
                flow("a_dexp").wait_next(dve, "dve")
                bank[3].read(dve, "dve")
                step(stt(out=dexp[0:n, 0:4 * n], in0=mp[3][0:n, 0:4 * n], scalar=P ** -0.5, in1=dexp[0:n, 0:4 * n],
                         op0=MUL, op1=MUL), bank[3].empty["dve"])

            def a_chunk_out(l, g):
                n, at = group(g)
                bank[3].wait_emptied(dve, ("a_den", l, g))
                bank[0].read(dve, "dve")
                step(tt(a_den[:, :, at:at + n], a_den[:, :, at:at + n], gv(mp[0], n), MAX), bank[0].empty["dve"])
                for b in range(2):
                    bank[1 + b].read(dve, "dve")
                    for i in range(2):
                        h = 2 * b + i
                        step(stt(out=cn[:, h, :], in0=cn[:, h, :], scalar=a_dec[:, h:h + 1],
                                 in1=mp[1 + b][:, i * 256:(i + 1) * 256], op0=MUL, op1=ADD),
                             bank[1 + b].empty["dve"] if i else None)

            def a_finish(l):
                step(ts(a_den[:], a_den[:], 4e12, None, MIN), flow("a_den_ok"))
                flow("a_den_sq").wait_next(dve, "dve")
                for h in range(4):
                    for b in range(2):
                        bk = 2 * (h % 2) + b
                        bank[bk].read(dve, "dve")
                        cols_ = a_den[:, h, b * HALF:(b + 1) * HALF]
                        step(stt(out=cols_, in0=cols_, scalar=P * NORM_EPS, in1=mp[bk][:, 0:HALF], op0=MUL, op1=ADD),
                             bank[bk].empty["dve"])

            def a_norm(l):
                flow("a_o_tanh").wait_next(dve, "dve")
                g0 = PARAM_AT["a_norm"]
                for h in range(4):
                    flow("a_r").wait_next(dve, "dve")
                    hh = acols[:, AQ + h, :]
                    step(tt(hh, hh, a_den[:, h, :], MUL))
                    step(stt(out=hh, in0=acols[:, AO + h, :], scalar=1.0, in1=hh, op0=ADD, op1=MUL))
                    step(ts(hh, hh, prm[:, l, g0 + h:g0 + h + 1], 0.5, MUL, MUL),
                         flow("a_h") if h == 3 else None)

            def b_values(l):
                bank[1].read(dve, "dve")
                step(dve.tensor_copy(vb[:, 0:3, :], mp[1][:, 0:3 * P].rearrange("p (j d) -> p j d", d=P)))
                step(dve.tensor_copy(vb[0:64, 3, :], mp[1][0:64, 3 * P:4 * P]), bank[1].empty["dve"])
                bank[3].read(dve, "dve")
                step(dve.tensor_copy(ks[:, 0:P], mp[3][:, 0:P]), bank[3].empty["dve"])
                step(dve.tensor_copy(ks[:, P:KEYS_S], bkv[:, 0, TP:T]), flow("b_values"))

            def b_chunk(l, c):
                sample = c == 8
                nt = 2 if sample else 4
                nk = KEYS_S if sample else CHUNK * min(3, c + 1)
                if l == 0 and c == 0:
                    dve.wait_ge(bias_in.sem, 16 * 16)
                per = nt // 2
                for v in range(2):
                    bank[v].read(dve, "dve")
                    bias = bias_s[:, v:v + 1, :] if sample else bias_p[:, 2 * v:2 * v + 2, KEYS - nk:KEYS]
                    step(stt(out=sc[:, per * v:per * v + per, 0:nk], in0=mp[v][:, 0:per * nk].rearrange("p (i k) -> p i k", k=nk),
                             scalar=B_HD ** -0.5, in1=bias, op0=MUL, op1=ADD), bank[v].empty["dve"])
                s0 = 4 if sample else 0
                step(dve.tensor_reduce(stats[:, 0:nt], sc[:, 0:nt, 0:nk], AX.X, MAX))
                step(tt(stats[:, 0:nt], stats[:, 0:nt], sinks[:, s0:s0 + nt], MAX))
                step(tt(stats[:, 16:16 + nt], sinks[:, s0:s0 + nt], stats[:, 0:nt], SUB))
                step(ts(stats[:, 8:8 + nt], stats[:, 0:nt], -1.0, None, MUL), flow("b_max"))
                flow("b_exp").wait_next(dve, "dve")
                step(tt(stats[:, 32:32 + nt], stats[:, 24:24 + nt], stats[:, 16:16 + nt], ADD))
                step(dve.reciprocal(stats[:, 40:40 + nt], stats[:, 32:32 + nt]))
                step(tt(sc[:, 0:nt, 0:nk], sc[:, 0:nt, 0:nk], view(stats[:], [[1, nt], [0, nk]], 40), MUL), flow("b_probs"))
                if nk > P:
                    bank[3].read(dve, "dve")
                    step(dve.tensor_copy(pt1[0:nk - P, 0:nt * P], mp[3][0:nk - P, 0:nt * P]), bank[3].empty["dve"])

            def branch(s):
                l, b, m = s[1:]
                i = GATES.index((b, m))
                if i == 0:
                    dve.wait_ge(flow("b_stored").sem, 96 * (l + 1))
                pair = product_done(s)
                dve.wait_ge(emptied["act"].sem, tiles[("gate", l, b, m)][2])
                dst = merged[:, m, :] if b == 0 else prod[:, i % 2, :]
                gate_ = gate_c[:, m, :] if b == 2 else gate_t[:, i % 2, :]
                step(stt(out=halves(dst), in0=halves(gate_), scalar=1.0, in1=pair_view(pair), op0=ADD, op1=MUL), emptied["dve"])
                if b:
                    step(tt(merged[:, m, :], merged[:, m, :], dst, ADD), flow("merged") if b == 2 else None)

            def hidden_low(j):
                flow("hidden_high").wait_next(dve, "dve")
                step(tt(hid_l[:, j, :], ffn_p[:, j % 2, :], hid_h[:, j, :].bitcast(F32), SUB), flow("hidden"))

            for s in plan:
                kind, l = s[0], s[1] if len(s) > 1 else 0
                if kind == "load_x":
                    load_x()
                elif kind == "norm_pre":
                    norm_pre(*s[1:])
                elif kind == "norm_post":
                    norm_post(*s[1:])
                elif kind == "cols_c":
                    cols_c(s)
                elif kind == "branch":
                    branch(s)
                elif kind == "merge_split":
                    for k in range(KD):
                        dve.wait_ge(xh_ready.sem, split_base(l, 1) + k + 1)
                        step(stt(out=xl[:, k, :], in0=merged[:, k, :], scalar=0.5, in1=xh[:, k, :].bitcast(F32),
                                 op0=MUL, op1=SUB), xl_ready)
                elif kind == "ffn_gate":
                    j = s[2]
                    pair = tiles[s][0]
                    flow("ffn_tanh").wait_next(dve, "dve")
                    step(stt(out=halves(ffn_p[:, j % 2, :]), in0=halves(ffn_t[:, j % 2, :]), scalar=1.0, in1=pair_view(pair),
                             op0=ADD, op1=MUL), emptied["dve"])
                    if j:
                        hidden_low(j - 1)
                elif kind == "ffn_up":
                    j = s[2]
                    pair = product_done(s)
                    step(stt(out=halves(ffn_p[:, j % 2, :]), in0=halves(ffn_p[:, j % 2, :]), scalar=0.5, in1=pair_view(pair),
                             op0=MUL, op1=MUL), emptied["dve"])
                    if j == KF - 1:
                        hidden_low(j)
                elif kind == "store_y":
                    for t in range(5):
                        n, at = group(t)
                        b = bank[2 * (t % 2)]
                        b.read(dve, "dve")
                        step(dve.tensor_copy(y_tok[0:n, t, 0:512], b.t[0:n, :]), b.empty["dve"])
                elif kind == "mix" or (kind == "ffn_out" and s[3] == 2):
                    sq, m, w_ = (squares, s[2], 1) if kind == "mix" else (sq2, s[2], 3)
                    if m:
                        dve.wait_ge(sq_ready.sem, norm_base(l, w_) + m + 1)
                        step(tt(sq[:, 0, :], sq[:, 0, :], sq[:, m, :], ADD), flow("squares_added") if m == KD - 1 else None)
                elif kind in ("cols_a", "cols_b", "gate", "ffn_out", "c_shift_out", "a_rows_exp", "c_state_out",
                              "c_rsqrt"):
                    pass
                else:
                    {"c_prep": c_prep, "c_gram": c_gram, "c_level": c_level, "c_chain": c_chain, "c_finish": c_finish,
                     "c_scale": c_scale, "c_keys": c_keys, "c_scaled": c_scaled, "a_norm": a_norm,
                     "c_gate_in": c_gate_in, "c_variance": c_variance,
                     "a_chunk_out": a_chunk_out,
                     "a_rows": a_rows, "a_chunk": a_chunk, "a_finish": a_finish, "b_values": b_values,
                     "b_chunk": b_chunk}[kind](*s[1:])

        @block.sync
        def _(sp):
            with nc.allow_non_contiguous_dma(reason="small vectors"):
                def put(c, dst, src):
                    c.inc(sp.dma_start(dst, src), 16)

                put(ld_const, cst[:], consts_dram)
                for t in range(4):
                    put(ld_x, x_tok[:, t, :], a["x_prompt"][0, t * P:(t + 1) * P, :])
                put(ld_x, x_tok[0:TS, 4, :], a["x_sample"][0])
                put(ld_prm, table[:], a["rel_bias"])
                for l in range(DEPTH):
                    for name, rows in PARAM_ROWS:
                        src = a[name][l] if name != "state_rwkv_shift" else a[name][l, 0, 0]
                        at = PARAM_AT[name]
                        put(ld_prm, prm_rows[at:at + rows, l, :], src.rearrange("(r c) -> r c", c=P))
                def free_raw(u):
                    s = units[u]
                    if s in split_no:
                        sp.wait_ge(low_ready.sem, split_no[s] + 1)
                    else:
                        sp.wait_ge(products.sem, unit_no[s] + 1)

                def load_unit(s):
                    u = unit_no[s]
                    if u >= NRAW:
                        free_raw(u - NRAW)
                    for (ps, ks_, ms), src in unit_parts(s):
                        put(landed[u % NRAW], wraw[ps, u % NRAW, ks_, ms], src)

                for s in units[0:NRAW - 1]:
                    load_unit(s)

                flow("bias_line").wait_next(sp, "sp")
                put(bias_out, bias_dram.rearrange("h (q n) -> h q n", n=256), view(bias_line[:], [[0, 64], [1, 256]]))
                bias_out.wait_next(sp, "sp", 16)
                h0 = bias_dram
                for hh in range(2):
                    for t in range(4):
                        head = 4 * (t // 2) + 2 * (t % 2) + hh
                        src = bass.AP(tensor=h0.tensor, offset=h0.offset + head * 64 * 256 + 63, ap=[[255, 64], [1, KEYS]])
                        put(bias_in, bias_p[64 * hh:64 * hh + 64, t, :], src)
                for kv in range(2):
                    for m in range(4):
                        src = bass.AP(tensor=h0.tensor, offset=h0.offset + (4 * kv + m) * 64 * 256 + 63,
                                      ap=[[255, TS], [1, KEYS_S]])
                        put(bias_in, bias_s[TS * m:TS * m + TS, kv, :], src)

                def vec(ap):
                    return ap.rearrange("(n u) -> n u", u=1)

                for s in plan:
                    kind, l = s[0], s[1] if len(s) > 1 else 0
                    if kind in GEMMS and unit_no[s] + NRAW - 1 < len(units):
                        load_unit(units[unit_no[s] + NRAW - 1])
                    if kind == "norm_pre" and s[2] == 0:
                        sp.wait_ge(sq_ready.sem, KD * (4 * l + 1))
                        put(flow("x_kept"), x_dram, x[:].rearrange("p k t -> p (k t)"))
                        if l > 0:
                            sp.wait_ge(products.sem, unit_no[("mix", l - 1, 0)] + 1)
                        put(ld_layer, lora[0:64, 0:512], a["c_w_w2"][l])
                        put(ld_layer, lora[64:128, 0:512], a["c_w_a2"][l])
                        put(ld_layer, lora[:, 512:1024], a["c_w_g2"][l])
                        sk = a["b_sinks"][l]
                        for hh in range(2):
                            src = bass.AP(tensor=sk.tensor, offset=sk.offset + hh, ap=[[0, 64], [2, 4]])
                            put(ld_layer, sinks[64 * hh:64 * hh + 64, 0:4], src)
                        for m in range(4):
                            src = bass.AP(tensor=sk.tensor, offset=sk.offset + m, ap=[[0, TS], [4, 2]])
                            put(ld_layer, sinks[TS * m:TS * m + TS, 4:6], src)
                        gb = vec(a["a_gate_bias"][l])
                        put(ld_layer, gate_bias[0:4, :], gb[0:4])
                        put(ld_layer, gate_bias[32:36, :], gb[4:8])
                        put(ld_layer, m_init[0:4, :], vec(a["state_mlstm_m"][l, 0]))
                        put(flow("c_state_in"), s_nat[:], a["state_rwkv_s"][l, 0].rearrange("(p q) i j -> (q i) p j", q=2))
                    if kind == "c_shift_out":
                        flow("shift_rows").wait_next(sp, "sp")
                        for i, name in enumerate(("p_rwkv_shift", "s_rwkv_shift")):
                            put(flow("shift_stored"), o[name][l, 0, 0].rearrange("(r c) -> r c", c=P),
                                shift_rows[CT * i:CT * i + CT, :])
                    if kind == "c_state_out":
                        bank[3].wait_emptied(sp, ("c_state", l, s[2]))
                        put(flow("c_state_stored"),
                            o["p_rwkv_s" if s[2] == 3 else "s_rwkv_s"][l, 0].rearrange("(p q) i j -> (q i) p j", q=2), s_out[:])
                    if kind == "mix" and s[2] == 0:
                        sp.wait_ge(products.sem, unit_no[s] + 1)
                        sp.wait_ge(flow("x_kept").sem, 16 * (l + 1))
                        put(flow("x_back"), x[:].rearrange("p k t -> p (k t)"), x_dram)
                    if kind == "a_chunk_out" and s[2] in (3, 4):
                        pre = "p" if s[2] == 3 else "s"
                        bank[2].wait_emptied(sp, ("a_state", l, s[2]))
                        done = flow("a_state_stored")
                        put(done, o[f"{pre}_mlstm_c"][l, 0].rearrange("h k v -> k h v"), cn[:, :, 0:P])
                        put(done, o[f"{pre}_mlstm_n"][l, 0].rearrange("h k -> k h"), cn[:, :, P])
                        put(done, vec(o[f"{pre}_mlstm_m"][l, 0]), r_m[0:4, TP - 1:TP] if s[2] == 3 else r_m[0:4, T - 1:T])
                        if s[2] == 3:
                            sp.wait_ge(done.sem, done.value)
                            put(flow("a_state_in"), cn[:, :, 0:P], a["state_mlstm_c"][l, 0].rearrange("h k v -> k h v"))
                            put(flow("a_state_in"), ncol[:], a["state_mlstm_n"][l, 0].rearrange("h k -> k h"))
                    if kind == "a_norm":
                        flow("a_h").wait_next(sp, "sp")
                        sp.wait_ge(flow("x_kept").sem, 16 * (l + 1))
                        put(flow("b_cache_in"), kcache[:], a["cache_swa_k"][l, 0].rearrange("t v d -> t (v d)"))
                        put(flow("b_cache_in"), vcache[:], a["cache_swa_v"][l, 0].rearrange("t v d -> t (v d)"))
                    if kind == "b_values":
                        bank[2].wait_emptied(sp, ("b_values", l))
                        pk, pv, sk_, sv = (o[n][l, 0].rearrange("t v d -> t (v d)") for n in
                                           ("p_swa_k", "p_swa_v", "s_swa_k", "s_swa_v"))
                        done = flow("b_stored")
                        put(done, pk, kout[:, 0, :])
                        put(done, pv, va[:, 3, :])
                        sp.wait_ge(flow("b_cache_in").sem, 32 * (l + 1))
                        put(done, sk_[0:WINDOW - TS], kcache[TS:P, :])
                        put(done, sv[0:WINDOW - TS], vcache[TS:P, :])
                        put(done, sk_[WINDOW - TS:], kout[0:TS, 1, :])
                        put(done, sv[WINDOW - TS:], va[0:TS, 4, :])
                for t in range(5):
                    bank[2 * (t % 2)].wait_emptied(sp, ("y", t, 0))
                    bank[2 * (t % 2) + 1].wait_emptied(sp, ("y", t, 1))
                    if t < 4:
                        put(stored, o["y_prompt"][0, t * P:(t + 1) * P, :], y_tok[:, t, :])
                    else:
                        put(stored, o["y_sample"][0], y_tok[0:TS, 4, :])
                for c in (stored, flow("shift_stored"), flow("c_state_stored"), flow("a_state_stored"), flow("b_stored")):
                    sp.wait_ge(c.sem, c.value)

        @block.gpsimd
        def _(pool):
            step = Lane(pool, chains["pool"])

            def low_part(s):
                n = split_no[s]
                slot = unit_no[s] % NRAW
                nk = nk_of(s)
                pool.wait_ge(high_ready.sem, n + 1)
                low_ready.inc(pool.tensor_tensor(wl[:, n % NSPLIT, 0:nk], wraw[:, slot, 0:nk],
                                                 wh[:, n % NSPLIT, 0:nk].bitcast(F32), ALU.subtract))

            def c_keys(l, g):
                n, at, nch, L = c_group(g)
                flow("c_ss").wait_next(pool, "pool")
                step(pool.tensor_tensor(gv(scratch, n), cc[:, 0:4, at:at + n],
                                        view(prm[:, l, PARAM_AT["c_r_k"]:], [[1, 4], [0, n]]), ALU.mult))
                flow("c_kprime").wait_next(pool, "pool")
                step(pool.tensor_tensor(scratch[:, 0:4 * n], scratch[:, 0:4 * n], kprime[:, 0:4 * n], ALU.mult), flow("c_rk"))

            low_made = {0}
            low_part(units[0])
            for s in plan:
                if s[0] in GEMMS:
                    for s2 in units[unit_no[s] + 1:unit_no[s] + 3]:
                        if s2 in split_no:
                            if split_no[s2] not in low_made:
                                low_made.add(split_no[s2])
                                low_part(s2)
                            break
                elif s[0] == "c_keys":
                    c_keys(*s[1:])
                elif s[0] == "norm_pre":
                    for k in range(1, KD, 2):
                        pool.wait_ge(xh_ready.sem, split_base(s[1], s[2]) + k + 1)
                        step(pool.tensor_tensor(xl[:, k, :], squares[:, k, :], xh[:, k, :].bitcast(F32), ALU.subtract), xl_odd)
                elif s[0] == "norm_post":
                    tmp = squares if s[2] == 1 else sq2
                    for k in range(1, KD, 2):
                        flow("x_step_odd").wait_next(pool, "pool")
                        step(pool.tensor_tensor(x[:, k, :], x[:, k, :], tmp[:, k, :], ALU.add), flow("x_new_odd"))


_INS = ['x_prompt', 'x_sample', 'cache_swa_k', 'cache_swa_v', 'state_mlstm_c', 'state_mlstm_n', 'state_mlstm_m',
        'state_rwkv_s', 'state_rwkv_shift', 'w_in', 'norm_mix_pre', 'norm_mix_post', 'norm_ffn_pre', 'norm_ffn_post',
        'a_gate_bias', 'a_norm', 'rel_bias', 'b_sinks', 'c_mu', 'c_w0', 'c_w_w2', 'c_a0', 'c_w_a2', 'c_w_g2', 'c_k_k',
        'c_k_a', 'c_r_k', 'c_gn_g', 'c_gn_b', 'w_branch_a', 'w_branch_b', 'w_branch_c', 'w_out', 'w_ffn_in', 'w_ffn_out']
_STATES = [("swa_k", (DEPTH, 1, WINDOW, 2, 64)), ("swa_v", (DEPTH, 1, WINDOW, 2, 64)), ("mlstm_c", (DEPTH, 1, 4, P, P)),
           ("mlstm_n", (DEPTH, 1, 4, P)), ("mlstm_m", (DEPTH, 1, 4)), ("rwkv_s", (DEPTH, 1, 8, 64, 64)),
           ("rwkv_shift", (DEPTH, 1, 1, C_COLS))]
_OUTS = ([("y_prompt", (1, TP, D)), ("y_sample", (1, TS, D))] + [("p_" + n, s) for n, s in _STATES]
         + [("s_" + n, s) for n, s in _STATES])


def kernel(**inputs):
    import concourse.bacc as _bacc
    from concourse.bass_utils import run_bass_kernel_spmd as _run

    nc = _bacc.Bacc("TRN2", target_bir_lowering=False, num_devices=1)
    arrays, a, o = {}, {}, {}
    for name in _INS:
        v = np.ascontiguousarray(inputs[name])
        arrays[f"in_{name}"] = v
        a[name] = nc.dram_tensor(f"in_{name}", v.shape, mybir.dt.from_np(v.dtype), kind="ExternalInput").ap()
    for name, shape in _OUTS:
        o[name] = nc.dram_tensor(f"out_{name}", shape, mybir.dt.float32, kind="ExternalOutput").ap()
    build(nc, a, o)
    r = _run(nc, [arrays], core_ids=[0])
    return tuple(r.results[0][f"out_{name}"] for name, _ in _OUTS)
```
